# Optimizing a Trainium2 kernel written in Bass

```python
import math
import numpy as np
import jax, jax.numpy as jnp
from jax import lax

D_MODEL = 1024
BATCH = 1
SEQ = 512
DEPTH = 1

N_HEADS = 8
HEAD_DIM = 64
N_KV_GROUPS = 2
HEADS_PER_GROUP = N_HEADS // N_KV_GROUPS
ATTN_WIDTH = N_HEADS * HEAD_DIM
KV_WIDTH = N_KV_GROUPS * HEAD_DIM
CMP_BLOCK = 32
CMP_STRIDE = 16
CMP_HIDDEN = 128
SEL_BLOCK = 64
SEL_TOP = 16
WINDOW = 512
Q_CHUNK = 64
FORCE_BONUS = 1.0e4
NEG_INF = -1.0e30
CONV_CH = 512
CONV_WIDTH = 31
FFN_DIM = 2816
FFN_CONV_WIDTH = 3
NORM_EPS = 1e-6

IN_SIZES = (ATTN_WIDTH, KV_WIDTH, KV_WIDTH, KV_WIDTH, KV_WIDTH, KV_WIDTH, KV_WIDTH,
            3 * N_HEADS, 2 * CONV_CH, 2 * D_MODEL)
N_IN = sum(IN_SIZES)


def rms_norm(x, g):
    xf = x.astype(jnp.float32)
    y = xf * lax.rsqrt(jnp.mean(xf * xf, axis=-1, keepdims=True) + NORM_EPS)
    return (y * g.astype(jnp.float32)).astype(x.dtype)

def layer_norm(x, g, b):
    xf = x.astype(jnp.float32)
    mu = jnp.mean(xf, axis=-1, keepdims=True)
    var = jnp.mean(jnp.square(xf - mu), axis=-1, keepdims=True)
    y = (xf - mu) * lax.rsqrt(var + NORM_EPS)
    return (y * g.astype(jnp.float32) + b.astype(jnp.float32)).astype(x.dtype)

def causal_dwconv(x, w):
    k, c = w.shape
    return lax.conv_general_dilated(x, w[:, None, :], window_strides=(1,), padding=[(k - 1, 0)],
                                    dimension_numbers=('NWC', 'WIO', 'NWC'), feature_group_count=c)

def alibi_slopes():
    return jnp.power(2.0, -8.0 * jnp.arange(1, N_HEADS + 1, dtype=jnp.float32) / N_HEADS)

def compress(kv, pe, w1, w2):
    b, s, g, dh = kv.shape
    ncmp = (s - CMP_BLOCK) // CMP_STRIDE + 1
    idx = np.arange(ncmp)[:, None] * CMP_STRIDE + np.arange(CMP_BLOCK)[None, :]
    blk = kv[:, idx] + pe[None, None, :, None, :]
    blk = jnp.transpose(blk, (0, 1, 3, 2, 4)).reshape(b, ncmp, g, CMP_BLOCK * dh)
    return jax.nn.gelu(blk @ w1) @ w2

def cmp_to_sel_map(s):
    ncmp = (s - CMP_BLOCK) // CMP_STRIDE + 1
    nsel = s // SEL_BLOCK
    cs = np.arange(ncmp) * CMP_STRIDE
    ce = cs + CMP_BLOCK - 1
    ss = np.arange(nsel) * SEL_BLOCK
    se = ss + SEL_BLOCK - 1
    ov = np.minimum(ce[:, None], se[None, :]) - np.maximum(cs[:, None], ss[None, :]) + 1
    return jnp.asarray(np.clip(ov, 0, None).astype(np.float32) / CMP_BLOCK)

def nsa_attention(q, k_cmp, v_cmp, k_sel, v_sel, k_win, v_win, gate_logits, pe_k, pe_v, ck1, ck2, cv1, cv2):
    b, s, _ = q.shape
    G, J, Dh = N_KV_GROUPS, HEADS_PER_GROUP, HEAD_DIM
    f32 = jnp.float32
    q = q.reshape(b, s, G, J, Dh)
    kv = lambda t: t.reshape(b, s, G, Dh)
    k_cmp, v_cmp, k_sel, v_sel, k_win, v_win = map(kv, (k_cmp, v_cmp, k_sel, v_sel, k_win, v_win))
    slopes = alibi_slopes().reshape(G, J)
    pos = jnp.arange(s)
    scale = HEAD_DIM ** -0.5

    kc = compress(k_cmp, pe_k, ck1, ck2)
    vc = compress(v_cmp, pe_v, cv1, cv2)
    ncmp = kc.shape[1]
    c_end = jnp.arange(ncmp) * CMP_STRIDE + CMP_BLOCK - 1
    dist_c = pos[:, None] - c_end[None, :]
    valid_c = dist_c >= 0
    s_c = jnp.einsum('btgjd,bngd->bgjtn', q, kc).astype(f32) * scale - slopes[:, :, None, None] * dist_c
    s_c = jnp.where(valid_c, s_c, NEG_INF)
    p_c = jax.nn.softmax(s_c, axis=-1) * valid_c
    o_c = jnp.einsum('bgjtn,bngd->btgjd', p_c.astype(vc.dtype), vc)

    nsel = s // SEL_BLOCK
    n_top = min(SEL_TOP, nsel)
    imp = jnp.einsum('bgjtn,nk->bgtk', p_c, cmp_to_sel_map(s))
    blk_id = jnp.arange(nsel)[None, :]
    cur = (pos // SEL_BLOCK)[:, None]
    forced = (blk_id == 0) | (blk_id == cur) | (blk_id == cur - 1)
    imp = jnp.where(blk_id <= cur, imp + FORCE_BONUS * forced, NEG_INF)
    _, sel_idx = lax.top_k(imp, n_top)

    ks_blocks = k_sel.reshape(b, nsel, SEL_BLOCK, G, Dh).transpose(0, 3, 1, 2, 4)
    vs_blocks = v_sel.reshape(b, nsel, SEL_BLOCK, G, Dh).transpose(0, 3, 1, 2, 4)
    gather = jax.vmap(jax.vmap(lambda blocks, ids: blocks[ids]))
    kw_pad = jnp.pad(k_win, ((0, 0), (WINDOW, 0), (0, 0), (0, 0)))
    vw_pad = jnp.pad(v_win, ((0, 0), (WINDOW, 0), (0, 0), (0, 0)))
    m_sel = n_top * SEL_BLOCK

    def chunk(c):
        t0 = c * Q_CHUNK
        qc = lax.dynamic_slice_in_dim(q, t0, Q_CHUNK, axis=1)
        tq = t0 + jnp.arange(Q_CHUNK)
        ids = lax.dynamic_slice_in_dim(sel_idx, t0, Q_CHUNK, axis=2)
        ksg = gather(ks_blocks, ids).reshape(b, G, Q_CHUNK, m_sel, Dh)
        vsg = gather(vs_blocks, ids).reshape(b, G, Q_CHUNK, m_sel, Dh)
        kpos = (ids[..., None] * SEL_BLOCK + jnp.arange(SEL_BLOCK)).reshape(b, G, Q_CHUNK, m_sel)
        dist_s = (tq[None, None, :, None] - kpos)[:, :, None]
        s_s = jnp.einsum('btgjd,bgtmd->bgjtm', qc, ksg).astype(f32) * scale \
            - slopes[None, :, :, None, None] * dist_s
        p_s = jax.nn.softmax(jnp.where(dist_s >= 0, s_s, NEG_INF), axis=-1)
        o_s = jnp.einsum('bgjtm,bgtmd->btgjd', p_s.astype(vsg.dtype), vsg)
        kw = lax.dynamic_slice_in_dim(kw_pad, t0, Q_CHUNK + WINDOW, axis=1)
        vw = lax.dynamic_slice_in_dim(vw_pad, t0, Q_CHUNK + WINDOW, axis=1)
        kpos_w = t0 - WINDOW + jnp.arange(Q_CHUNK + WINDOW)
        dist_w = tq[:, None] - kpos_w[None, :]
        valid_w = (dist_w >= 0) & (dist_w < WINDOW) & (kpos_w[None, :] >= 0)
        s_w = jnp.einsum('btgjd,bsgd->bgjts', qc, kw).astype(f32) * scale - slopes[:, :, None, None] * dist_w
        p_w = jax.nn.softmax(jnp.where(valid_w, s_w, NEG_INF), axis=-1)
        o_w = jnp.einsum('bgjts,bsgd->btgjd', p_w.astype(vw.dtype), vw)
        return o_s, o_w

    o_s, o_w = lax.map(chunk, jnp.arange(s // Q_CHUNK))
    o_s = jnp.moveaxis(o_s, 0, 1).reshape(b, s, G, J, Dh)
    o_w = jnp.moveaxis(o_w, 0, 1).reshape(b, s, G, J, Dh)

    g = jax.nn.sigmoid(gate_logits).reshape(b, s, G, J, 3)
    o = g[..., 0:1] * o_c + g[..., 1:2] * o_s + g[..., 2:3] * o_w
    return o.reshape(b, s, ATTN_WIDTH)

def conformer_conv(u, dw_w, dw_b, ln_g, ln_b, w_proj):
    a, gate = jnp.split(u, 2, axis=-1)
    z = a * jax.nn.sigmoid(gate)
    z = causal_dwconv(z, dw_w) + dw_b
    z = jax.nn.silu(layer_norm(z, ln_g, ln_b))
    return z @ w_proj

def conv_ffn(h, w_up, dw_w, dw_b, w_down):
    u = causal_dwconv(h @ w_up, dw_w) + dw_b
    a, v = jnp.split(u, 2, axis=-1)
    return (jax.nn.silu(a) * v) @ w_down

def first_inputs(seed: int = 0) -> dict:
    key = jax.random.key(seed)
    keys = jax.random.split(key, 32)
    counter = [0]
    f32 = jnp.float32

    def nxt():
        k = keys[counter[0]]
        counter[0] += 1
        return k

    def dense(shape, fan_in):
        return jax.random.normal(nxt(), shape, f32) * fan_in ** -0.5

    def gain(shape):
        return 1.0 + 0.05 * jax.random.normal(nxt(), shape, f32)

    def small(shape, scale=0.02):
        return scale * jax.random.normal(nxt(), shape, f32)

    L = DEPTH
    return {
        "x": jax.random.normal(nxt(), (BATCH, SEQ, D_MODEL), f32),
        "norm1_g": gain((L, D_MODEL)),
        "w_in": dense((L, D_MODEL, N_IN), D_MODEL),
        "cmp_pe_k": small((L, CMP_BLOCK, HEAD_DIM), 0.1),
        "cmp_pe_v": small((L, CMP_BLOCK, HEAD_DIM), 0.1),
        "cmp_k_w1": dense((L, CMP_BLOCK * HEAD_DIM, CMP_HIDDEN), CMP_BLOCK * HEAD_DIM),
        "cmp_k_w2": dense((L, CMP_HIDDEN, HEAD_DIM), CMP_HIDDEN),
        "cmp_v_w1": dense((L, CMP_BLOCK * HEAD_DIM, CMP_HIDDEN), CMP_BLOCK * HEAD_DIM),
        "cmp_v_w2": dense((L, CMP_HIDDEN, HEAD_DIM), CMP_HIDDEN),
        "w_attn_br": dense((L, ATTN_WIDTH, D_MODEL), ATTN_WIDTH),
        "conv_dw_w": dense((L, CONV_WIDTH, CONV_CH), CONV_WIDTH),
        "conv_dw_b": small((L, CONV_CH)),
        "conv_ln_g": gain((L, CONV_CH)),
        "conv_ln_b": small((L, CONV_CH)),
        "w_conv_br": dense((L, CONV_CH, D_MODEL), CONV_CH),
        "w_out": dense((L, D_MODEL, D_MODEL), D_MODEL),
        "norm2_g": gain((L, D_MODEL)),
        "ffn_w_up": dense((L, D_MODEL, 2 * FFN_DIM), D_MODEL),
        "ffn_dw_w": dense((L, FFN_CONV_WIDTH, 2 * FFN_DIM), FFN_CONV_WIDTH),
        "ffn_dw_b": small((L, 2 * FFN_DIM)),
        "ffn_w_down": dense((L, FFN_DIM, D_MODEL), FFN_DIM),
        "final_g": gain((D_MODEL,)),
    }

def first_block(x, norm1_g, w_in, cmp_pe_k, cmp_pe_v, cmp_k_w1, cmp_k_w2, cmp_v_w1, cmp_v_w2,
              w_attn_br, conv_dw_w, conv_dw_b, conv_ln_g, conv_ln_b, w_conv_br, w_out,
              norm2_g, ffn_w_up, ffn_dw_w, ffn_dw_b, ffn_w_down, final_g):
    split_points = list(np.cumsum(IN_SIZES)[:-1])
    for l in range(DEPTH):
        h = rms_norm(x, norm1_g[l])
        proj = h @ w_in[l]
        (q, k_c, v_c, k_s, v_s, k_w, v_w, g_nsa, u_conv, g_merge) = jnp.split(proj, split_points, axis=-1)
        y_attn = nsa_attention(q, k_c, v_c, k_s, v_s, k_w, v_w, g_nsa, cmp_pe_k[l], cmp_pe_v[l],
                               cmp_k_w1[l], cmp_k_w2[l], cmp_v_w1[l], cmp_v_w2[l]) @ w_attn_br[l]
        y_conv = conformer_conv(u_conv, conv_dw_w[l], conv_dw_b[l], conv_ln_g[l], conv_ln_b[l], w_conv_br[l])
        g_a, g_b = jnp.split(jax.nn.sigmoid(g_merge), 2, axis=-1)
        x = x + (g_a * y_attn + g_b * y_conv) @ w_out[l]
        x = x + conv_ffn(rms_norm(x, norm2_g[l]), ffn_w_up[l], ffn_dw_w[l], ffn_dw_b[l], ffn_w_down[l])
    return rms_norm(x, final_g)


MIX_WIDTH = D_MODEL
ATTN_HEAD_DIM = 64
ATTN_WIDTH_2 = MIX_WIDTH // 2
ATTN_HEADS = ATTN_WIDTH_2 // ATTN_HEAD_DIM
ATTN_KV_HEADS = ATTN_HEADS // 4
ATTN_KV_WIDTH = ATTN_KV_HEADS * ATTN_HEAD_DIM
WINDOW_2 = 128
ATTN_BLOCK = 128
HGRN_KEY_DIM = 128
HGRN_WIDTH = MIX_WIDTH - ATTN_WIDTH_2
HGRN_HEADS = HGRN_WIDTH // HGRN_KEY_DIM
HGRN_VAL_DIM = HGRN_WIDTH // HGRN_HEADS
HGRN_KEY_WIDTH = HGRN_HEADS * HGRN_KEY_DIM
CHUNK = 64
IN_SPLITS = (ATTN_WIDTH_2, ATTN_KV_WIDTH, ATTN_KV_WIDTH, HGRN_KEY_WIDTH, HGRN_KEY_WIDTH, HGRN_WIDTH, HGRN_WIDTH)
IN_COLS = sum(IN_SPLITS)
IN_OFFSETS = tuple(int(s) for s in np.cumsum(IN_SPLITS)[:-1])
D_FF = ((8 * D_MODEL) // 3 + 255) // 256 * 256
CONV_WIDTH_2 = 3
N_MOD = 6
EPS = 1e-6


def rms_norm_2(x, gain):
    xf = x.astype(jnp.float32)
    y = xf * lax.rsqrt(jnp.mean(xf * xf, axis=-1, keepdims=True) + EPS)
    return (y * gain.astype(jnp.float32)).astype(x.dtype)

def sliding_window_gqa_with_sinks(q, k, v, sinks):
    B, T = q.shape[0], q.shape[1]
    nb = T // ATTN_BLOCK
    G = ATTN_HEADS // ATTN_KV_HEADS
    qb = q.reshape(B, nb, ATTN_BLOCK, ATTN_KV_HEADS, G, ATTN_HEAD_DIM)

    def band_keys(t):
        prev = jnp.pad(t, ((0, 0), (ATTN_BLOCK, 0), (0, 0), (0, 0)))[:, :T]
        shp = (B, nb, ATTN_BLOCK, ATTN_KV_HEADS, ATTN_HEAD_DIM)
        return jnp.concatenate([prev.reshape(shp), t.reshape(shp)], axis=2)

    kb, vb = band_keys(k), band_keys(v)
    scores = jnp.einsum('bnqhgd,bnkhd->bnhgqk', qb.astype(jnp.float32), kb.astype(jnp.float32)) * (ATTN_HEAD_DIM ** -0.5)
    qi = jnp.arange(ATTN_BLOCK)[:, None]
    ki = jnp.arange(2 * ATTN_BLOCK)[None, :]
    rel = ATTN_BLOCK + qi - ki
    band = (rel >= 0) & (rel < WINDOW_2)
    not_pad = (jnp.arange(nb)[:, None, None] > 0) | (ki >= ATTN_BLOCK)[None]
    mask = band[None] & not_pad
    scores = jnp.where(mask[None, :, None, None], scores, -jnp.inf)
    sink = sinks.astype(jnp.float32).reshape(1, 1, ATTN_KV_HEADS, G, 1, 1)
    m = jnp.maximum(scores.max(axis=-1, keepdims=True), sink)
    e = jnp.exp(scores - m)
    p = e / (e.sum(axis=-1, keepdims=True) + jnp.exp(sink - m))
    out = jnp.einsum('bnhgqk,bnkhd->bnqhgd', p, vb.astype(jnp.float32))
    return out.reshape(B, T, ATTN_WIDTH_2).astype(q.dtype)

def hgrn2_chunkwise(q, f_logit, i, lower_bound):
    B, T, H, Dk = q.shape
    Dv = i.shape[-1]
    nc = T // CHUNK
    qf = jax.nn.silu(q.astype(jnp.float32))
    f = lower_bound + (1 - lower_bound) * jax.nn.sigmoid(f_logit.astype(jnp.float32))
    kf = 1 - f
    g = jnp.log(f)
    vf = i.astype(jnp.float32)

    def to_chunks(t):
        return t.reshape(B, nc, CHUNK, H, t.shape[-1]).transpose(1, 0, 3, 2, 4)

    qc, kc, vc = to_chunks(qf), to_chunks(kf), to_chunks(vf)
    bc = jnp.cumsum(to_chunks(g), axis=3)
    causal = jnp.tril(jnp.ones((CHUNK, CHUNK), dtype=bool))

    def step(S, inp):
        q_, k_, v_, b_ = inp
        b_last = b_[:, :, -1:, :]
        o_inter = jnp.einsum('bhtk,bhkv->bhtv', q_ * jnp.exp(b_), S)
        diff = b_[:, :, :, None, :] - b_[:, :, None, :, :]
        decay = jnp.exp(jnp.where(causal[:, :, None], diff, -jnp.inf))
        scores = jnp.einsum('bhtk,bhtsk,bhsk->bhts', q_, decay, k_)
        o_intra = jnp.einsum('bhts,bhsv->bhtv', scores, v_)
        S_new = jnp.exp(b_last[:, :, 0, :])[..., None] * S + jnp.einsum('bhsk,bhsv->bhkv', k_ * jnp.exp(b_last - b_), v_)
        return S_new, o_inter + o_intra

    S0 = jnp.zeros((B, H, Dk, Dv), jnp.float32)
    _, o = lax.scan(step, S0, (qc, kc, vc, bc))
    return o.transpose(1, 0, 3, 2, 4).reshape(B, T, H, Dv).astype(q.dtype)

def causal_depthwise_conv(u, w, b):
    out = lax.conv_general_dilated(
        u, w[:, None, :].astype(u.dtype), window_strides=(1,),
        padding=[(CONV_WIDTH_2 - 1, 0)], dimension_numbers=('NWC', 'WIO', 'NWC'),
        feature_group_count=u.shape[-1])
    return out + b

def second_inputs(seed: int = 0) -> dict:
    key = jax.random.key(seed)
    ks = jax.random.split(key, 18)
    f32 = jnp.float32

    def normal(k, shape, scale):
        return jax.random.normal(k, shape, f32) * scale

    def gain(k, shape):
        return 1.0 + 0.05 * jax.random.normal(k, shape, f32)

    return {
        "x": normal(ks[0], (BATCH, SEQ, D_MODEL), 1.0),
        "c": normal(ks[1], (BATCH, D_MODEL), 1.0),
        "ada_w": normal(ks[2], (DEPTH, D_MODEL, N_MOD * D_MODEL), 0.5 * D_MODEL ** -0.5),
        "ada_b": normal(ks[3], (DEPTH, N_MOD * D_MODEL), 0.02),
        "mix_norm_g": gain(ks[4], (DEPTH, D_MODEL)),
        "w_in": normal(ks[5], (DEPTH, D_MODEL, IN_COLS), D_MODEL ** -0.5),
        "b_in": normal(ks[6], (DEPTH, IN_COLS), 0.02),
        "attn_sinks": normal(ks[7], (DEPTH, ATTN_HEADS), 0.5),
        "attn_out_g": gain(ks[8], (DEPTH, ATTN_WIDTH_2)),
        "hgrn_lb_logits": normal(ks[9], (DEPTH + 1, HGRN_KEY_WIDTH), 0.5),
        "hgrn_out_g": gain(ks[10], (DEPTH, HGRN_WIDTH)),
        "w_out": normal(ks[11], (DEPTH, MIX_WIDTH, D_MODEL), MIX_WIDTH ** -0.5),
        "ffn_norm_g": gain(ks[12], (DEPTH, D_MODEL)),
        "w_up": normal(ks[13], (DEPTH, D_MODEL, 2 * D_FF), D_MODEL ** -0.5),
        "conv_w": normal(ks[14], (DEPTH, CONV_WIDTH_2, D_FF), CONV_WIDTH_2 ** -0.5),
        "conv_b": normal(ks[15], (DEPTH, D_FF), 0.02),
        "w_down": normal(ks[16], (DEPTH, D_FF, D_MODEL), D_FF ** -0.5),
        "final_norm_g": gain(ks[17], (D_MODEL,)),
    }

def second_block(x, c, ada_w, ada_b, mix_norm_g, w_in, b_in, attn_sinks, attn_out_g, hgrn_lb_logits,
              hgrn_out_g, w_out, ffn_norm_g, w_up, conv_w, conv_b, w_down, final_norm_g):
    B, T = x.shape[0], x.shape[1]
    lower_bounds = jnp.cumsum(jax.nn.softmax(hgrn_lb_logits.astype(jnp.float32), axis=0), axis=0)
    cond = jax.nn.silu(c)
    for l in range(DEPTH):
        mod = cond @ ada_w[l] + ada_b[l]
        shift_m, scale_m, gate_m, shift_f, scale_f, gate_f = jnp.split(mod[:, None, :], N_MOD, axis=-1)

        h = rms_norm_2(x, mix_norm_g[l]) * (1 + scale_m) + shift_m
        proj = h @ w_in[l] + b_in[l]
        q_a, k_a, v_a, q_h, f_h, i_h, g_h = jnp.split(proj, IN_OFFSETS, axis=-1)
        attn = sliding_window_gqa_with_sinks(
            q_a.reshape(B, T, ATTN_HEADS, ATTN_HEAD_DIM),
            k_a.reshape(B, T, ATTN_KV_HEADS, ATTN_HEAD_DIM),
            v_a.reshape(B, T, ATTN_KV_HEADS, ATTN_HEAD_DIM),
            attn_sinks[l])
        attn = rms_norm_2(attn, attn_out_g[l])
        rec = hgrn2_chunkwise(
            q_h.reshape(B, T, HGRN_HEADS, HGRN_KEY_DIM),
            f_h.reshape(B, T, HGRN_HEADS, HGRN_KEY_DIM),
            i_h.reshape(B, T, HGRN_HEADS, HGRN_VAL_DIM),
            lower_bounds[l].reshape(HGRN_HEADS, HGRN_KEY_DIM))
        rec = rms_norm_2(rec, hgrn_out_g[l].reshape(HGRN_HEADS, HGRN_VAL_DIM)) * jax.nn.silu(g_h.reshape(B, T, HGRN_HEADS, HGRN_VAL_DIM))
        mixed = jnp.concatenate([attn, rec.reshape(B, T, HGRN_WIDTH)], axis=-1) @ w_out[l]
        x = x + gate_m * mixed

        h = rms_norm_2(x, ffn_norm_g[l]) * (1 + scale_f) + shift_f
        u, v = jnp.split(h @ w_up[l], 2, axis=-1)
        u = causal_depthwise_conv(u, conv_w[l], conv_b[l])
        x = x + gate_f * ((jax.nn.silu(u) * v) @ w_down[l])
    return rms_norm_2(x, final_norm_g)


def setup_inputs(seed=0):
    out = dict(first_inputs(seed))
    for name, value in second_inputs(seed + 1).items():
        if name != "x":
            out[name + "_2"] = value
    return out


def reference(
    x, norm1_g, w_in, cmp_pe_k, cmp_pe_v, cmp_k_w1, cmp_k_w2, cmp_v_w1, cmp_v_w2, w_attn_br,
    conv_dw_w, conv_dw_b, conv_ln_g, conv_ln_b, w_conv_br, w_out, norm2_g, ffn_w_up, ffn_dw_w,
    ffn_dw_b, ffn_w_down, final_g, c_2, ada_w_2, ada_b_2, mix_norm_g_2, w_in_2, b_in_2,
    attn_sinks_2, attn_out_g_2, hgrn_lb_logits_2, hgrn_out_g_2, w_out_2, ffn_norm_g_2, w_up_2,
    conv_w_2, conv_b_2, w_down_2, final_norm_g_2,
):
    x = first_block(
        x, norm1_g, w_in, cmp_pe_k, cmp_pe_v, cmp_k_w1, cmp_k_w2, cmp_v_w1, cmp_v_w2, w_attn_br,
        conv_dw_w, conv_dw_b, conv_ln_g, conv_ln_b, w_conv_br, w_out, norm2_g, ffn_w_up,
        ffn_dw_w, ffn_dw_b, ffn_w_down, final_g,
    )
    return second_block(
        x, c_2, ada_w_2, ada_b_2, mix_norm_g_2, w_in_2, b_in_2, attn_sinks_2, attn_out_g_2,
        hgrn_lb_logits_2, hgrn_out_g_2, w_out_2, ffn_norm_g_2, w_up_2, conv_w_2, conv_b_2,
        w_down_2, final_norm_g_2,
    )


_drawn_inputs = setup_inputs


def setup_inputs(seed=0):
    import zlib

    import numpy as np

    out = dict(_drawn_inputs(seed))
    spreads = {}
    factors = {'cmp_pe_k': 8.0,
     'cmp_pe_v': 2.763,
     'conv_dw_b': 3.592,
     'conv_ln_g': 2.725,
     'conv_ln_b': 7.485,
     'ffn_dw_b': 3.975,
     'mix_norm_g_2': 4.079,
     'b_in_2': 3.925,
     'attn_sinks_2': 64.0,
     'attn_out_g_2': 23.265,
     'hgrn_lb_logits_2': 8.0,
     'hgrn_out_g_2': 7.863,
     'ffn_norm_g_2': 3.659,
     'conv_b_2': 26.377}
    for name, (base, spread) in spreads.items():
        noise = np.random.default_rng([zlib.crc32(name.encode()), seed]).standard_normal(out[name].shape)
        drawn = base * np.exp(spread * noise) if base else spread * noise
        out[name] = __import__('jax').numpy.asarray(drawn.astype(out[name].dtype))
    for name, factor in factors.items():
        out[name] = (out[name] * factor).astype(out[name].dtype)
    return out
```

```python
import numpy as np
import concourse.bass as bass
from concourse import mybir
from contextlib import ExitStack

F32 = mybir.dt.float32
F32R = mybir.dt.float32r
I32 = mybir.dt.int32
U8 = mybir.dt.uint8
ALU = mybir.AluOpType
ACT = mybir.ActivationFunctionType
AX = mybir.AxisListType

P = 128
D = 1024
T = 512
KD = D // P
QT = T // P
HEADS = 8
DH = 64
PAIRS = HEADS // 2
CMP_BLOCK, CMP_STRIDE = 32, 16
NCMP = (T - CMP_BLOCK) // CMP_STRIDE + 1
CONV_CH, CONV_W = 512, 31
CC = CONV_CH // P
PAD = CONV_W - 1
FFN = 2816
FT = FFN // P
PARTS = [(0, 8), (8, 7), (15, 7)]
MASKED = 1.0e30
EPS = 1e-6
SLOPES = [2.0 ** -(h + 1) for h in range(HEADS)]
SCALE = DH ** -0.5
HG = 4
NMOD = 6
LEVELS = [1, 2, 4, 8, 16, 32, 64]

S_CMP, S_Q, S_K, S_V, S_U, S_MERGE = 0, 2, 6, 8, 10, 18
S_ATTN, S_CONV, S_OUT, S_UP, S_DOWN = 34, 42, 50, 58, 102
S_FH, S_QH, S_IH, S_Q2, S_KV2, S_GH = 126, 130, 134, 138, 142, 144
S_OUT2, S_UP2, S_DOWN2, S_END = 148, 156, 200, 224

ADA_EARLY = 4


ALL = LEVELS + [128, 256]
GELU_C = 0.7978845608028654

CHUNKS = [(1, (h,), None) for h in range(HG)]
CHUNKS += [(b, (2 * c, 2 * c + 1), n) for n, b in enumerate(ALL[:-1]) for c in range(2)]
CHUNKS += [(256, (h,), len(ALL) - 1) for h in range(HG)]
N_SEL = HG + 2 * len(LEVELS)
CHUNK_BANK = [3, 7]
R_BANK = 1
OFF_AT = {(0, 1): 0, (2, 3): 128, (0, 2): 256, (0, 3): 384, (1, 2): 512, (1, 3): 640}
EARLY_CHUNKS = S_GH - S_Q2


def chunk_at(j):
    return j + EARLY_CHUNKS if 0 <= j < len(CHUNKS) - EARLY_CHUNKS else None


def off_chunk_at(j):
    c = chunk_at(j)
    return c if c is not None and c >= N_SEL else None


def av_at(j):
    return (j - 20) // 3 if j >= 20 and (j - 20) % 3 == 0 and (j - 20) // 3 < HG else None


def gh_at(j):
    return (j - 19) // 3 if j >= 19 and (j - 19) % 3 == 0 and (j - 19) // 3 < HG else None


def small_rows():
    sizes = [("norm1_g", 8), ("norm2_g", 8), ("final_g", 8), ("mix_norm_g_2", 8), ("ffn_norm_g_2", 8),
             ("final_norm_g_2", 8), ("c_2", 8), ("conv_dw_b", 4), ("conv_ln_g", 4), ("conv_ln_b", 4),
             ("ada_b_2", 48), ("hgrn_out_g_2", 4), ("hgrn_lb_logits_2", 8), ("conv_dw_w", 124),
             ("ffn_dw_w", 132), ("ffn_dw_b", 44), ("conv_w_2", 66), ("conv_b_2", 22),
             ("bq", 4), ("attn_out_g_2", 4), ("bk", 1), ("bqh", 4), ("bfh", 4), ("bgh", 4),
             ("pe_k", 32), ("pe_v", 32)]
    at, where = 0, {}
    for name, n in sizes:
        where[name] = (at, n)
        at += n
    return where, at


def evacuations():
    bank, freed = {}, {}
    count = {"act": 0, "dve": 0}

    def out(s, who):
        count[who] += 1
        freed[s] = (who, count[who])

    for s in range(S_END):
        if s < S_OUT or S_FH <= s < S_OUT2:
            bank[s] = s % 2 if s < S_GH else 0
            if S_U <= s < S_MERGE and (s - S_U) % 4 >= 2:
                bank[s] = 6 + s % 2
        elif S_DOWN <= s < S_FH or s >= S_DOWN2:
            n = s - (S_DOWN if s < S_FH else S_DOWN2)
            bank[s] = (n // 6 * 2 + n % 2) % 4
        else:
            bank[s] = s % 4
    for s in range(S_END):
        if s < S_Q:
            out(s, "dve")
        elif s < S_U:
            out(s, "act")
        elif s < S_MERGE:
            out(s, "dve" if (s - S_U) % 4 < 2 else "act")
        elif s < S_ATTN:
            out(s, "act")
        elif s < S_DOWN:
            out(s, "dve")
        elif s < S_FH:
            if (s - S_DOWN) % 6 >= 4:
                out(s, "dve")
        elif s < S_IH:
            out(s, "act")
        elif s < S_Q2:
            out(s, "dve")
        elif s < S_KV2 + 1:
            out(s, "act")
        elif s < S_GH:
            out(s, "dve")
        elif s < S_OUT2:
            out(s, "act")
        elif s < S_DOWN2:
            out(s, "dve")
        elif (s - S_DOWN2) % 6 >= 4:
            out(s, "dve")
    return bank, freed


def build(nc, a, out):
    where, n_small = small_rows()
    BANK, FREED = evacuations()
    NSM = (n_small + P - 1) // P

    ctx = ExitStack()
    with ctx:
        base = (nc.sbuf_base + 63) // 64 * 64
        end = nc.sbuf_usable_end
        offset = [base]

        def sb(name, shape, dtype=F32, at=None):
            size = int(np.prod(shape[1:])) * (1 if dtype == U8 else 4)
            if at is None:
                at = offset[0]
                offset[0] += (size + 31) // 32 * 32
            assert at + size <= end, (name, at, size, end)
            return nc.alloc_sbuf_tensor_at(name, list(shape), dtype, offset=at)

        def sem(name):
            return nc.alloc_semaphore(name)

        raw = [sb(f"raw{i}", [P, 2048]) for i in range(2)]
        w_hi = [sb(f"w_hi{i}", [P, 8, P], F32R) for i in range(4)]
        w_lo = [sb(f"w_lo{i}", [P, 8, P], F32R) for i in range(4)]
        xT = sb("xT", [P, KD, T])
        h_at = offset[0]
        h_hi = sb("h_hi", [P, KD, T], F32R)
        h_lo = sb("h_lo", [P, KD, T], F32R)
        ident = sb("ident", [P, P])
        ones = sb("ones", [P, P])
        small = sb("small", [P, NSM, P])
        sm = small[:, :, :].rearrange("p a b -> p (a b)")
        rstd = sb("rstd", [P, T])
        sq = sb("sq", [P, 2, T])
        hn = sb("hn", [P, 2, T])
        mod = sb("mod", [P, NMOD * KD])
        gain2 = sb("gain2", [P, 2, KD])
        cond = sb("cond", [P, KD])
        lower = sb("lower", [P, 4, HG])
        nq_bias = sb("nq_bias", [P, PAIRS])
        sinks = sb("sinks", [P, 2, HEADS])
        eps_t = sb("eps_t", [P, 1])
        stat = sb("stat", [P, 64])
        gates = sb("gates", [P, QT, 24])

        G0 = offset[0]

        qT = sb("qT", [P, PAIRS, T])
        kT = sb("kT", [P, 2, T])
        vN = sb("vN", [P, 2, QT, P])
        mg_at = offset[0]
        mg = sb("mg", [P, 2 * KD, T])
        w1 = [sb(f"w1_{n}", [P, CMP_BLOCK, P], at=mg_at + n * 16384) for n in range(2)]
        z = sb("z", [P, CC, PAD + T])
        acc_at = offset[0]
        acc = sb("acc", [P, CC, T])
        rows = sb("rows", [P, NSM, P], at=acc_at)
        wg = sb("wg", [P, KD, 24], at=acc_at + 4096)
        wg_hi = sb("wg_hi", [P, KD, 24], F32R, at=acc_at + 5120)
        wg_lo = sb("wg_lo", [P, KD, 24], F32R, at=acc_at + 6144)
        dist = sb("dist", [P, T])
        cdist = sb("cdist", [P, QT, 32])
        cvalid = sb("cvalid", [P, QT, 32])
        cbias = sb("cbias", [P, QT * HEADS, 32])
        cp = sb("cp", [P, QT * HEADS, 32])
        w2 = sb("w2", [P, 2, DH])
        hc = sb("hc", [P, 3, 2, 2, 32])
        kcT = sb("kcT", [P, 32])
        vcN = sb("vcN", [32, P])
        pcT = sb("pcT", [32, 2, P])
        sc_at = offset[0]
        sc = sb("sc", [P, 2, 2, T])
        pT = sb("pT", [P, 2, 2, T])
        x_in = sb("x_in", [P, QT, D], at=sc_at)
        blk = sb("blk", [P, 2, CMP_BLOCK, NCMP], at=sc_at + 8192)
        att_hi = sb("att_hi", [P, PAIRS, T], F32R, at=sc_at)
        att_lo = sb("att_lo", [P, PAIRS, T], F32R, at=sc_at + 8192)
        z_at = acc_at - 4 * CC * (PAD + T)
        z_at = (z_at + 31) // 32 * 32
        cv_hi = sb("cv_hi", [P, CC, T], F32R, at=z_at)
        kv_at = G0 + 4 * PAIRS * T
        cv_lo = sb("cv_lo", [P, CC, T], F32R, at=kv_at)
        hbias = [sq[:, n, :] for n in range(2)]
        sgt = [hn[:, n, :] for n in range(2)]
        top1 = offset[0]

        offset[0] = G0
        g_hi = sb("g_hi", [P, FT, T], F32R)
        g_lo = sb("g_lo", [P, FT, T], F32R)
        ada_at = offset[0]
        ada = [sb(f"ada{n}", [P, KD, P], at=ada_at + 4096 * n) for n in range(2)]
        ua = sq
        uv = hn
        assert max(top1, ada_at + 8192) <= end

        offset[0] = G0
        q2T = sb("q2T", [P, PAIRS, T])
        k2T = sb("k2T", [P, T])
        v2N = sb("v2N", [P, QT, P])
        hq = sb("hq", [P, HG, T])
        hk = sb("hk", [P, HG, T])
        f_at = offset[0]
        hf = sb("hf", [P, HG, T])
        hgo = sb("hgo", [P, HG, T], at=f_at)
        hg = sb("hg", [P, HG, T])
        iN = sb("iN", [P, QT, T])
        qd = sb("qd", [P, HG, T // 2])
        kd = sb("kd", [P, HG, T])
        hs = sb("hs", [P, HG, T])
        off_at = offset[0]
        off = sb("off", [P, HG, 768])
        mask = sb("mask", [P, len(LEVELS), T], U8)
        eye8 = sb("eye8", [P, T], U8)
        dist2 = sb("dist2", [P, 2 * P])
        brow = sb("brow", [P, 640])
        sc2 = sb("sc2", [P, 2, 2 * P])
        pT2 = sb("pT2", [P, 2, 2 * P])
        msk_f = sb("msk_f", [P, T], at=off_at)
        assert offset[0] <= end, (offset[0], end)
        offset[0] = G0
        y_out = sb("y_out", [P, QT, D])

        ps = [nc.alloc_psum_tensor(f"ps{i}", [P, 512], F32) for i in range(8)]

        raw_in = [sem(f"raw_in{i}") for i in range(2)]
        hi_done, lo_done, tile_done = sem("hi_done"), sem("lo_done"), sem("tile_done")
        freed = {"act": sem("freed_by_act"), "dve": sem("freed_by_dve")}
        x_loaded, small_loaded, w1_loaded, wg_loaded = sem("x_loaded"), sem("small_loaded"), sem("w1_loaded"), sem("wg_loaded")
        misc_loaded, brow_loaded = sem("misc_loaded"), sem("brow_loaded")
        consts = sem("consts")
        x_turned, x_copied = sem("x_turned"), sem("x_copied")
        small_turned, small_ready = sem("small_turned"), sem("small_ready")
        squared, summed, rooted, inverted = sem("squared"), sem("summed"), sem("rooted"), sem("inverted")
        normed, n_hi, n_lo = sem("normed"), sem("n_hi"), sem("n_lo")
        blocks_ready, hid_done, hid_copied, gelu_parts, gelu_done = (
            sem("blocks_ready"), sem("hid_done"), sem("hid_copied"), sem("gelu_parts"), sem("gelu_done"))
        cmp_kv_done, cmp_kv_copied = sem("cmp_kv_done"), sem("cmp_kv_copied")
        wg_split_hi, wg_split, gate_done, gate_ready = sem("wg_split_hi"), sem("wg_split"), sem("gate_done"), sem("gate_ready")
        sig_ready, cbias_ready = sem("sig_ready"), sem("cbias_ready")
        cqk_done, cx_ready, cexp_done, cp_ready = sem("cqk_done"), sem("cx_ready"), sem("cexp_done"), sem("cp_ready")
        hbias_ready, qk_done, scores_ready, exp_done, p_ready = (
            sem("hbias_ready"), sem("qk_done"), sem("scores_ready"), sem("exp_done"), sem("p_ready"))
        pc_turned, ps_turned, pw_turned = sem("pc_turned"), sem("ps_turned"), sem("pw_turned")
        pc_copied, ps_copied, pw_copied = sem("pc_copied"), sem("ps_copied"), sem("pw_copied")
        pv_done, o_copied = sem("pv_done"), sem("o_copied")
        tap_done, ln_sum, ln_centred, ln_sq, ln_sqsum, ln_root, ln_norm, cv_ready, cv_hi_done, cv_lo_done = (
            sem("tap_done"), sem("ln_sum"), sem("ln_centred"), sem("ln_sq"), sem("ln_sqsum"), sem("ln_root"),
            sem("ln_norm"), sem("cv_ready"), sem("cv_hi_done"), sem("cv_lo_done"))
        att_hi_done, att_lo_done, gate_sig = sem("att_hi_done"), sem("att_lo_done"), sem("gate_sig")
        merged, m_hi, m_lo = sem("merged"), sem("m_hi"), sem("m_lo")
        biased, tap1_done, silu_done, prod_done, g_hi_done, g_lo_done = (
            sem("biased"), sem("tap1_done"), sem("silu_done"), sem("prod_done"), sem("g_hi_done"), sem("g_lo_done"))
        ada_in = [sem(f"ada_in{i}") for i in range(2)]
        ada_done, ada_ready, cond_ready, mod_ready = sem("ada_done"), sem("ada_ready"), sem("cond_ready"), sem("mod_ready")
        x2_ready = sem("x2_ready")
        lb_max, lb_exp, lb_ready = sem("lb_max"), sem("lb_exp"), sem("lb_ready")
        f_ready, k_scaled, q_scaled, chunk_done, lvl_done, sel_done, off_copied, f_merged, g_merged = (
            sem("f_ready"), sem("k_scaled"), sem("q_scaled"), sem("chunk_done"), sem("lvl_done"),
            sem("sel_done"), sem("off_copied"), sem("f_merged"), sem("g_merged"))
        setup2 = sem("setup2")
        qk2_done, s2_ready, e2_done, sink_exp, p2_ready, t2_done, t2_copied, pv2_done, o2_copied = (
            sem("qk2_done"), sem("s2_ready"), sem("e2_done"), sem("sink_exp"), sem("p2_ready"), sem("t2_done"),
            sem("t2_copied"), sem("pv2_done"), sem("o2_copied"))
        n2_sq, n2_sum, n2_root, n2_norm, n2_hi, n2_lo = (
            sem("n2_sq"), sem("n2_sum"), sem("n2_root"), sem("n2_norm"), sem("n2_hi"), sem("n2_lo"))
        av_done, av_copied, r_sq, r_sum, r_var, r_inv, r_root, r_norm, r_hi, r_lo, gate2_silu = (
            sem("av_done"), sem("av_copied"), sem("r_sq"), sem("r_sum"), sem("r_var"), sem("r_inv"), sem("r_root"),
            sem("r_norm"), sem("r_hi"), sem("r_lo"), sem("gate2_silu"))
        y_ready, y_turned, stored = sem("y_ready"), sem("y_turned"), sem("stored")
        y_copied = [sem("y_copied_act"), sem("y_copied_dve")]
        act_chain, dve_chain, pool_chain = sem("act_chain"), sem("dve_chain"), sem("pool_chain")

        def col(name, i=0, n=1):
            at = where[name][0]
            return sm[:, at + i:at + i + n] if isinstance(i, int) else sm[:, bass.ds(i + at, n)]

        def k_tiles(w, rows_from, nk, c0, n=2 * P):
            return w[rows_from:rows_from + nk * P, bass.ds(c0, n)].rearrange("(k p) n -> p k n", p=P)

        def standard(w, c0, u, nk=KD, r0=0):
            return [(raw[u % 2][:, 0:nk * 256].rearrange("p (k n) -> p k n", k=nk), k_tiles(w, r0, nk, c0))]

        def two_columns(w, cols, u, width=P):
            dst = raw[u % 2][:, :].rearrange("p (k n) -> p k n", k=KD)
            return [(dst[:, :, n * width:(n + 1) * width], k_tiles(w, 0, KD, c, width)) for n, c in enumerate(cols)]

        def paired_columns(w, c0, i, u):
            return two_columns(w, [c0 + g * 256 + (i + m) * DH for m in range(2) for g in range(2)], u, DH)

        def paired_rows(w, c0, u, nk_dst=PAIRS, more=None):
            dst = raw[u % 2][:, 0:nk_dst * 256].rearrange("p (k n) -> p k n", k=nk_dst)
            got = [(dst[g * DH:(g + 1) * DH, 0:PAIRS, :],
                    w[g * 256:(g + 1) * 256, c0:c0 + 256].rearrange("(i d) n -> d i n", d=DH)) for g in range(2)]
            if more is not None:
                got.append((dst[:, PAIRS:nk_dst, :], k_tiles(w, PAIRS * P, nk_dst - PAIRS, c0)))
            return got

        w_in, w_in2 = a["w_in"][0], a["w_in_2"][0]
        LOADS = {}
        for n in range(S_END // 2):
            s = 2 * n
            if s < S_Q:
                LOADS[n] = standard(w_in, 512, n)
            elif s < S_K:
                LOADS[n] = paired_columns(w_in, 0, s - S_Q, n)
            elif s < S_V:
                LOADS[n] = two_columns(w_in, [768, 1024], n)
            elif s < S_U:
                LOADS[n] = two_columns(w_in, [896, 1152], n)
            elif s < S_MERGE:
                m = (s - S_U) // 2
                LOADS[n] = standard(w_in, 1304 + (m % 2) * CONV_CH + (m // 2) * 256, n)
            elif s < S_ATTN:
                LOADS[n] = standard(w_in, 2328 + (s - S_MERGE) * P, n)
            elif s < S_CONV:
                LOADS[n] = paired_rows(a["w_attn_br"][0], (s - S_ATTN) * P, n)
            elif s < S_OUT:
                LOADS[n] = standard(a["w_conv_br"][0], (s - S_CONV) * P, n, CC)
            elif s < S_UP:
                LOADS[n] = standard(a["w_out"][0], (s - S_OUT) * P, n)
            elif s < S_DOWN:
                m = (s - S_UP) // 2
                LOADS[n] = standard(a["ffn_w_up"][0], (m % 2) * FFN + (m // 2) * 256, n)
            elif s < S_FH or s >= S_DOWN2:
                w = a["ffn_w_down"][0] if s < S_FH else a["w_down_2"][0]
                m = (s - (S_DOWN if s < S_FH else S_DOWN2)) // 2
                k0, nk = PARTS[m % 3]
                LOADS[n] = standard(w, m // 3 * 256, n, nk, k0 * P)
            elif s < S_QH:
                LOADS[n] = standard(w_in2, 1280 + (s - S_FH) * P, n)
            elif s < S_IH:
                LOADS[n] = standard(w_in2, 768 + (s - S_QH) * P, n)
            elif s < S_Q2:
                LOADS[n] = standard(w_in2, 1792 + (s - S_IH) * P, n)
            elif s < S_KV2:
                LOADS[n] = paired_columns(w_in2, 0, s - S_Q2, n)
            elif s < S_GH:
                LOADS[n] = standard(w_in2, 512, n)
            elif s < S_OUT2:
                LOADS[n] = standard(w_in2, 2304 + (s - S_GH) * P, n)
            elif s < S_UP2:
                LOADS[n] = paired_rows(a["w_out_2"][0], (s - S_OUT2) * P, n, KD, True)
            else:
                m = (s - S_UP2) // 2
                LOADS[n] = standard(a["w_up_2"][0], (m % 2) * FFN + (m // 2) * 256, n)
        RAW_COUNT, total = {}, [0, 0]
        for n in range(S_END // 2):
            total[n % 2] += 16 * len(LOADS[n])
            RAW_COUNT[n] = total[n % 2]
        DEPTH_OF = {s: (4 if S_ATTN <= s < S_OUT else
                        PARTS[(s - (S_DOWN if s < S_FH else S_DOWN2)) // 2 % 3][1]
                        if S_DOWN <= s < S_FH or s >= S_DOWN2 else KD) for s in range(S_END)}

        def wait_bank(eng, s, shift=0):
            prev = max((t for t in range(s) if BANK[t] == BANK[s] and t in FREED), default=None)
            if prev is not None:
                who, n = FREED[prev]
                eng.wait_ge(freed[who], n + shift)

        def x_ready(eng, norm, k):
            if norm == 0:
                eng.wait_ge(x_copied, k + 1)
            elif norm == 3:
                eng.wait_ge(x2_ready, k + 1)
            else:
                s = {1: S_OUT + k, 4: S_OUT2 + k,
                     2: S_DOWN + k // 2 * 6 + 4 + k % 2, 5: S_DOWN2 + k // 2 * 6 + 4 + k % 2}[norm]
                eng.wait_ge(freed["dve"], FREED[s][1])

        SQ_BASE = [0, 8, 16, 24, 32, 40]
        HN_BASE = {0: 0, 1: 8, 3: 16, 4: 24}

        ITEMS = [(i, g, t) for i in range(PAIRS) for g in range(2) for t in range(QT)]
        NI = len(ITEMS)
        FIRST_KEYS = [max(0, t - 1) for t in range(QT)]

        def small_dmas(pool):
            flat = rows[:, :, :]

            def put(name, rows_ap, c0=0, c1=P):
                at, n = where[name]
                done = 0
                while done < n:
                    r, m = (at + done) % P, (at + done) // P
                    take = min(n - done, P - r)
                    pool.dma_start(flat[r:r + take, m, c0:c1], rows_ap[done:done + take, :]).then_inc(small_loaded, 16)
                    count[0] += 16
                    done += take

            count = [0]
            as_rows = lambda v, n: v.rearrange("a (r c) -> (a r) c", c=n)
            for name in ("norm1_g", "norm2_g", "mix_norm_g_2", "ffn_norm_g_2", "c_2", "conv_dw_b", "conv_ln_g",
                         "conv_ln_b", "ada_b_2", "hgrn_out_g_2", "hgrn_lb_logits_2", "ffn_dw_b", "conv_b_2"):
                put(name, as_rows(a[name], P))
            for name in ("final_g", "final_norm_g_2"):
                put(name, a[name].rearrange("(r c) -> r c", c=P))
            for name in ("conv_dw_w", "ffn_dw_w", "conv_w_2"):
                put(name, as_rows(a[name][0], P))
            b = a["b_in_2"]
            for name, c0, c1 in (("bk", 512, 640), ("bqh", 768, 1280), ("bfh", 1280, 1792), ("bgh", 2304, 2816)):
                put(name, as_rows(b[:, c0:c1], P))
            for g in range(2):
                put("bq", as_rows(b[:, g * 256:(g + 1) * 256], DH), g * DH, (g + 1) * DH)
                put("attn_out_g_2", as_rows(a["attn_out_g_2"][:, g * 256:(g + 1) * 256], DH), g * DH, (g + 1) * DH)
                put("pe_k", a["cmp_pe_k"][0], g * DH, (g + 1) * DH)
                put("pe_v", a["cmp_pe_v"][0], g * DH, (g + 1) * DH)
            small_total[0] = count[0]

        small_total = [0]

        def tables2(pool, link):
            pool.wait_ge(tile_done, S_FH)
            link(pool.memset(dist2[:, :], 0.0))
            link(pool.affine_select(out=dist2[:, :], in_=dist2[:, :], compare_op=ALU.is_ge, fill=MASKED,
                                    base=P, pattern=[[-1, 2 * P]], channel_multiplier=1))
            link(pool.affine_select(out=dist2[:, :], in_=dist2[:, :], compare_op=ALU.is_ge, fill=MASKED,
                                    base=-1, pattern=[[1, 2 * P]], channel_multiplier=-1))
            link(pool.memset(hg[:, :, :], 1.0))
            link(pool.memset(kd[:, :, :], 0.0))
            link(pool.memset(hs[:, :, :], 0.0))
            rep = T // P

            def as_mask(dst, n):
                link(pool.tensor_copy(dst, msk_f[:, 0:n]))

            link(pool.memset(msk_f[:, :], 0.0))
            link(pool.affine_select(out=msk_f[:, :].rearrange("p (r c) -> p r c", r=rep),
                                    in_=msk_f[:, :].rearrange("p (r c) -> p r c", r=rep),
                                    compare_op=ALU.not_equal, fill=1.0, base=0, pattern=[[0, rep], [-1, P]],
                                    channel_multiplier=1))
            as_mask(eye8[:, :], T)
            for n, b in enumerate(LEVELS):
                nb = P // (2 * b)
                v = msk_f[:, :].rearrange("p (r m c) -> p r m c", r=8, m=nb)
                link(pool.memset(msk_f[:, :], 1.0))
                link(pool.affine_select(out=v, in_=v, compare_op=ALU.is_ge, fill=0.0, base=0,
                                        pattern=[[0, 8], [-2 * b, nb], [0, b]], channel_multiplier=1))
                link(pool.affine_select(out=v, in_=v, compare_op=ALU.is_ge, fill=0.0, base=b - 1,
                                        pattern=[[0, 8], [2 * b, nb], [0, b]], channel_multiplier=-1))
                as_mask(mask[:, n, :], T)
            pool.memset(msk_f[:, 0:1], 0.0).then_inc(setup2, 1)

        def pairs_of(x, b):
            return x[:, :, :].rearrange("p h t -> p (h t)").rearrange("p (m e c) -> p m e c", e=2, c=b)

        def hgrn_pool(pool, lo):
            s = S_Q2
            pool.wait_ge(f_ready, 2 * HG)
            for n, b in enumerate(ALL):
                g, f, k, kk = pairs_of(hg, b), pairs_of(hf, b), pairs_of(hk, b), pairs_of(kd, b)
                if n:
                    if n >= 2:
                        pool.wait_ge(lvl_done, n)
                    pool.tensor_tensor(kk[:, :, 0, :], k[:, :, 0, :], g[:, :, 0, :], ALU.mult).then_inc(k_scaled, 1)
                if n < len(ALL) - 1:
                    if n:
                        pool.wait_ge(f_merged, n)
                    pool.tensor_tensor(g[:, :, 0, :], g[:, :, 0, :],
                                       f[:, :, 1, b - 1:b].to_broadcast([P, HG * T // (2 * b), b]),
                                       ALU.mult).then_inc(g_merged, 1)
                    pool.wait_ge(g_merged, n + 1)
                while s < (S_GH, S_GH + 4)[n > 0]:
                    lo(s)
                    s += 1
            while s < S_UP2:
                lo(s)
                s += 1

        block = ctx.enter_context(nc.Block())

        @block.sync
        def _(sp):
            for t in range(QT):
                sp.dma_start(x_in[:, t, :], a["x"][0, t * P:(t + 1) * P, :]).then_inc(x_loaded, 16)

            def unit(n):
                if n >= 2:
                    sp.wait_ge(lo_done, 2 * n - 2)
                for dst, src in LOADS[n]:
                    sp.dma_start(dst, src).then_inc(raw_in[n % 2], 16)

            unit(0)
            unit(1)
            for n, w in enumerate(("cmp_k_w1", "cmp_v_w1")):
                for g in range(2):
                    sp.dma_start(w1[n][g * DH:(g + 1) * DH, :, :],
                                 a[w][0].rearrange("(i d) n -> d i n", d=DH)).then_inc(w1_loaded, 16)
            last = S_OUT // 2
            for n in range(2, last):
                unit(n)

            def ada_load(n, count=None, c0=None):
                if count is None:
                    if n >= 2:
                        sp.wait_ge(ada_done, n - 1)
                    c0 = n * P
                else:
                    sp.wait_ge(ada_done, count)
                sp.dma_start(ada[n % 2][:, :, :], k_tiles(a["ada_w_2"][0], 0, KD, c0, P)).then_inc(ada_in[n % 2], 16)

            for n in range(S_OUT // 2, S_UP // 2):
                unit(n)
            sp.wait_ge(m_lo, KD)
            w = a["ffn_w_up"][0]
            u0 = S_UP // 2
            for n in range(2):
                ada_load(2 * n)
                ada_load(2 * n + 1)
                unit(u0 + 2 * n)
                unit(u0 + 2 * n + 1)
            with sp.Fori(0, FT // 2 - 2) as i:
                for half in range(2):
                    for n in ((0, 1, 2), (3,))[half]:
                        ada_load(n, i * 4 + (ADA_EARLY + n - 1), i * (4 * P) + (ADA_EARLY + n) * P)
                    n = u0 + 4 + half
                    sp.wait_ge(lo_done, i * 4 + (2 * n - 2))
                    sp.dma_start(raw[n % 2][:, :].rearrange("p (k n) -> p k n", k=KD),
                                 k_tiles(w, 0, KD, i * 256 + (512 + half * FFN))).then_inc(raw_in[n % 2], 16)
            for n in range(NMOD * KD - 8, NMOD * KD):
                ada_load(n)
            for n in range(S_DOWN // 2, S_UP2 // 2):
                unit(n)
            w = a["w_up_2"][0]
            u0 = S_UP2 // 2
            with sp.Fori(0, FT // 2) as i:
                for half in range(2):
                    n = u0 + half
                    sp.wait_ge(lo_done, i * 4 + (2 * n - 2))
                    sp.dma_start(raw[n % 2][:, :].rearrange("p (k n) -> p k n", k=KD),
                                 k_tiles(w, 0, KD, i * 256 + half * FFN)).then_inc(raw_in[n % 2], 16)
            for n in range(S_DOWN2 // 2, S_END // 2):
                unit(n)
            for t in range(QT):
                for half in range(2):
                    sp.wait_ge(y_copied[half], t + 1)
                sp.dma_start(out[0, t * P:(t + 1) * P, :], y_out[:, t, :]).then_inc(stored, 16)
            sp.wait_ge(stored, 16 * QT)

        @block.gpsimd
        def _(pool):
            chain = [0]

            def link(ins):
                chain[0] += 1
                ins.then_inc(pool_chain, 1)
                pool.wait_ge(pool_chain, chain[0])

            link(pool.memset(ident[:, :], 0.0))
            link(pool.affine_select(out=ident[:, :], in_=ident[:, :], compare_op=ALU.not_equal, fill=1.0,
                                    base=0, pattern=[[-1, P]], channel_multiplier=1))
            pool.memset(eps_t[:, :], EPS)
            pool.memset(ones[:, :], 1.0).then_inc(consts, 1)
            link(pool.memset(rows[:, NSM - 1, :], 0.0))
            small_dmas(pool)
            link(pool.iota(dist[:, :], [[-1, T]], base=T - P, channel_multiplier=1,
                           allow_small_or_imprecise_dtypes=True))
            link(pool.affine_select(out=dist[:, :], in_=dist[:, :], compare_op=ALU.is_ge, fill=MASKED,
                                    base=T - P, pattern=[[-1, T]], channel_multiplier=1))
            cpat = [[P, QT], [-CMP_STRIDE, 32]]
            link(pool.iota(cdist[:, :, :], cpat, base=1 - CMP_BLOCK, channel_multiplier=1,
                           allow_small_or_imprecise_dtypes=True))
            link(pool.affine_select(out=cdist[:, :, :], in_=cdist[:, :, :], compare_op=ALU.is_ge, fill=MASKED,
                                    base=1 - CMP_BLOCK, pattern=cpat, channel_multiplier=1))
            link(pool.memset(cvalid[:, :, :], 1.0))
            pool.affine_select(out=cvalid[:, :, :], in_=cvalid[:, :, :], compare_op=ALU.is_ge, fill=0.0,
                               base=1 - CMP_BLOCK, pattern=cpat, channel_multiplier=1).then_inc(consts, 1)
            pool.memset(z[:, :, 0:PAD], 0.0).then_inc(consts, 1)

            def lo(s, slot=None, count=None):
                pool.wait_ge(hi_done, s + 1 if count is None else count)
                slot = s if slot is None else slot
                nk = 8 if count is not None else DEPTH_OF[s]
                part = raw[slot // 2 % 2][:, 0:nk * 256].rearrange("p (k n) -> p k n", k=nk)
                pool.tensor_tensor(w_lo[slot % 4][:, 0:nk, :], part[:, :, slot % 2 * P:(slot % 2 + 1) * P],
                                   w_hi[slot % 4][:, 0:nk, :].bitcast(F32), ALU.subtract).then_inc(lo_done, 1)

            for s in range(S_UP):
                lo(s)
            with pool.Fori(0, FT // 2) as i:
                for j in range(4):
                    lo(None, S_UP + j, i * 4 + (S_UP + j + 1))
            for s in range(S_DOWN, S_Q2):
                lo(s)
                if s == S_FH + 3:
                    tables2(pool, link)
            hgrn_pool(pool, lo)
            with pool.Fori(0, FT // 2) as i:
                for j in range(4):
                    lo(None, S_UP2 + j, i * 4 + (S_UP2 + j + 1))
            for s in range(S_DOWN2, S_END):
                lo(s)

        @block.scalar
        def _(act):
            chain = [0]

            def link(ins):
                chain[0] += 1
                ins.then_inc(act_chain, 1)
                act.wait_ge(act_chain, chain[0])

            def hi(s):
                if s >= S_END:
                    return
                u = s // 2
                act.wait_ge(raw_in[u % 2], RAW_COUNT[u])
                if s >= 4:
                    act.wait_ge(tile_done, s - 3)
                nk = DEPTH_OF[s]
                part = raw[u % 2][:, 0:nk * 256].rearrange("p (k n) -> p k n", k=nk)
                act.activation(w_hi[s % 4][:, 0:nk, :], part[:, :, s % 2 * P:(s % 2 + 1) * P],
                               ACT.Copy).then_inc(hi_done, 1)

            def evac(s, dst, func=ACT.Copy, src=None, **kw):
                act.wait_ge(tile_done, s + 1)
                act.activation(dst, ps[BANK[s]][:, :] if src is None else src, func, **kw).then_inc(freed["act"], 1)

            def square(norm, k):
                x_ready(act, norm, k)
                if k >= 2:
                    act.wait_ge(summed, SQ_BASE[norm] + k - 1)
                act.activation(sq[:, k % 2, :], xT[:, k, :], ACT.Square).then_inc(squared, 1)

            def root(norm):
                act.wait_ge(summed, SQ_BASE[norm] + KD)
                act.activation(rstd[:, :], ps[7][:, :], ACT.Sqrt, scale=1.0 / D, bias=eps_t[:, 0:1]).then_inc(rooted, 1)

            def norm_hi(norm):
                for k in range(KD):
                    act.wait_ge(normed, HN_BASE[norm] + k + 1)
                    act.activation(h_hi[:, k, :], hn[:, k % 2, :], ACT.Copy).then_inc(n_hi, 1)

            act.dma_start(w2[:, 0, :], a["cmp_k_w2"][0]).then_inc(misc_loaded, 16)
            act.dma_start(w2[:, 1, :], a["cmp_v_w2"][0]).then_inc(misc_loaded, 16)
            act.dma_start(sinks[:, 0, :], a["attn_sinks_2"].to_broadcast([P, HEADS])).then_inc(misc_loaded, 16)
            act.dma_start(wg[:, :, :], k_tiles(w_in, 0, KD, 1280, 24)).then_inc(wg_loaded, 16)
            for s in range(2):
                hi(s)
            for k in range(KD):
                square(0, k)
            root(0)
            for s in range(2, 4):
                hi(s)
            norm_hi(0)
            act.wait_ge(small_ready, 1)
            act.activation(cond[:, :], col("c_2", 0, KD), ACT.Silu).then_inc(cond_ready, 1)
            act.activation(nq_bias[:, :], col("bq", 0, PAIRS), ACT.Copy, scale=-SCALE).then_inc(cond_ready, 1)
            act.wait_ge(lb_max, 1)
            act.activation(lower[:, 0:2, :], lower[:, 0:2, :], ACT.Exp).then_inc(lb_exp, 1)
            act.wait_ge(consts, 3)
            for h in range(HEADS):
                g, i = divmod(h, PAIRS)
                dst = cbias[:, g * 16:(g + 1) * 16, :].rearrange("p (t i) n -> p t i n", i=PAIRS)[:, :, i, :]
                act.activation(dst, cdist[:, :, :], ACT.Copy, scale=SLOPES[h]).then_inc(cbias_ready, 1)

            act.wait_ge(wg_loaded, 16)
            act.activation(wg_hi[:, :, :], wg[:, :, :], ACT.Copy).then_inc(wg_split_hi, 1)
            for s in range(S_CMP, S_U):
                hi(s + 4)
                if s < S_Q:
                    continue
                if s < S_K:
                    evac(s, qT[:, s - S_Q, :], scale=-SCALE)
                elif s < S_V:
                    evac(s, kT[:, s - S_K, :])
                else:
                    evac(s, vN[:, s - S_V, :, :].rearrange("p t n -> p (t n)"))
            act.wait_ge(gelu_parts, 1)
            act.activation(hc[:, 1, :, :, 0:NCMP], hc[:, 1, :, :, 0:NCMP], ACT.Tanh).then_inc(gelu_done, 1)
            act.wait_ge(gate_done, 1)
            act.activation(gates[:, :, :].rearrange("p t n -> p (t n)"), ps[2][:, 0:QT * 24],
                           ACT.Sigmoid).then_inc(gate_ready, 1)
            for s in range(S_U, S_MERGE):
                hi(s + 4)
                n = s - S_U
                if n % 4 >= 2:
                    j = n // 4 * 2 + n % 2
                    if j >= 2:
                        act.wait_ge(freed["dve"], FREED[S_U + (n // 4 - 1) * 4 + n % 2][1])
                    act.wait_ge(tile_done, s + 1)
                    act.activation(sgt[j % 2], ps[BANK[s]][:, :], ACT.Sigmoid).then_inc(freed["act"], 1)
            for c in range(2):
                act.wait_ge(cx_ready, c + 1)
                x = cp[:, c * 16:(c + 1) * 16, 0:NCMP]
                act.activation(x, x, ACT.Exp, scale=-1.0).then_inc(cexp_done, 1)

            def head_bias(n):
                i, g, _ = ITEMS[n * QT]
                if n >= 2:
                    act.wait_ge(scores_ready, 2 * QT * (n - 1))
                act.activation(hbias[n % 2], dist[:, :], ACT.Copy, scale=SLOPES[i + 4 * g]).then_inc(hbias_ready, 1)

            head_bias(0)
            for j in range(NI + 2):
                if j < NI:
                    i, g, t = ITEMS[j]
                    if t == 0 and j // QT + 1 < HEADS:
                        head_bias(j // QT + 1)
                    L = (t + 1) * P
                    for b in range(2):
                        act.wait_ge(scores_ready, 2 * j + b + 1)
                        x = sc[:, j % 2, b, 0:L]
                        act.activation(x, x, ACT.Exp, scale=-1.0, bias=stat[:, 2 * (j % 2) + b:2 * (j % 2) + b + 1],
                                       accum_out=stat[:, 4 + 2 * (j % 2) + b:5 + 2 * (j % 2) + b]).then_inc(exp_done, 1)
                if j < NI and j % 2 == 0:
                    hi(S_MERGE + j // 2 + 4)
                    if j >= 2:
                        s = S_MERGE + j // 2 - 1
                        evac(s, mg[:, s - S_MERGE, :])
                if 1 <= j <= NI:
                    m = j - 1
                    L = (ITEMS[m][2] + 1) * P
                    act.wait_ge(pc_turned, m + 1)
                    if m >= 2:
                        act.wait_ge(pv_done, m - 1)
                    act.activation(pcT[0:NCMP, m % 2, :], ps[3][0:NCMP, 0:P], ACT.Copy).then_inc(pc_copied, 1)
                    act.wait_ge(ps_turned, m + 1)
                    act.activation(pT[:, m % 2, 0, 0:L], ps[6][:, 0:L], ACT.Copy).then_inc(ps_copied, 1)
                if j >= 2 and (j - 1) % (2 * QT) == 0:
                    i = (j - 1) // (2 * QT) - 1
                    act.wait_ge(pv_done, 2 * QT * (i + 1))
                    act.activation(qT[:, i, :], ps[2][:, :], ACT.Copy).then_inc(o_copied, 1)
                    act.wait_ge(o_copied, i + 1)
            evac(S_ATTN - 1, mg[:, 2 * KD - 1, :])

            for i in range(PAIRS):
                act.activation(att_hi[:, i, :], qT[:, i, :], ACT.Copy).then_inc(att_hi_done, 1)
            for c in range(2):
                x = mg[:, c * 4:(c + 1) * 4, :]
                act.wait_ge(freed["act"], FREED[S_MERGE + 4 * c + 3][1])
                act.activation(x, x, ACT.Sigmoid).then_inc(gate_sig, 1)
            for c in range(CC):
                act.wait_ge(ln_centred, c + 1)
                if c >= 2:
                    act.wait_ge(ln_sqsum, c - 1)
                act.activation(sq[:, c % 2, :], acc[:, c, :], ACT.Square).then_inc(ln_sq, 1)
            hi(S_ATTN + 4)
            for c in range(2, 4):
                x = mg[:, c * 4:(c + 1) * 4, :]
                act.wait_ge(freed["act"], FREED[S_MERGE + 4 * c + 3][1])
                act.activation(x, x, ACT.Sigmoid).then_inc(gate_sig, 1)
            hi(S_ATTN + 5)
            act.wait_ge(ln_sqsum, CC)
            act.activation(rstd[:, :], ps[5][:, :], ACT.Sqrt, scale=1.0 / CONV_CH, bias=eps_t[:, 0:1]).then_inc(ln_root, 1)
            hi(S_ATTN + 6)
            for c in range(CC):
                act.wait_ge(ln_norm, c + 1)
                act.activation(acc[:, c, :], acc[:, c, :], ACT.Silu, scale=col("conv_ln_g", c),
                               bias=col("conv_ln_b", c)).then_inc(cv_ready, 1)
                act.wait_ge(cv_ready, c + 1)
                act.activation(cv_hi[:, c, :], acc[:, c, :], ACT.Copy).then_inc(cv_hi_done, 1)
            hi(S_ATTN + 7)
            for s in range(S_ATTN + 4, S_CONV):
                hi(s + 4)
            for s in range(S_CONV, S_OUT):
                hi(s + 4)
                m = s - S_CONV
                act.wait_ge(merged, m + 1)
                act.activation(h_hi[:, m, :], mg[:, m, :], ACT.Copy).then_inc(m_hi, 1)

            for k in range(KD):
                hi(S_OUT + k + 4)
                square(1, k)
            root(1)
            norm_hi(1)

            def ffn_act(s0, second):
                wname, bname = ("conv_w_2", "conv_b_2") if second else ("ffn_dw_w", "ffn_dw_b")
                wide = FT if second else 2 * FT
                done0 = FREED[s0][1]
                with act.Fori(0, FT // 2) as i:
                    for j in range(4):
                        half, t = j // 2, j % 2
                        s = s0 + 4 + j
                        u = s // 2
                        act.wait_ge(raw_in[u % 2], i * 16 + RAW_COUNT[u])
                        act.wait_ge(tile_done, i * 4 + (s - 3))
                        part = raw[u % 2][:, :].rearrange("p (k n) -> p k n", k=KD)
                        act.activation(w_hi[s % 4][:, :, :], part[:, :, s % 2 * P:(s % 2 + 1) * P],
                                       ACT.Copy).then_inc(hi_done, 1)
                        if half == 0 or not second:
                            act.wait_ge(g_lo_done, i * 2 + (second * (FT + 2) + t + 1))
                            act.wait_ge(tile_done, i * 4 + (s0 + j + 1))
                            m = i * 2 + (half * FT + t)
                            act.activation((ua, uv)[half][:, t, :], ps[BANK[s0 + j]][:, :], ACT.Identity,
                                           scale=col(wname, m + 2 * wide), bias=col(bname, m)).then_inc(biased, 1)
                        if half == 1:
                            act.wait_ge(freed["dve"], i * 4 + (done0 + t))
                            act.activation(ua[:, t, :], ua[:, t, :], ACT.Silu).then_inc(silu_done, 1)
                    for t in range(2):
                        act.wait_ge(prod_done, i * 2 + (second * FT + t + 1))
                        act.activation(g_hi[:, bass.ds(i * 2 + t, 1), :].rearrange("p a n -> p (a n)"),
                                       uv[:, t, :], ACT.Copy).then_inc(g_hi_done, 1)

            def act_down(s0, norm):
                for n in range(25):
                    if n >= 5 and n % 6 in (5, 0):
                        square(norm, (n - 5) // 6 * 2 + (n % 6 == 0))
                    if n < 24:
                        hi(s0 + n + 4)

            ffn_act(S_UP, 0)
            act_down(S_DOWN, 2)

            act.wait_ge(tile_done, S_FH)
            for c0, c1, at in ((640, 768, 0), (1792, 2304, P)):
                act.dma_start(brow[:, at:at + c1 - c0],
                              a["b_in_2"][:, c0:c1].to_broadcast([P, c1 - c0])).then_inc(brow_loaded, 16)
            root(2)
            for k in range(KD):
                square(3, k)
            root(3)
            norm_hi(3)
            for s in range(S_FH, S_GH):
                hi(s + 4)
                bank = ps[BANK[s]][:, :]
                if s < S_QH:
                    evac(s, hf[:, s - S_FH, :], ACT.Sigmoid, bias=col("bfh", s - S_FH))
                elif s < S_IH:
                    evac(s, hq[:, s - S_QH, :], ACT.Silu, bias=col("bqh", s - S_QH))
                elif s < S_Q2:
                    pass
                elif s < S_KV2:
                    evac(s, q2T[:, s - S_Q2, :], ACT.Identity, scale=-SCALE, bias=nq_bias[:, s - S_Q2:s - S_Q2 + 1])
                elif s == S_KV2:
                    evac(s, k2T[:, :], ACT.Identity, bias=col("bk"))
            for j in range(NI + 2):
                if j < NI:
                    i, g, t = ITEMS[j]
                    L = P if t == 0 else 2 * P
                    r = j % 2
                    act.wait_ge(s2_ready, j + 1)
                    act.activation(sc2[:, r, 0:L], sc2[:, r, 0:L], ACT.Exp, scale=-1.0, bias=stat[:, 18 + r:19 + r],
                                   accum_out=stat[:, 20 + r:21 + r]).then_inc(e2_done, 1)
                    h = i + 4 * g
                    act.activation(stat[:, 22 + r:23 + r], stat[:, 18 + r:19 + r], ACT.Exp,
                                   bias=sinks[:, 0, h:h + 1]).then_inc(e2_done, 1)
                if 1 <= j <= NI:
                    m = j - 1
                    L = P if ITEMS[m][2] == 0 else 2 * P
                    act.wait_ge(t2_done, m + 1)
                    if m >= 2:
                        act.wait_ge(pv2_done, m - 1)
                    act.activation(pT2[:, m % 2, 0:L], ps[6][:, 0:L], ACT.Copy).then_inc(t2_copied, 1)
                c = off_chunk_at(j - 1)
                if c is not None:
                    heads, _ = CHUNKS[c][1:]
                    act.wait_ge(chunk_done, c + 1)
                    bank = ps[CHUNK_BANK[c % 2]]
                    if CHUNKS[c][0] == 128:
                        dst = off[:, heads[0]:heads[0] + 2, 0:256]
                        src = bank[:, :].rearrange("p (h n) -> p h n", h=2)
                    else:
                        dst, src = off[:, heads[0], 256:768], bank[:, :]
                    act.activation(dst, src, ACT.Copy).then_inc(off_copied, 1)
                hd = av_at(j - 1)
                if hd is not None:
                    act.wait_ge(av_done, hd + 1)
                    act.activation(hq[:, hd, :], ps[CHUNK_BANK[hd % 2]][:, :], ACT.Copy).then_inc(av_copied, 1)
                    act.wait_ge(av_copied, hd + 1)
                    if hd >= 2:
                        act.wait_ge(r_sum, hd - 1)
                    act.activation(sq[:, hd % 2, :], hq[:, hd, :], ACT.Square).then_inc(r_sq, 1)
                n = gh_at(j)
                if n is not None:
                    hi(S_GH + n + 4)
                n = gh_at(j - 1)
                if n is not None:
                    act.wait_ge(q_scaled, len(ALL))
                    evac(S_GH + n, hgo[:, n, :], ACT.Identity, bias=col("bgh", n))
                if j >= 2 and (j - 1) % (2 * QT) == 0:
                    i = (j - 1) // (2 * QT) - 1
                    act.wait_ge(pv2_done, 2 * QT * (i + 1))
                    act.activation(q2T[:, i, :], ps[2][:, :], ACT.Copy).then_inc(o2_copied, 1)
            act.wait_ge(r_sum, HG)
            for i in range(PAIRS):
                act.wait_ge(o2_copied, i + 1)
                if i >= 2:
                    act.wait_ge(n2_sum, i - 1)
                act.activation(sq[:, i % 2, :], q2T[:, i, :], ACT.Square).then_inc(n2_sq, 1)
            act.wait_ge(r_inv, HG)
            act.activation(kd[:, :, :], kd[:, :, :], ACT.Sqrt).then_inc(r_root, 1)
            act.wait_ge(n2_sum, PAIRS)
            act.activation(rstd[:, :], ps[7][:, :], ACT.Sqrt, scale=1.0 / CONV_CH, bias=eps_t[:, 0:1]).then_inc(n2_root, 1)
            act.wait_ge(freed["act"], FREED[S_GH + 3][1])
            act.activation(hgo[:, :, :], hgo[:, :, :], ACT.Silu).then_inc(gate2_silu, 1)
            for hd in range(HG):
                act.wait_ge(r_norm, hd + 1)
                act.activation(h_hi[:, PAIRS + hd, :], hq[:, hd, :], ACT.Copy).then_inc(r_hi, 1)
            for i in range(PAIRS):
                act.wait_ge(n2_norm, i + 1)
                act.activation(h_hi[:, i, :], q2T[:, i, :], ACT.Copy).then_inc(n2_hi, 1)
            for k in range(KD):
                hi(S_OUT2 + k + 4)
                square(4, k)
            root(4)
            norm_hi(4)
            ffn_act(S_UP2, 1)
            act_down(S_DOWN2, 5)
            root(5)
            for t in range(QT):
                act.wait_ge(y_turned, t + 1)
                act.activation(y_out[:, t, 0:512], ps[t][:, :], ACT.Copy).then_inc(y_copied[0], 1)

        @block.vector
        def _(dve):
            chain = [0]

            def link(ins):
                chain[0] += 1
                ins.then_inc(dve_chain, 1)
                dve.wait_ge(dve_chain, chain[0])

            def norm(n, gain, shift=None):
                dve.wait_ge(rooted, n + 1)
                dve.reciprocal(rstd[:, :], rstd[:, :]).then_inc(inverted, 1)
                dve.wait_ge(inverted, n + 1)
                if n in (2, 5):
                    for k in range(KD):
                        dve.scalar_tensor_tensor(out=xT[:, k, :], in0=xT[:, k, :], scalar=gain(k), in1=rstd[:, :],
                                                 op0=ALU.mult, op1=ALU.mult).then_inc(x2_ready if n == 2 else y_ready, 1)
                    return
                b = HN_BASE[n]
                for k in range(KD + 1):
                    if k < KD:
                        if k >= 2:
                            dve.wait_ge(n_lo, b + k - 1)
                        t = hn[:, k % 2, :]
                        ins = dve.scalar_tensor_tensor(out=t, in0=xT[:, k, :], scalar=gain(k), in1=rstd[:, :],
                                                       op0=ALU.mult, op1=ALU.mult)
                        if shift is not None:
                            link(ins)
                            ins = dve.tensor_scalar(t, t, shift(k), None, ALU.add)
                        ins.then_inc(normed, 1)
                    if k:
                        dve.wait_ge(n_hi, b + k)
                        dve.tensor_tensor(h_lo[:, k - 1, :], hn[:, (k - 1) % 2, :], h_hi[:, k - 1, :].bitcast(F32),
                                          ALU.subtract).then_inc(n_lo, 1)

            for k in range(KD):
                dve.wait_ge(x_turned, k + 1)
                dve.tensor_copy(xT[:, k, :], ps[k % 4][:, :]).then_inc(x_copied, 1)
            dve.wait_ge(small_turned, 1)
            n = min(512, NSM * P)
            dve.tensor_copy(sm[:, 0:n], ps[4][:, 0:n])
            link(dve.tensor_copy(sm[:, n:NSM * P], ps[5][:, 0:NSM * P - n]))
            dve.sem_inc(small_ready, 1)
            norm(0, lambda k: col("norm1_g", k))

            l0, l1 = col("hgrn_lb_logits_2", 0, HG), col("hgrn_lb_logits_2", HG, HG)
            link(dve.tensor_tensor(lower[:, 2, :], l0, l1, ALU.max))
            dve.tensor_tensor(lower[:, 0, :], l0, lower[:, 2, :], ALU.subtract)
            dve.tensor_tensor(lower[:, 1, :], l1, lower[:, 2, :], ALU.subtract).then_inc(lb_max, 1)
            dve.wait_ge(misc_loaded, 48)
            dve.tensor_scalar(sinks[:, 1, :], sinks[:, 0, :], -1.0, None, ALU.mult).then_inc(cond_ready, 1)
            dve.wait_ge(lb_exp, 1)
            link(dve.tensor_tensor(lower[:, 2, :], lower[:, 0, :], lower[:, 1, :], ALU.add))
            link(dve.reciprocal(lower[:, 2, :], lower[:, 2, :]))
            link(dve.tensor_tensor(lower[:, 2, :], lower[:, 0, :], lower[:, 2, :], ALU.mult))
            dve.tensor_scalar(lower[:, 3, :], lower[:, 2, :], -1.0, 1.0, ALU.mult, ALU.add).then_inc(lb_ready, 1)

            dve.wait_ge(wg_split_hi, 1)
            dve.tensor_tensor(wg_lo[:, :, :], wg[:, :, :], wg_hi[:, :, :].bitcast(F32), ALU.subtract).then_inc(wg_split, 1)
            for n in range(2):
                dve.wait_ge(tile_done, n + 1)
                src = ps[BANK[n]]
                pe_v = col(("pe_k", "pe_v")[n], 0, CMP_BLOCK)
                for half in range(2):
                    b = blk[:, n, half * 16:(half + 1) * 16, :]
                    tok = src[:, half * 16:half * 16 + NCMP * CMP_STRIDE].rearrange("p (m i) -> p i m", i=CMP_STRIDE)
                    ins = dve.tensor_tensor(b, tok, pe_v[:, half * 16:(half + 1) * 16].unsqueeze(2)
                                            .to_broadcast([P, 16, NCMP]), ALU.add)
                ins.then_inc(freed["dve"], 1)
            dve.wait_ge(hid_done, 2)
            H = lambda n: hc[:, n, :, :, 0:NCMP]
            for g in range(2):
                ins = dve.tensor_copy(hc[:, 0, :, g, 0:NCMP],
                                      ps[3 + g][:, 0:64].rearrange("p (n m) -> p n m", n=2)[:, :, 0:NCMP])
            link(ins)
            link(dve.tensor_tensor(H(1), H(0), H(0), ALU.mult))
            link(dve.tensor_scalar(H(1), H(1), 0.044715 * GELU_C, GELU_C, ALU.mult, ALU.add))
            dve.tensor_tensor(H(1), H(1), H(0), ALU.mult).then_inc(gelu_parts, 1)

            def glu(n):
                s = S_U + n // 2 * 4 + n % 2
                dve.wait_ge(freed["act"], FREED[s + 2][1])
                dve.tensor_tensor(z[:, n, PAD:PAD + T], ps[BANK[s]][:, :], sgt[n % 2], ALU.mult).then_inc(freed["dve"], 1)

            dve.wait_ge(gelu_done, 1)
            link(dve.scalar_tensor_tensor(out=H(2), in0=H(1), scalar=1.0, in1=H(0), op0=ALU.add, op1=ALU.mult))
            dve.tensor_scalar(H(2), H(2), 0.5, None, ALU.mult).then_inc(hid_copied, 1)
            dve.wait_ge(cmp_kv_done, 1)
            dve.tensor_copy(kcT[:, 0:NCMP], ps[5][:, 0:NCMP])
            dve.tensor_copy(vcN[0:NCMP, :], ps[5][0:NCMP, 64:64 + P]).then_inc(cmp_kv_copied, 1)
            glu(0)
            glu(1)
            for g in range(2):
                x = cp[:, g * 16:(g + 1) * 16, 0:NCMP]
                dve.wait_ge(cqk_done, g + 1)
                dve.wait_ge(cbias_ready, HEADS)
                link(dve.tensor_tensor(x, ps[4 + g][:, :].rearrange("p (n m) -> p n m", m=32)[:, :, 0:NCMP],
                                       cbias[:, g * 16:(g + 1) * 16, 0:NCMP], ALU.add))
                low = stat[:, 32:48]
                link(dve.tensor_reduce(low, x, AX.X, ALU.min))
                dve.tensor_tensor(x, x, low.unsqueeze(2).to_broadcast([P, 16, NCMP]), ALU.subtract).then_inc(cx_ready, 1)
                dve.wait_ge(cexp_done, g + 1)
                link(dve.tensor_reduce(low, x, AX.X, ALU.add))
                link(dve.reciprocal(low, low))
                dve.wait_ge(gate_ready, 1)
                r = stat[:, 48:64]
                gc = gates[:, :, 12 * g:12 * g + 12].rearrange("p t (i c) -> p t i c", c=3)[:, :, :, 0]
                link(dve.tensor_tensor(r.rearrange("p (t i) -> p t i", t=QT), low.rearrange("p (t i) -> p t i", t=QT),
                                       gc, ALU.mult))
                link(dve.tensor_tensor(x, x, r.unsqueeze(2).to_broadcast([P, 16, NCMP]), ALU.mult))
                for t in range(QT):
                    xt = cp[:, g * 16 + t * 4:g * 16 + t * 4 + 4, 0:NCMP]
                    v = cvalid[:, t, 0:NCMP].unsqueeze(1).to_broadcast([P, 4, NCMP])
                    ins = dve.tensor_tensor(xt, xt, v, ALU.mult)
                ins.then_inc(cp_ready, 1)
            glu(2)
            glu(3)
            dve.wait_ge(freed["dve"], FREED[S_U + 5][1])

            def tap(n):
                c, m = n % CC, n // CC
                src = z[:, c, m:m + T]
                w = col("conv_dw_w", 4 * m + c)
                if m == 0:
                    ins = dve.tensor_scalar(acc[:, c, :], src, w, col("conv_dw_b", c), ALU.mult, ALU.add)
                else:
                    dve.wait_ge(tap_done, n - CC + 1)
                    ins = dve.scalar_tensor_tensor(out=acc[:, c, :], in0=src, scalar=w, in1=acc[:, c, :],
                                                   op0=ALU.mult, op1=ALU.add)
                ins.then_inc(tap_done, 1)

            for j in range(NI + 1):
                if j < NI:
                    i, g, t = ITEMS[j]
                    L = (t + 1) * P
                    hn_ = j // QT
                    for b in range(2):
                        if b == 0 and t == 0:
                            dve.wait_ge(hbias_ready, hn_ + 1)
                        dve.wait_ge(qk_done, 2 * j + b + 1)
                        if j >= 2:
                            dve.wait_ge((ps_turned, pw_turned)[b], j - 1)
                        q = 2 * (j % 2) + b
                        dve.tensor_tensor_reduce(out=sc[:, j % 2, b, 0:L], in0=ps[4 + b][:, 0:L],
                                                 in1=hbias[hn_ % 2][:, (QT - 1 - t) * P:T], scale=1.0, scalar=3.0e38,
                                                 op0=ALU.add, op1=ALU.min, accum_out=stat[:, q:q + 1])\
                           .then_inc(scores_ready, 1)
                for n in range(4 * j, min(4 * j + 2, CC * CONV_W)):
                    tap(n)
                if j >= 1:
                    m = j - 1
                    L2 = (ITEMS[m][2] + 1) * P
                    dve.wait_ge(pw_turned, m + 1)
                    if m >= 2:
                        dve.wait_ge(pv_done, m - 1)
                    dve.tensor_copy(pT[:, m % 2, 1, 0:L2], ps[7][:, 0:L2]).then_inc(pw_copied, 1)
                for n in range(4 * j + 2, min(4 * j + 4, CC * CONV_W)):
                    tap(n)
                if j < NI:
                    q = 2 * (j % 2)
                    dve.wait_ge(exp_done, 2 * j + 2)
                    link(dve.reciprocal(stat[:, 8 + q:10 + q], stat[:, 4 + q:6 + q]))
                    h = i + 4 * g
                    link(dve.tensor_tensor(stat[:, 8 + q:10 + q], stat[:, 8 + q:10 + q],
                                           gates[:, t, 3 * h + 1:3 * h + 3], ALU.mult))
                    for b in range(2):
                        x = sc[:, j % 2, b, 0:L]
                        ins = dve.tensor_scalar(x, x, stat[:, 8 + q + b:9 + q + b], None, ALU.mult)
                    ins.then_inc(p_ready, 1)

            for i in range(PAIRS):
                dve.wait_ge(att_hi_done, i + 1)
                dve.tensor_tensor(att_lo[:, i, :], qT[:, i, :], att_hi[:, i, :].bitcast(F32),
                                  ALU.subtract).then_inc(att_lo_done, 1)
            dve.wait_ge(ln_sum, 1)
            for c in range(CC):
                dve.scalar_tensor_tensor(out=acc[:, c, :], in0=ps[4][:, :], scalar=-1.0 / CONV_CH, in1=acc[:, c, :],
                                         op0=ALU.mult, op1=ALU.add).then_inc(ln_centred, 1)

            def gated_attention(m):
                s = S_ATTN + m
                dve.wait_ge(gate_sig, m // 4 + 1)
                dve.wait_ge(tile_done, s + 1)
                dve.tensor_tensor(mg[:, m, :], ps[BANK[s]][:, :], mg[:, m, :], ALU.mult).then_inc(freed["dve"], 1)

            gated_attention(0)
            gated_attention(1)
            dve.wait_ge(ln_root, 1)
            link(dve.reciprocal(rstd[:, :], rstd[:, :]))
            for c in range(CC):
                dve.tensor_tensor(acc[:, c, :], acc[:, c, :], rstd[:, :], ALU.mult).then_inc(ln_norm, 1)
            for c in range(CC):
                dve.wait_ge(cv_hi_done, c + 1)
                dve.tensor_tensor(cv_lo[:, c, :], acc[:, c, :], cv_hi[:, c, :].bitcast(F32),
                                  ALU.subtract).then_inc(cv_lo_done, 1)
            for m in range(2, KD):
                gated_attention(m)
            for m in range(KD + 1):
                if m < KD:
                    s = S_CONV + m
                    dve.wait_ge(gate_sig, 3 + m // 4)
                    dve.wait_ge(tile_done, s + 1)
                    dve.tensor_tensor(mg[:, KD + m, :], ps[BANK[s]][:, :], mg[:, KD + m, :], ALU.mult)\
                       .then_inc(freed["dve"], 1)
                    dve.wait_ge(freed["dve"], FREED[s][1])
                    dve.tensor_tensor(mg[:, m, :], mg[:, m, :], mg[:, KD + m, :], ALU.add).then_inc(merged, 1)
                if m:
                    dve.wait_ge(m_hi, m)
                    dve.tensor_tensor(h_lo[:, m - 1, :], mg[:, m - 1, :], h_hi[:, m - 1, :].bitcast(F32),
                                      ALU.subtract).then_inc(m_lo, 1)
            for k in range(KD):
                s = S_OUT + k
                dve.wait_ge(tile_done, s + 1)
                dve.tensor_tensor(xT[:, k, :], ps[BANK[s]][:, :], xT[:, k, :], ALU.add).then_inc(freed["dve"], 1)
            norm(1, lambda k: col("norm2_g", k))

            def ffn_dve(s0, second):
                wname = "conv_w_2" if second else "ffn_dw_w"
                wide = FT if second else 2 * FT
                per = 2 if second else 4
                dve.sem_inc(g_lo_done, 2)
                with dve.Fori(0, FT // 2) as i:
                    for j in range(4):
                        half, t = j // 2, j % 2
                        src = ps[BANK[s0 + j]]
                        if half and second:
                            dve.wait_ge(silu_done, i * 2 + (FT + t + 1))
                            dve.wait_ge(tile_done, i * 4 + (s0 + j + 1))
                            dve.tensor_tensor(uv[:, t, :], src[:, :], ua[:, t, :], ALU.mult).then_inc(freed["dve"], 1)
                            continue
                        u = (ua, uv)[half]
                        n = i * per + (second * 2 * FT + j + 1)
                        m = i * 2 + (half * FT + t)
                        dve.wait_ge(biased, n)
                        dve.scalar_tensor_tensor(out=u[:, t, 1:T], in0=src[:, 0:T - 1], scalar=col(wname, m + wide),
                                                 in1=u[:, t, 1:T], op0=ALU.mult, op1=ALU.add).then_inc(tap1_done, 1)
                        dve.wait_ge(tap1_done, n)
                        dve.scalar_tensor_tensor(out=u[:, t, 2:T], in0=src[:, 0:T - 2], scalar=col(wname, m),
                                                 in1=u[:, t, 2:T], op0=ALU.mult, op1=ALU.add).then_inc(freed["dve"], 1)
                    for t in range(2):
                        if second:
                            dve.wait_ge(freed["dve"], i * 4 + (FREED[s0][1] + 2 + t))
                            dve.sem_inc(prod_done, 1)
                        else:
                            dve.wait_ge(silu_done, i * 2 + (t + 1))
                            dve.wait_ge(freed["dve"], i * 4 + (FREED[s0][1] + 2 + t))
                            dve.tensor_tensor(uv[:, t, :], uv[:, t, :], ua[:, t, :], ALU.mult).then_inc(prod_done, 1)
                    for t in range(2):
                        k = i * 2 + t
                        dve.wait_ge(g_hi_done, i * 2 + (second * FT + t + 1))
                        dve.tensor_tensor(g_lo[:, bass.ds(k, 1), :].rearrange("p a n -> p (a n)"), uv[:, t, :],
                                          g_hi[:, bass.ds(k, 1), :].rearrange("p a n -> p (a n)").bitcast(F32),
                                          ALU.subtract).then_inc(g_lo_done, 1)

            ffn_dve(S_UP, 0)
            dve.wait_ge(ada_done, NMOD * KD)
            link(dve.tensor_tensor(mod[:, :], ps[6][:, 0:NMOD * KD], col("ada_b_2", 0, NMOD * KD), ALU.add))
            for n, (name, c) in enumerate((("mix_norm_g_2", KD), ("ffn_norm_g_2", 4 * KD))):
                link(dve.tensor_scalar(gain2[:, n, :], mod[:, c:c + KD], 1.0, None, ALU.add))
                link(dve.tensor_tensor(gain2[:, n, :], gain2[:, n, :], col(name, 0, KD), ALU.mult))
            for k in range(KD):
                s = S_DOWN + k // 2 * 6 + 4 + k % 2
                dve.wait_ge(tile_done, s + 1)
                dve.tensor_tensor(xT[:, k, :], ps[BANK[s]][:, :], xT[:, k, :], ALU.add).then_inc(freed["dve"], 1)
            norm(2, lambda k: col("final_g", k))
            norm(3, lambda k: gain2[:, 0, k:k + 1], lambda k: mod[:, k:k + 1])

            for h in range(HG):
                dve.wait_ge(freed["act"], FREED[S_FH + h][1])
                dve.tensor_scalar(hf[:, h, :], hf[:, h, :], lower[:, 3, h:h + 1], lower[:, 2, h:h + 1],
                                  ALU.mult, ALU.add).then_inc(f_ready, 1)
                dve.wait_ge(f_ready, 2 * h + 1)
                dve.tensor_scalar(hk[:, h, :], hf[:, h, :], -1.0, 1.0, ALU.mult, ALU.add).then_inc(f_ready, 1)
            dve.wait_ge(brow_loaded, 32)

            def biased_rows(s, dst, b0):
                dve.wait_ge(tile_done, s + 1)
                dve.tensor_tensor(dst, ps[BANK[s]][:, :].rearrange("p (t n) -> p t n", t=QT),
                                  brow[:, b0:b0 + P].unsqueeze(1).to_broadcast([P, QT, P]),
                                  ALU.add).then_inc(freed["dve"], 1)

            for h in range(HG):
                biased_rows(S_IH + h, iN[:, :, h * P:(h + 1) * P], P + h * P)
            dve.wait_ge(freed["act"], FREED[S_QH + 3][1])

            def scale_queries(n):
                b = ALL[n]
                if n:
                    dve.wait_ge(lvl_done, n)
                dst = qd[:, :, :].rearrange("p h t -> p (h t)").rearrange("p (m c) -> p m c", c=b)
                dve.tensor_tensor(dst, pairs_of(hq, b)[:, :, 1, :], pairs_of(hf, b)[:, :, 1, :],
                                  ALU.mult).then_inc(q_scaled, 1)

            def merge_decays(n):
                b = ALL[n]
                dve.wait_ge(g_merged, n + 1)
                f = pairs_of(hf, b)
                dve.tensor_tensor(f[:, :, 1, :], f[:, :, 1, :],
                                  f[:, :, 0, b - 1:b].to_broadcast([P, HG * T // (2 * b), b]),
                                  ALU.mult).then_inc(f_merged, 1)
                dve.wait_ge(f_merged, n + 1)

            def take_scores(c):
                kind, heads, n = CHUNKS[c]
                if n is not None and kind > 64:
                    return
                dve.wait_ge(chunk_done, c + 1)
                if n is None:
                    dve.copy_predicated(hs[:, heads[0], :], eye8[:, :], ps[CHUNK_BANK[c % 2]][:, :]).then_inc(sel_done, 1)
                else:
                    half = HG * T // (2 * kind) // 2
                    m0 = half * (heads[0] // 2)
                    sel = lambda x: x.rearrange("p (m c) -> p m c", c=kind)
                    dve.copy_predicated(pairs_of(hs, kind)[:, m0:m0 + half, 1, :], sel(mask[:, n, :]),
                                        sel(ps[CHUNK_BANK[c % 2]][:, :])).then_inc(sel_done, 1)

            def hgrn_step(c):
                take_scores(c)
                nxt = CHUNKS[c + 1][2] if c + 1 < len(CHUNKS) else None
                if nxt is not None and nxt != CHUNKS[c][2]:
                    if nxt:
                        merge_decays(nxt - 1)
                    scale_queries(nxt)

            dve.wait_ge(setup2, 1)
            for s in range(S_Q2, S_GH):
                if s == S_KV2 + 1:
                    biased_rows(s, v2N[:, :, :], 0)
                hgrn_step(s - S_Q2)
            for j in range(NI + 1):
                if j < NI:
                    i, g, t = ITEMS[j]
                    h = i + 4 * g
                    L = P if t == 0 else 2 * P
                    r = j % 2
                    dve.wait_ge(qk2_done, j + 1)
                    if j >= 2:
                        dve.wait_ge(t2_done, j - 1)
                    if j == 0:
                        dve.wait_ge(cond_ready, 3)
                    link(dve.tensor_tensor_reduce(out=sc2[:, r, 0:L], in0=ps[4 + r][:, 0:L], in1=dist2[:, 2 * P - L:],
                                                  scale=1.0, scalar=3.0e38, op0=ALU.add, op1=ALU.min,
                                                  accum_out=stat[:, 16 + r:17 + r]))
                    dve.tensor_scalar(stat[:, 18 + r:19 + r], stat[:, 16 + r:17 + r], sinks[:, 1, h:h + 1], None,
                                      ALU.min).then_inc(s2_ready, 1)
                c = chunk_at(j)
                if c is not None:
                    hgrn_step(c)
                hd = av_at(j - 1)
                if hd is not None:
                    dve.wait_ge(r_sum, hd + 1)
                    dve.tensor_scalar(kd[:, hd, :], ps[R_BANK][:, :], 1.0 / P, EPS, ALU.mult,
                                      ALU.add).then_inc(r_var, 1)
                    dve.wait_ge(r_var, hd + 1)
                    dve.reciprocal(kd[:, hd, :], kd[:, hd, :]).then_inc(r_inv, 1)
                if j < NI:
                    dve.wait_ge(e2_done, 2 * j + 2)
                    link(dve.tensor_tensor(stat[:, 24 + r:25 + r], stat[:, 20 + r:21 + r], stat[:, 22 + r:23 + r], ALU.add))
                    link(dve.reciprocal(stat[:, 24 + r:25 + r], stat[:, 24 + r:25 + r]))
                    dve.tensor_scalar(sc2[:, r, 0:L], sc2[:, r, 0:L], stat[:, 24 + r:25 + r], None,
                                      ALU.mult).then_inc(p2_ready, 1)
            dve.wait_ge(r_root, 1)
            for hd in range(HG):
                dve.wait_ge(av_copied, hd + 1)
                link(dve.tensor_tensor(hq[:, hd, :], hq[:, hd, :], kd[:, hd, :], ALU.mult))
            dve.wait_ge(n2_root, 1)
            link(dve.reciprocal(rstd[:, :], rstd[:, :]))
            for i in range(PAIRS):
                dve.scalar_tensor_tensor(out=q2T[:, i, :], in0=q2T[:, i, :], scalar=col("attn_out_g_2", i),
                                         in1=rstd[:, :], op0=ALU.mult, op1=ALU.mult).then_inc(n2_norm, 1)
            dve.wait_ge(gate2_silu, 1)
            for hd in range(HG):
                dve.scalar_tensor_tensor(out=hq[:, hd, :], in0=hq[:, hd, :], scalar=col("hgrn_out_g_2", hd),
                                         in1=hgo[:, hd, :], op0=ALU.mult, op1=ALU.mult).then_inc(r_norm, 1)
            for i in range(PAIRS):
                dve.wait_ge(n2_hi, i + 1)
                dve.tensor_tensor(h_lo[:, i, :], q2T[:, i, :], h_hi[:, i, :].bitcast(F32), ALU.subtract).then_inc(n2_lo, 1)
            for hd in range(HG):
                dve.wait_ge(r_hi, hd + 1)
                dve.tensor_tensor(h_lo[:, PAIRS + hd, :], hq[:, hd, :], h_hi[:, PAIRS + hd, :].bitcast(F32),
                                  ALU.subtract).then_inc(r_lo, 1)

            def gated_residual(s, k, gate):
                dve.wait_ge(tile_done, s + 1)
                dve.scalar_tensor_tensor(out=xT[:, k, :], in0=ps[BANK[s]][:, :], scalar=mod[:, gate * KD + k:gate * KD + k + 1],
                                         in1=xT[:, k, :], op0=ALU.mult, op1=ALU.add).then_inc(freed["dve"], 1)

            for k in range(KD):
                gated_residual(S_OUT2 + k, k, 2)
            norm(4, lambda k: gain2[:, 1, k:k + 1], lambda k: mod[:, 3 * KD + k:3 * KD + k + 1])
            ffn_dve(S_UP2, 1)
            for k in range(KD):
                gated_residual(S_DOWN2 + k // 2 * 6 + 4 + k % 2, k, 5)
            norm(5, lambda k: col("final_norm_g_2", k))
            for t in range(QT):
                dve.wait_ge(y_turned, QT + t + 1)
                dve.tensor_copy(y_out[:, t, 512:D], ps[4 + t][:, :]).then_inc(y_copied[1], 1)

        @block.tensor
        def _(pe):
            def split_product(out_ap, w, wl, x, xl, first, last):
                pe.matmul(out_ap, w, x, start=first, stop=False)
                pe.matmul(out_ap, w, xl, start=False, stop=False)
                return pe.matmul(out_ap, wl, x, start=False, stop=last)

            def tile(s, x, xl, k0=0, first=True, last=True, part=(0, None), ready=None, signal=True):
                nk = DEPTH_OF[s]
                lo_k, hi_k = part[0], nk if part[1] is None else part[1]
                if lo_k == 0:
                    pe.wait_ge(lo_done, s + 1)
                    if first:
                        wait_bank(pe, s)
                for k in range(lo_k, hi_k):
                    if ready is not None:
                        pe.wait_ge(ready[0], ready[1] + k0 + k + 1)
                    ins = split_product(ps[BANK[s]][:, :], w_hi[s % 4][:, k, :], w_lo[s % 4][:, k, :],
                                        x[:, k0 + k, :], xl[:, k0 + k, :], first and k == 0, last and k == nk - 1)
                if hi_k == nk and signal:
                    ins.then_inc(tile_done, 1)

            def rows_tile(s):
                pe.wait_ge(lo_done, s + 1)
                wait_bank(pe, s)
                for t in range(QT):
                    for k in range(KD):
                        ins = split_product(ps[BANK[s]][:, t * P:(t + 1) * P], h_hi[:, k, t * P:(t + 1) * P],
                                            h_lo[:, k, t * P:(t + 1) * P], w_hi[s % 4][:, k, :], w_lo[s % 4][:, k, :],
                                            k == 0, k == KD - 1)
                ins.then_inc(tile_done, 1)

            def norm_sum(n, k):
                pe.wait_ge(squared, SQ_BASE[n] + k + 1)
                pe.matmul(ps[7][:, :], ones[:, :], sq[:, k % 2, :], start=k == 0, stop=k == KD - 1).then_inc(summed, 1)

            def norm_sums(n):
                for k in range(KD):
                    norm_sum(n, k)

            pe.wait_ge(consts, 1)
            pe.wait_ge(x_loaded, 16 * QT)
            for k in range(KD):
                if k >= 4:
                    pe.wait_ge(x_copied, k - 3)
                for t in range(QT):
                    ins = pe.transpose(ps[k % 4][:, t * P:(t + 1) * P], x_in[:, t, k * P:(k + 1) * P], ident[:, :])
                ins.then_inc(x_turned, 1)
            pe.wait_ge(small_loaded, small_total[0])
            for m in range(NSM):
                ins = pe.transpose(ps[4 + m // 4][:, m % 4 * P:(m % 4 + 1) * P], rows[:, m, :], ident[:, :])
            ins.then_inc(small_turned, 1)
            norm_sums(0)
            pe.wait_ge(x_copied, KD)
            for s in range(S_CMP, S_V):
                tile(s, h_hi, h_lo, ready=(n_lo, 0) if s == 0 else None)
            for s in range(S_V, S_U):
                rows_tile(s)
            pe.wait_ge(wg_split, 1)
            for t in range(QT):
                for k in range(KD):
                    ins = split_product(ps[2][:, t * 24:(t + 1) * 24], h_hi[:, k, t * P:(t + 1) * P],
                                        h_lo[:, k, t * P:(t + 1) * P], wg_hi[:, k, :], wg_lo[:, k, :],
                                        k == 0, k == KD - 1)
            ins.then_inc(gate_done, 1)
            pe.wait_ge(w1_loaded, 64)
            pe.wait_ge(freed["dve"], FREED[1][1])
            for g in range(2):
                for n in range(2):
                    for m in range(CMP_BLOCK):
                        ins = pe.matmul(ps[3 + g][:, n * 32:n * 32 + NCMP], w1[n][g * DH:(g + 1) * DH, m, :],
                                        blk[g * DH:(g + 1) * DH, n, m, :], start=m == 0, stop=m == CMP_BLOCK - 1)
                ins.then_inc(hid_done, 1)
            for s in range(S_U, S_MERGE):
                tile(s, h_hi, h_lo)
                if s == S_U + 1:
                    pe.wait_ge(hid_copied, 1)
                    pe.wait_ge(misc_loaded, 48)
                    for g in range(2):
                        pe.matmul(ps[5][g * DH:(g + 1) * DH, 0:NCMP], w2[:, 0, :], hc[:, 2, 0, g, 0:NCMP],
                                  start=True, stop=True)
                    for g in range(2):
                        ins = pe.matmul(ps[5][0:NCMP, 64 + g * DH:64 + (g + 1) * DH], hc[:, 2, 1, g, 0:NCMP],
                                        w2[:, 1, :], start=True, stop=True)
                    ins.then_inc(cmp_kv_done, 1)
                if s == S_U + 3:
                    pe.wait_ge(cmp_kv_copied, 1)
                    pe.wait_ge(freed["act"], FREED[S_U - 1][1])
                    for g in range(2):
                        for t in range(QT):
                            for i in range(PAIRS):
                                n = (t * PAIRS + i) * 32
                                ins = pe.matmul(ps[4 + g][:, n:n + NCMP], qT[g * DH:(g + 1) * DH, i, t * P:(t + 1) * P],
                                                kcT[g * DH:(g + 1) * DH, 0:NCMP], start=True, stop=True)
                        ins.then_inc(cqk_done, 1)
            pe.wait_ge(cx_ready, 2)
            pe.wait_ge(gate_ready, 1)
            pe.wait_ge(freed["act"], FREED[S_MERGE - 1][1])
            for j in range(NI + 2):
                if j < NI:
                    i, g, t = ITEMS[j]
                    L = (t + 1) * P
                    grp = slice(g * DH, (g + 1) * DH)
                    for b in range(2):
                        if j:
                            pe.wait_ge(scores_ready, 2 * j + b - 1)
                        pe.matmul(ps[4 + b][:, 0:L], qT[grp, i, t * P:(t + 1) * P], kT[grp, b, 0:L],
                                  start=True, stop=True).then_inc(qk_done, 1)
                    tile(S_MERGE + j // 2, h_hi, h_lo, part=(4 * (j % 2), 4 * (j % 2) + 4))
                if 1 <= j <= NI:
                    m = j - 1
                    i, g, t = ITEMS[m]
                    pe.wait_ge(p_ready, m + 1)
                    pe.wait_ge(cp_ready, 2)
                    if m:
                        pe.wait_ge(pc_copied, m)
                    pe.transpose(ps[3][0:NCMP, 0:P], cp[:, g * 16 + t * 4 + i, 0:NCMP], ident[:, :]).then_inc(pc_turned, 1)
                    for b in range(2):
                        if m:
                            pe.wait_ge((ps_copied, pw_copied)[b], m)
                        for kt in range(t + 1):
                            ins = pe.transpose(ps[6 + b][:, kt * P:(kt + 1) * P], sc[:, m % 2, b, kt * P:(kt + 1) * P],
                                               ident[:, :])
                        ins.then_inc((ps_turned, pw_turned)[b], 1)
                if j >= 2:
                    m = j - 2
                    i, g, t = ITEMS[m]
                    pe.wait_ge(pc_copied, m + 1)
                    pe.wait_ge(ps_copied, m + 1)
                    pe.wait_ge(pw_copied, m + 1)
                    if m and m % (2 * QT) == 0:
                        pe.wait_ge(o_copied, m // (2 * QT))
                    o = ps[2][g * DH:(g + 1) * DH, t * P:(t + 1) * P]
                    for b in range(2):
                        for kt in range(t + 1):
                            pe.matmul(o, vN[:, b, kt, g * DH:(g + 1) * DH], pT[:, m % 2, b, kt * P:(kt + 1) * P],
                                      start=b == 0 and kt == 0, stop=False)
                    pe.matmul(o, vcN[0:NCMP, g * DH:(g + 1) * DH], pcT[0:NCMP, m % 2, :],
                              start=False, stop=True).then_inc(pv_done, 1)
            pe.wait_ge(tap_done, CC * CONV_W)
            for c in range(CC):
                ins = pe.matmul(ps[4][:, :], ones[:, :], acc[:, c, :], start=c == 0, stop=c == CC - 1)
            ins.then_inc(ln_sum, 1)
            tile(S_ATTN, att_hi, att_lo, ready=(att_lo_done, 0))
            for c in range(CC):
                pe.wait_ge(ln_sq, c + 1)
                pe.matmul(ps[5][:, :], ones[:, :], sq[:, c % 2, :], start=c == 0, stop=c == CC - 1).then_inc(ln_sqsum, 1)
            for s in range(S_ATTN + 1, S_CONV):
                tile(s, att_hi, att_lo)
            for s in range(S_CONV, S_OUT):
                tile(s, cv_hi, cv_lo, ready=(cv_lo_done, 0) if s == S_CONV else None)

            def ada_tile(n, buf, count):
                pe.wait_ge(ada_in[buf], count)
                for k in range(KD):
                    ins = pe.matmul(ps[6][:, bass.ds(n, 1)] if not isinstance(n, int) else ps[6][:, n:n + 1],
                                    ada[buf][:, k, :], cond[:, k:k + 1], start=k == 0, stop=k == KD - 1)
                ins.then_inc(ada_done, 1)

            for s in range(S_OUT, S_UP):
                tile(s, h_hi, h_lo, ready=(m_lo, 0) if s == S_OUT else None)
                if s > S_OUT:
                    norm_sum(1, s - S_OUT - 1)
            norm_sum(1, KD - 1)
            pe.wait_ge(cond_ready, 1)
            pe.wait_ge(ps_copied, NI)
            for n in range(ADA_EARLY):
                ada_tile(n, n % 2, 16 * (n // 2 + 1))

            def ffn_pe(s0, norm):
                for k in range(KD):
                    pe.wait_ge(n_lo, HN_BASE[norm] + k + 1)
                with pe.Fori(0, FT // 2) as i:
                    for j in range(4):
                        s = s0 + j
                        pe.wait_ge(lo_done, i * 4 + (s + 1))
                        pe.wait_ge(freed["dve"], i * 4 + (FREED[s][1] - 4))
                        for k in range(KD):
                            ins = split_product(ps[BANK[s]][:, :], w_hi[s % 4][:, k, :], w_lo[s % 4][:, k, :],
                                                h_hi[:, k, :], h_lo[:, k, :], k == 0, k == KD - 1)
                        ins.then_inc(tile_done, 1)
                        if norm == 1:
                            ada_tile(i * 4 + (ADA_EARLY + j), j % 2, i * 32 + 16 * ((ADA_EARLY + j) // 2 + 1))

            ffn_pe(S_UP, 1)

            def down(s0, second):
                norm = 5 if second else 2
                for n in range(24):
                    k0, nk = PARTS[n // 2 % 3]
                    if n >= 6 and n % 6 in (0, 1):
                        norm_sum(norm, (n // 6 - 1) * 2 + n % 6)
                    s = s0 + n
                    tile(s, g_hi, g_lo, k0, first=n // 2 % 3 == 0, last=n // 2 % 3 == 2,
                         ready=(g_lo_done, second * (FT + 2) + 2) if n in (0, 2, 4) else None)
                for k in range(KD - 2, KD):
                    norm_sum(norm, k)

            down(S_DOWN, 0)
            norm_sums(3)
            for s in range(S_FH, S_IH):
                tile(s, h_hi, h_lo, ready=(n_lo, HN_BASE[3]) if s == S_FH else None)
            for s in range(S_IH, S_Q2):
                rows_tile(s)

            def chunk(c):
                kind, heads, n = CHUNKS[c]
                bank = ps[CHUNK_BANK[c % 2]]
                if c >= 2:
                    if c - 2 < N_SEL:
                        pe.wait_ge(sel_done, c - 1)
                    else:
                        pe.wait_ge(off_copied, c - 1 - N_SEL)
                if n is None:
                    pe.wait_ge(f_ready, 2 * HG)
                    pe.wait_ge(freed["act"], FREED[S_QH + 3][1])
                    for t in range(QT):
                        tk = slice(t * P, (t + 1) * P)
                        ins = pe.matmul(bank[:, tk], hk[:, heads[0], tk], hq[:, heads[0], tk], start=True, stop=True)
                    ins.then_inc(chunk_done, 1)
                    return
                pe.wait_ge(q_scaled, n + 1)
                if n:
                    pe.wait_ge(k_scaled, n)
                keys = kd if n else hk
                for hd in heads:
                    if kind == 256:
                        todo = [(m * 256, m, 0, 256) for m in range(2)]
                    elif kind == 128:
                        todo = [(hd % 2 * 256 + m * P, 2 * m, m * P, P) for m in range(2)]
                    else:
                        todo = [(hd % 2 * 256 + t * 64, t, t * 64, 64) for t in range(QT)]
                    for at, t, q0, nq in todo:
                        ins = pe.matmul(bank[:, at:at + nq], keys[:, hd, t * P:(t + 1) * P], qd[:, hd, q0:q0 + nq],
                                        start=True, stop=True)
                ins.then_inc(chunk_done, 1)
                if c + 1 == len(CHUNKS) or CHUNKS[c + 1][2] != n:
                    pe.wait_ge(chunk_done, c + 1)
                    pe.sem_inc(lvl_done, 1)

            for s in range(S_Q2, S_GH):
                if s <= S_KV2:
                    tile(s, h_hi, h_lo)
                else:
                    rows_tile(s)
                chunk(s - S_Q2)
            pe.wait_ge(freed["act"], FREED[S_KV2][1])
            pe.wait_ge(freed["dve"], FREED[S_KV2 + 1][1])
            for j in range(NI + 2):
                if j < NI:
                    i, g, t = ITEMS[j]
                    L = P if t == 0 else 2 * P
                    grp = slice(g * DH, (g + 1) * DH)
                    if j >= 2:
                        pe.wait_ge(s2_ready, j - 1)
                    pe.matmul(ps[4 + j % 2][:, 0:L], q2T[grp, i, t * P:(t + 1) * P], k2T[grp, (t + 1) * P - L:(t + 1) * P],
                              start=True, stop=True).then_inc(qk2_done, 1)
                c = chunk_at(j)
                if c is not None:
                    chunk(c)
                hd = av_at(j)
                if hd is not None:
                    pe.wait_ge(sel_done, N_SEL)
                    pe.wait_ge(off_copied, len(CHUNKS) - N_SEL)
                    if hd >= 2:
                        pe.wait_ge(av_copied, hd - 1)
                    for t in range(QT):
                        for k in range(t + 1):
                            if k == t:
                                w = hs[:, hd, t * P:(t + 1) * P]
                            elif (k, t) in OFF_AT:
                                w = off[:, hd, OFF_AT[k, t]:OFF_AT[k, t] + P]
                            ins = pe.matmul(ps[CHUNK_BANK[hd % 2]][:, t * P:(t + 1) * P], iN[:, k, hd * P:(hd + 1) * P],
                                            w, start=k == 0, stop=k == t)
                    ins.then_inc(av_done, 1)
                n = gh_at(j)
                if n is not None:
                    tile(S_GH + n, h_hi, h_lo)
                if 1 <= j <= NI:
                    m = j - 1
                    nk = 1 if ITEMS[m][2] == 0 else 2
                    pe.wait_ge(p2_ready, m + 1)
                    if m:
                        pe.wait_ge(t2_copied, m)
                    for kt in range(nk):
                        ins = pe.transpose(ps[6][:, kt * P:(kt + 1) * P], sc2[:, m % 2, kt * P:(kt + 1) * P], ident[:, :])
                    ins.then_inc(t2_done, 1)
                if j >= 2:
                    m = j - 2
                    i, g, t = ITEMS[m]
                    nk = 1 if t == 0 else 2
                    pe.wait_ge(t2_copied, m + 1)
                    if m and m % (2 * QT) == 0:
                        pe.wait_ge(o2_copied, m // (2 * QT))
                    for n in range(nk):
                        ins = pe.matmul(ps[2][g * DH:(g + 1) * DH, t * P:(t + 1) * P],
                                        v2N[:, t + 1 - nk + n, g * DH:(g + 1) * DH], pT2[:, m % 2, n * P:(n + 1) * P],
                                        start=n == 0, stop=n == nk - 1)
                    ins.then_inc(pv2_done, 1)
                hd = av_at(j - 1)
                if hd is not None:
                    pe.wait_ge(r_sq, hd + 1)
                    if hd:
                        pe.wait_ge(r_var, hd)
                    pe.matmul(ps[R_BANK][:, :], ones[:, :], sq[:, hd % 2, :], start=True, stop=True).then_inc(r_sum, 1)
            pe.wait_ge(av_copied, HG)
            for i in range(PAIRS):
                pe.wait_ge(n2_sq, i + 1)
                pe.matmul(ps[7][:, :], ones[:, :], sq[:, i % 2, :], start=i == 0, stop=i == PAIRS - 1).then_inc(n2_sum, 1)
            for k in range(PAIRS):
                pe.wait_ge(n2_lo, k + 1)
                pe.wait_ge(r_lo, k + 1)
            for s in range(S_OUT2, S_UP2):
                tile(s, h_hi, h_lo)
                if s > S_OUT2:
                    norm_sum(4, s - S_OUT2 - 1)
            norm_sum(4, KD - 1)
            ffn_pe(S_UP2, 4)
            down(S_DOWN2, 1)
            pe.wait_ge(rooted, 6)
            for half in range(2):
                for t in range(QT):
                    for k in range(4 * half, 4 * half + 4):
                        if t == 0:
                            pe.wait_ge(y_ready, k + 1)
                        ins = pe.transpose(ps[4 * half + t][:, k % 4 * P:(k % 4 + 1) * P], xT[:, k, t * P:(t + 1) * P],
                                           ident[:, :])
                    ins.then_inc(y_turned, 1)


INPUTS = ["x", "norm1_g", "w_in", "cmp_pe_k", "cmp_pe_v", "cmp_k_w1", "cmp_k_w2", "cmp_v_w1", "cmp_v_w2",
          "w_attn_br", "conv_dw_w", "conv_dw_b", "conv_ln_g", "conv_ln_b", "w_conv_br", "w_out", "norm2_g",
          "ffn_w_up", "ffn_dw_w", "ffn_dw_b", "ffn_w_down", "final_g", "c_2", "ada_w_2", "ada_b_2",
          "mix_norm_g_2", "w_in_2", "b_in_2", "attn_sinks_2", "attn_out_g_2", "hgrn_lb_logits_2",
          "hgrn_out_g_2", "w_out_2", "ffn_norm_g_2", "w_up_2", "conv_w_2", "conv_b_2", "w_down_2",
          "final_norm_g_2"]


def kernel(**inputs):
    import concourse.bacc as bacc
    from concourse.bass_utils import run_bass_kernel_spmd as run

    nc = bacc.Bacc("TRN2", target_bir_lowering=False, num_devices=1)
    arrays, aps = {}, {}
    for name in INPUTS:
        arrays[f"in_{name}"] = np.ascontiguousarray(inputs[name])
        aps[name] = nc.dram_tensor(f"in_{name}", arrays[f"in_{name}"].shape, F32, kind="ExternalInput").ap()
    out = nc.dram_tensor("out", (1, T, D), F32, kind="ExternalOutput").ap()
    build(nc, aps, out)
    return run(nc, [arrays], core_ids=[0]).results[0]["out"]
```

```python
import numpy as np
import concourse.bass as bass
from concourse import mybir
from contextlib import ExitStack

F32 = mybir.dt.float32
F32R = mybir.dt.float32r
I32 = mybir.dt.int32
U8 = mybir.dt.uint8
ALU = mybir.AluOpType
ACT = mybir.ActivationFunctionType
AX = mybir.AxisListType

P = 128
D = 1024
T = 512
KD = D // P
QT = T // P
HEADS = 8
DH = 64
PAIRS = HEADS // 2
CMP_BLOCK, CMP_STRIDE = 32, 16
NCMP = (T - CMP_BLOCK) // CMP_STRIDE + 1
CONV_CH, CONV_W = 512, 31
CC = CONV_CH // P
PAD = CONV_W - 1
FFN = 2816
FT = FFN // P
PARTS = [(0, 8), (8, 7), (15, 7)]
MASKED = 1.0e30
EPS = 1e-6
SLOPES = [2.0 ** -(h + 1) for h in range(HEADS)]
SCALE = DH ** -0.5
HG = 4
NMOD = 6
LEVELS = [1, 2, 4, 8, 16, 32, 64]

S_CMP, S_Q, S_K, S_V, S_U, S_MERGE = 0, 2, 6, 8, 10, 18
S_ATTN, S_CONV, S_OUT, S_UP, S_DOWN = 34, 42, 50, 58, 102
S_FH, S_QH, S_IH, S_Q2, S_KV2, S_GH = 126, 130, 134, 138, 142, 144
S_OUT2, S_UP2, S_DOWN2, S_END = 148, 156, 200, 224

ADA_EARLY = 6
ADA_UP = FT


ALL = LEVELS + [128, 256]
GELU_C = 0.7978845608028654

CHUNKS = [(1, (h,), None) for h in range(HG)]
CHUNKS += [(b, (2 * c, 2 * c + 1), n) for n, b in enumerate(ALL[:-1]) for c in range(2)]
CHUNKS += [(256, (h,), len(ALL) - 1) for h in range(HG)]
N_SEL = HG + 2 * len(LEVELS)
CHUNK_BANK = [3, 7]
R_BANK = 1
V_BANK = [2, 4, 2, 4, 5]
OFF_AT = {(0, 1): 0, (2, 3): 128, (0, 2): 256, (0, 3): 384, (1, 2): 512, (1, 3): 640}
EARLY_CHUNKS = S_GH - S_Q2


def chunk_at(j):
    return j + EARLY_CHUNKS if 0 <= j < len(CHUNKS) - EARLY_CHUNKS else None


def off_chunk_at(j):
    c = chunk_at(j)
    return c if c is not None and c >= N_SEL else None


def av_at(j):
    return (j - 20) // 3 if j >= 20 and (j - 20) % 3 == 0 and (j - 20) // 3 < HG else None


def gh_at(j):
    return (j - 19) // 3 if j >= 19 and (j - 19) % 3 == 0 and (j - 19) // 3 < HG else None


def small_rows():
    sizes = [("norm1_g", 8), ("norm2_g", 8), ("final_g", 8), ("mix_norm_g_2", 8), ("ffn_norm_g_2", 8),
             ("final_norm_g_2", 8), ("c_2", 8), ("conv_dw_b", 4), ("conv_ln_g", 4), ("conv_ln_b", 4),
             ("ada_b_2", 48), ("hgrn_out_g_2", 4), ("hgrn_lb_logits_2", 8), ("conv_dw_w", 124),
             ("ffn_dw_w", 132), ("ffn_dw_b", 44), ("conv_w_2", 66), ("conv_b_2", 22),
             ("bq", 4), ("attn_out_g_2", 4), ("bk", 1), ("bv", 1), ("bqh", 4), ("bfh", 4), ("bih", 4), ("bgh", 4),
             ("pe_k", 32), ("pe_v", 32)]
    at, where = 0, {}
    for name, n in sizes:
        where[name] = (at, n)
        at += n
    return where, at


def evacuations():
    bank, freed = {}, {}
    count = {"act": 0, "dve": 0}

    def out(s, who):
        count[who] += 1
        freed[s] = (who, count[who])

    for s in range(S_END):
        if s < S_OUT or S_FH <= s < S_OUT2:
            bank[s] = s % 2 if s < S_GH else 0
            if S_U <= s < S_MERGE and (s - S_U) % 4 >= 2:
                bank[s] = 6 + s % 2
        elif S_DOWN <= s < S_FH or s >= S_DOWN2:
            n = s - (S_DOWN if s < S_FH else S_DOWN2)
            bank[s] = (n // 6 * 2 + n % 2) % 4
        else:
            bank[s] = s % 4
    for s in range(S_END):
        if s < S_Q:
            out(s, "dve")
        elif s < S_U:
            out(s, "act")
        elif s < S_MERGE:
            out(s, "dve" if (s - S_U) % 4 < 2 else "act")
        elif s < S_ATTN:
            out(s, "act")
        elif s < S_DOWN:
            out(s, "dve")
        elif s < S_FH:
            if (s - S_DOWN) % 6 >= 4:
                out(s, "dve")
        elif s < S_OUT2:
            out(s, "act")
        elif s < S_DOWN2:
            out(s, "dve")
        elif (s - S_DOWN2) % 6 >= 4:
            out(s, "dve")
    return bank, freed


def build(nc, a, out):
    where, n_small = small_rows()
    BANK, FREED = evacuations()
    NSM = (n_small + P - 1) // P

    ctx = ExitStack()
    with ctx:
        base = (nc.sbuf_base + 63) // 64 * 64
        end = nc.sbuf_usable_end
        offset = [base]

        def sb(name, shape, dtype=F32, at=None):
            size = int(np.prod(shape[1:])) * (1 if dtype == U8 else 4)
            if at is None:
                at = offset[0]
                offset[0] += (size + 31) // 32 * 32
            assert at + size <= end, (name, at, size, end)
            return nc.alloc_sbuf_tensor_at(name, list(shape), dtype, offset=at)

        def sem(name):
            return nc.alloc_semaphore(name)

        raw = [sb(f"raw{i}", [P, 2048]) for i in range(2)]
        w_hi = [sb(f"w_hi{i}", [P, 8, P], F32R) for i in range(4)]
        w_lo = [sb(f"w_lo{i}", [P, 8, P], F32R) for i in range(4)]
        xT = sb("xT", [P, KD, T])
        h_at = offset[0]
        h_hi = sb("h_hi", [P, KD, T], F32R)
        h_lo = sb("h_lo", [P, KD, T], F32R)
        ident = sb("ident", [P, P])
        ones = sb("ones", [P, P])
        small = sb("small", [P, NSM, P])
        sm = small[:, :, :].rearrange("p a b -> p (a b)")
        rstd = sb("rstd", [P, T])
        sq = sb("sq", [P, 2, T])
        hn = sb("hn", [P, 2, T])
        mod = sb("mod", [P, NMOD * KD])
        gain2 = sb("gain2", [P, 2, KD])
        cond = sb("cond", [P, KD])
        lower = sb("lower", [P, 4, HG])
        nq_bias = sb("nq_bias", [P, PAIRS])
        sinks = sb("sinks", [P, 2, HEADS])
        eps_t = sb("eps_t", [P, 1])
        stat = sb("stat", [P, 64])
        gates = sb("gates", [P, QT, 24])

        G0 = offset[0]

        qT = sb("qT", [P, PAIRS, T])
        kT = sb("kT", [P, 2, T])
        vN = sb("vN", [P, 2, QT, P])
        mg_at = offset[0]
        mg = sb("mg", [P, 2 * KD, T])
        w1 = [sb(f"w1_{n}", [P, CMP_BLOCK, P], at=mg_at + n * 16384) for n in range(2)]
        z = sb("z", [P, CC, PAD + T])
        acc_at = offset[0]
        acc = sb("acc", [P, CC, T])
        rows = sb("rows", [P, NSM, P], at=acc_at)
        wg = sb("wg", [P, KD, 24], at=acc_at + 4096)
        wg_hi = sb("wg_hi", [P, KD, 24], F32R, at=acc_at + 5120)
        wg_lo = sb("wg_lo", [P, KD, 24], F32R, at=acc_at + 6144)
        dist = sb("dist", [P, T])
        cdist = sb("cdist", [P, QT, 32])
        cvalid = sb("cvalid", [P, QT, 32])
        cbias = sb("cbias", [P, QT * HEADS, 32])
        cp = sb("cp", [P, QT * HEADS, 32])
        w2 = sb("w2", [P, 2, DH])
        hc = sb("hc", [P, 3, 2, 2, 32])
        kcT = sb("kcT", [P, 32])
        vcN = sb("vcN", [32, P])
        pcT = sb("pcT", [32, 2, P])
        sc_at = offset[0]
        sc = sb("sc", [P, 2, 2, T])
        pT = sb("pT", [P, 2, 2, T])
        x_in = sb("x_in", [P, QT, D], at=sc_at)
        blk = sb("blk", [P, 2, CMP_BLOCK, NCMP], at=sc_at + 8192)
        att_hi = sb("att_hi", [P, PAIRS, T], F32R, at=sc_at)
        att_lo = sb("att_lo", [P, PAIRS, T], F32R, at=sc_at + 8192)
        z_at = acc_at - 4 * CC * (PAD + T)
        z_at = (z_at + 31) // 32 * 32
        cv_hi = sb("cv_hi", [P, CC, T], F32R, at=z_at)
        kv_at = G0 + 4 * PAIRS * T
        cv_lo = sb("cv_lo", [P, CC, T], F32R, at=kv_at)
        hbias = [sq[:, n, :] for n in range(2)]
        sgt = [hn[:, n, :] for n in range(2)]
        top1 = offset[0]

        offset[0] = G0
        g_hi = sb("g_hi", [P, FT, T], F32R)
        g_lo = sb("g_lo", [P, FT, T], F32R)
        ada_at = offset[0]
        ada = [sb(f"ada{n}", [P, KD, P], at=ada_at + 4096 * n) for n in range(2)]
        ada_sum = [sb(f"ada_sum{n}", [P, P], at=ada_at + 8192 + 512 * n) for n in range(2)]
        ua = sq
        uv = hn
        assert max(top1, ada_at + 9216) <= end

        offset[0] = G0
        q2T = sb("q2T", [P, PAIRS, T])
        k2T = sb("k2T", [P, T])
        v2N = sb("v2N", [P, QT, P])
        hq = sb("hq", [P, HG, T])
        hk = sb("hk", [P, HG, T])
        f_at = offset[0]
        hf = sb("hf", [P, HG, T])
        hgo = sb("hgo", [P, HG, T], at=f_at)
        hg = sb("hg", [P, HG, T])
        iN = sb("iN", [P, QT, T])
        qd = sb("qd", [P, HG, T // 2])
        kd = sb("kd", [P, HG, T])
        hs = sb("hs", [P, HG, T])
        off_at = offset[0]
        off = sb("off", [P, HG, 768])
        mask = sb("mask", [P, len(LEVELS), DH], U8)
        eye8 = sb("eye8", [P, P], U8)
        dist2 = sb("dist2", [P, 2 * P])
        sc2 = sb("sc2", [P, 2, 2 * P])
        pT2 = sb("pT2", [P, 2, 2 * P])
        msk_f = sb("msk_f", [P, P], at=off_at)
        assert offset[0] <= end, (offset[0], end)
        offset[0] = G0
        y_out = sb("y_out", [P, QT, D])

        ps = [nc.alloc_psum_tensor(f"ps{i}", [P, 512], F32) for i in range(8)]

        raw_in = [sem(f"raw_in{i}") for i in range(2)]
        hi_done, lo_done, tile_done = sem("hi_done"), sem("lo_done"), sem("tile_done")
        freed = {"act": sem("freed_by_act"), "dve": sem("freed_by_dve")}
        x_loaded, small_loaded, w1_loaded, wg_loaded = sem("x_loaded"), sem("small_loaded"), sem("w1_loaded"), sem("wg_loaded")
        misc_loaded = sem("misc_loaded")
        consts = sem("consts")
        x_turned, x_copied = sem("x_turned"), sem("x_copied")
        small_turned, small_ready = sem("small_turned"), sem("small_ready")
        squared, summed, rooted, inverted = sem("squared"), sem("summed"), sem("rooted"), sem("inverted")
        normed, n_hi = sem("normed"), sem("n_hi")
        n_lo = [sem("n_lo_even"), sem("n_lo_odd")]
        squared2, summed2, mean_ready, shifted = sem("squared2"), sem("summed2"), sem("mean_ready"), sem("shifted")
        blocks_ready, hid_done, hid_copied, gelu_parts, gelu_done = (
            sem("blocks_ready"), sem("hid_done"), sem("hid_copied"), sem("gelu_parts"), sem("gelu_done"))
        cmp_kv_done, cmp_kv_copied = sem("cmp_kv_done"), sem("cmp_kv_copied")
        wg_split_hi, wg_split, gate_done, gate_ready = sem("wg_split_hi"), sem("wg_split"), sem("gate_done"), sem("gate_ready")
        sig_ready, cbias_ready = sem("sig_ready"), sem("cbias_ready")
        cqk_done, cx_ready, cexp_done, cp_ready = sem("cqk_done"), sem("cx_ready"), sem("cexp_done"), sem("cp_ready")
        hbias_ready, qk_done, scores_ready, exp_done, p_ready = (
            sem("hbias_ready"), sem("qk_done"), sem("scores_ready"), sem("exp_done"), sem("p_ready"))
        pc_turned, ps_turned, pw_turned = sem("pc_turned"), sem("ps_turned"), sem("pw_turned")
        pc_copied, ps_copied, pw_copied = sem("pc_copied"), sem("ps_copied"), sem("pw_copied")
        pv_done, o_copied = sem("pv_done"), sem("o_copied")
        tap_done, ln_sum, ln_centred, ln_sq, ln_sqsum, ln_root, ln_norm, cv_ready, cv_hi_done, cv_lo_done = (
            sem("tap_done"), sem("ln_sum"), sem("ln_centred"), sem("ln_sq"), sem("ln_sqsum"), sem("ln_root"),
            sem("ln_norm"), sem("cv_ready"), sem("cv_hi_done"), sem("cv_lo_done"))
        att_hi_done, att_lo_done, gate_sig = sem("att_hi_done"), sem("att_lo_done"), sem("gate_sig")
        merged, m_hi, m_lo = sem("merged"), sem("m_hi"), sem("m_lo")
        biased, tap1_done, silu_done, prod_done, g_hi_done, g_lo_done = (
            sem("biased"), sem("tap1_done"), sem("silu_done"), sem("prod_done"), sem("g_hi_done"), sem("g_lo_done"))
        ada_in = [sem(f"ada_in{i}") for i in range(2)]
        ada_scaled, ada_summed, ada_done, cond_ready = sem("ada_scaled"), sem("ada_summed"), sem("ada_done"), sem("cond_ready")
        x2_ready = sem("x2_ready")
        lb_max, lb_exp, lb_ready = sem("lb_max"), sem("lb_exp"), sem("lb_ready")
        f_ready, k_scaled, q_scaled, chunk_done, lvl_done, sel_done, off_copied, f_merged, g_merged = (
            sem("f_ready"), sem("k_scaled"), sem("q_scaled"), sem("chunk_done"), sem("lvl_done"),
            sem("sel_done"), sem("off_copied"), sem("f_merged"), sem("g_merged"))
        setup2 = sem("setup2")
        qk2_done, s2_ready, e2_done, sink_exp, p2_ready, t2_done, t2_copied, pv2_done, o2_copied = (
            sem("qk2_done"), sem("s2_ready"), sem("e2_done"), sem("sink_exp"), sem("p2_ready"), sem("t2_done"),
            sem("t2_copied"), sem("pv2_done"), sem("o2_copied"))
        n2_sq, n2_sum, n2_root, n2_norm, n2_hi, n2_lo = (
            sem("n2_sq"), sem("n2_sum"), sem("n2_root"), sem("n2_norm"), sem("n2_hi"), sem("n2_lo"))
        av_done, av_copied, r_sq, r_sum, r_var, r_inv, r_root, r_norm, r_hi, r_lo, gate2_silu = (
            sem("av_done"), sem("av_copied"), sem("r_sq"), sem("r_sum"), sem("r_var"), sem("r_inv"), sem("r_root"),
            sem("r_norm"), sem("r_hi"), sem("r_lo"), sem("gate2_silu"))
        y_ready, y_turned, stored = sem("y_ready"), sem("y_turned"), sem("stored")
        y_copied = [sem("y_copied_act"), sem("y_copied_dve")]
        v_turned, v_copied, hid_rows, hid_turned, sig_turned = (
            sem("v_turned"), sem("v_copied"), sem("hid_rows"), sem("hid_turned"), sem("sig_turned"))
        values_turned, values_copied = sem("values_turned"), sem("values_copied")
        act_chain, dve_chain, pool_chain = sem("act_chain"), sem("dve_chain"), sem("pool_chain")

        def col(name, i=0, n=1):
            at = where[name][0]
            return sm[:, at + i:at + i + n] if isinstance(i, int) else sm[:, bass.ds(i + at, n)]

        def k_tiles(w, rows_from, nk, c0, n=2 * P):
            return w[rows_from:rows_from + nk * P, bass.ds(c0, n)].rearrange("(k p) n -> p k n", p=P)

        def standard(w, c0, u, nk=KD, r0=0):
            return [(raw[u % 2][:, 0:nk * 256].rearrange("p (k n) -> p k n", k=nk), k_tiles(w, r0, nk, c0))]

        def two_columns(w, cols, u, width=P):
            dst = raw[u % 2][:, :].rearrange("p (k n) -> p k n", k=KD)
            return [(dst[:, :, n * width:(n + 1) * width], k_tiles(w, 0, KD, c, width)) for n, c in enumerate(cols)]

        def paired_columns(w, c0, i, u):
            return two_columns(w, [c0 + g * 256 + (i + m) * DH for m in range(2) for g in range(2)], u, DH)

        def paired_rows(w, c0, u, nk_dst=PAIRS, more=None):
            dst = raw[u % 2][:, 0:nk_dst * 256].rearrange("p (k n) -> p k n", k=nk_dst)
            got = [(dst[g * DH:(g + 1) * DH, 0:PAIRS, :],
                    w[g * 256:(g + 1) * 256, c0:c0 + 256].rearrange("(i d) n -> d i n", d=DH)) for g in range(2)]
            if more is not None:
                got.append((dst[:, PAIRS:nk_dst, :], k_tiles(w, PAIRS * P, nk_dst - PAIRS, c0)))
            return got

        w_in, w_in2 = a["w_in"][0], a["w_in_2"][0]
        LOADS = {}
        for n in range(S_END // 2):
            s = 2 * n
            if s < S_Q:
                LOADS[n] = standard(w_in, 512, n)
            elif s < S_K:
                LOADS[n] = paired_columns(w_in, 0, s - S_Q, n)
            elif s < S_V:
                LOADS[n] = two_columns(w_in, [768, 1024], n)
            elif s < S_U:
                LOADS[n] = two_columns(w_in, [896, 1152], n)
            elif s < S_MERGE:
                m = (s - S_U) // 2
                LOADS[n] = standard(w_in, 1304 + (m % 2) * CONV_CH + (m // 2) * 256, n)
            elif s < S_ATTN:
                LOADS[n] = standard(w_in, 2328 + (s - S_MERGE) * P, n)
            elif s < S_CONV:
                LOADS[n] = paired_rows(a["w_attn_br"][0], (s - S_ATTN) * P, n)
            elif s < S_OUT:
                LOADS[n] = standard(a["w_conv_br"][0], (s - S_CONV) * P, n, CC)
            elif s < S_UP:
                LOADS[n] = standard(a["w_out"][0], (s - S_OUT) * P, n)
            elif s < S_DOWN:
                m = (s - S_UP) // 2
                LOADS[n] = standard(a["ffn_w_up"][0], (m % 2) * FFN + (m // 2) * 256, n)
            elif s < S_FH or s >= S_DOWN2:
                w = a["ffn_w_down"][0] if s < S_FH else a["w_down_2"][0]
                m = (s - (S_DOWN if s < S_FH else S_DOWN2)) // 2
                k0, nk = PARTS[m % 3]
                LOADS[n] = standard(w, m // 3 * 256, n, nk, k0 * P)
            elif s < S_QH:
                LOADS[n] = standard(w_in2, 1280 + (s - S_FH) * P, n)
            elif s < S_IH:
                LOADS[n] = standard(w_in2, 768 + (s - S_QH) * P, n)
            elif s < S_Q2:
                LOADS[n] = standard(w_in2, 1792 + (s - S_IH) * P, n)
            elif s < S_KV2:
                LOADS[n] = paired_columns(w_in2, 0, s - S_Q2, n)
            elif s < S_GH:
                LOADS[n] = standard(w_in2, 512, n)
            elif s < S_OUT2:
                LOADS[n] = standard(w_in2, 2304 + (s - S_GH) * P, n)
            elif s < S_UP2:
                LOADS[n] = paired_rows(a["w_out_2"][0], (s - S_OUT2) * P, n, KD, True)
            else:
                m = (s - S_UP2) // 2
                LOADS[n] = standard(a["w_up_2"][0], (m % 2) * FFN + (m // 2) * 256, n)
        RAW_COUNT, total = {}, [0, 0]
        for n in range(S_END // 2):
            total[n % 2] += 16 * len(LOADS[n])
            RAW_COUNT[n] = total[n % 2]
        DEPTH_OF = {s: (4 if S_ATTN <= s < S_OUT else
                        PARTS[(s - (S_DOWN if s < S_FH else S_DOWN2)) // 2 % 3][1]
                        if S_DOWN <= s < S_FH or s >= S_DOWN2 else KD) for s in range(S_END)}

        def wait_bank(eng, s, shift=0):
            prev = max((t for t in range(s) if BANK[t] == BANK[s] and t in FREED), default=None)
            if prev is not None:
                who, n = FREED[prev]
                eng.wait_ge(freed[who], n + shift)

        def x_ready(eng, norm, k):
            if norm == 0:
                eng.wait_ge(x_copied, k + 1)
            else:
                s = {1: S_OUT + k, 4: S_OUT2 + k,
                     2: S_DOWN + k // 2 * 6 + 4 + k % 2, 5: S_DOWN2 + k // 2 * 6 + 4 + k % 2}[norm]
                eng.wait_ge(freed["dve"], FREED[s][1])

        SQ_BASE = {0: 0, 1: 8, 2: 16, 4: 24, 5: 32}
        HN_BASE = {0: 0, 1: 8, 3: 16, 4: 24}
        ROOT = {0: 1, 1: 2, 3: 3, 2: 4, 4: 5, 5: 6}

        def lo_ready(eng, norm, k):
            eng.wait_ge(n_lo[k % 2], (HN_BASE[norm] + k) // 2 + 1)

        ITEMS = [(i, g, t) for i in range(PAIRS) for g in range(2) for t in range(QT)]
        NI = len(ITEMS)
        FIRST_KEYS = [max(0, t - 1) for t in range(QT)]

        def small_dmas(pool):
            flat = rows[:, :, :]

            def put(name, rows_ap, c0=0, c1=P):
                at, n = where[name]
                done = 0
                while done < n:
                    r, m = (at + done) % P, (at + done) // P
                    take = min(n - done, P - r)
                    pool.dma_start(flat[r:r + take, m, c0:c1], rows_ap[done:done + take, :]).then_inc(small_loaded, 16)
                    count[0] += 16
                    done += take

            count = [0]
            as_rows = lambda v, n: v.rearrange("a (r c) -> (a r) c", c=n)
            for name in ("norm1_g", "norm2_g", "mix_norm_g_2", "ffn_norm_g_2", "c_2", "conv_dw_b", "conv_ln_g",
                         "conv_ln_b", "ada_b_2", "hgrn_out_g_2", "hgrn_lb_logits_2", "ffn_dw_b", "conv_b_2"):
                put(name, as_rows(a[name], P))
            for name in ("final_g", "final_norm_g_2"):
                put(name, a[name].rearrange("(r c) -> r c", c=P))
            for name in ("conv_dw_w", "ffn_dw_w", "conv_w_2"):
                put(name, as_rows(a[name][0], P))
            b = a["b_in_2"]
            for name, c0, c1 in (("bk", 512, 640), ("bv", 640, 768), ("bqh", 768, 1280), ("bfh", 1280, 1792),
                                 ("bih", 1792, 2304), ("bgh", 2304, 2816)):
                put(name, as_rows(b[:, c0:c1], P))
            for g in range(2):
                put("bq", as_rows(b[:, g * 256:(g + 1) * 256], DH), g * DH, (g + 1) * DH)
                put("attn_out_g_2", as_rows(a["attn_out_g_2"][:, g * 256:(g + 1) * 256], DH), g * DH, (g + 1) * DH)
                put("pe_k", a["cmp_pe_k"][0], g * DH, (g + 1) * DH)
                put("pe_v", a["cmp_pe_v"][0], g * DH, (g + 1) * DH)
            small_total[0] = count[0]

        small_total = [0]

        def tables2(pool, link):
            pool.wait_ge(tile_done, S_FH)
            link(pool.memset(dist2[:, :], 0.0))
            link(pool.affine_select(out=dist2[:, :], in_=dist2[:, :], compare_op=ALU.is_ge, fill=MASKED,
                                    base=P, pattern=[[-1, 2 * P]], channel_multiplier=1))
            link(pool.affine_select(out=dist2[:, :], in_=dist2[:, :], compare_op=ALU.is_ge, fill=MASKED,
                                    base=-1, pattern=[[1, 2 * P]], channel_multiplier=-1))
            link(pool.memset(hg[:, :, :], 1.0))
            link(pool.memset(kd[:, :, :], 0.0))
            link(pool.memset(hs[:, :, :], 0.0))
            link(pool.memset(msk_f[:, :], 0.0))
            link(pool.affine_select(out=msk_f[:, :], in_=msk_f[:, :], compare_op=ALU.not_equal, fill=1.0, base=0,
                                    pattern=[[-1, P]], channel_multiplier=1))
            link(pool.tensor_copy(eye8[:, :], msk_f[:, :]))
            for n, b in enumerate(LEVELS):
                nb = P // (2 * b)
                v = msk_f[:, 0:DH].rearrange("p (m c) -> p m c", m=nb)
                link(pool.memset(msk_f[:, 0:DH], 1.0))
                link(pool.affine_select(out=v, in_=v, compare_op=ALU.is_ge, fill=0.0, base=0,
                                        pattern=[[-2 * b, nb], [0, b]], channel_multiplier=1))
                link(pool.affine_select(out=v, in_=v, compare_op=ALU.is_ge, fill=0.0, base=b - 1,
                                        pattern=[[2 * b, nb], [0, b]], channel_multiplier=-1))
                link(pool.tensor_copy(mask[:, n, :], msk_f[:, 0:DH]))
            pool.memset(msk_f[:, 0:1], 0.0).then_inc(setup2, 1)

        def pairs_of(x, b):
            return x[:, :, :].rearrange("p h t -> p (h t)").rearrange("p (m e c) -> p m e c", e=2, c=b)

        def hgrn_pool(pool, lo):
            s = S_Q2
            pool.wait_ge(f_ready, 2 * HG)
            for n, b in enumerate(ALL):
                g, f, k, kk = pairs_of(hg, b), pairs_of(hf, b), pairs_of(hk, b), pairs_of(kd, b)
                if n:
                    if n >= 2:
                        pool.wait_ge(lvl_done, n)
                    pool.tensor_tensor(kk[:, :, 0, :], k[:, :, 0, :], g[:, :, 0, :], ALU.mult).then_inc(k_scaled, 1)
                if n < len(ALL) - 1:
                    if n:
                        pool.wait_ge(f_merged, n)
                    pool.tensor_tensor(g[:, :, 0, :], g[:, :, 0, :],
                                       f[:, :, 1, b - 1:b].to_broadcast([P, HG * T // (2 * b), b]),
                                       ALU.mult).then_inc(g_merged, 1)
                    pool.wait_ge(g_merged, n + 1)
                while s < (S_GH, S_GH + 4)[n > 0]:
                    lo(s)
                    s += 1
            while s < S_UP2 + 4:
                lo(s)
                s += 1

        block = ctx.enter_context(nc.Block())

        @block.sync
        def _(sp):
            for t in range(QT):
                sp.dma_start(x_in[:, t, :], a["x"][0, t * P:(t + 1) * P, :]).then_inc(x_loaded, 16)

            def unit(n):
                if n >= 2:
                    sp.wait_ge(lo_done, 2 * n - 2)
                for dst, src in LOADS[n]:
                    sp.dma_start(dst, src).then_inc(raw_in[n % 2], 16)

            unit(0)
            unit(1)
            for n, w in enumerate(("cmp_k_w1", "cmp_v_w1")):
                for g in range(2):
                    sp.dma_start(w1[n][g * DH:(g + 1) * DH, :, :],
                                 a[w][0].rearrange("(i d) n -> d i n", d=DH)).then_inc(w1_loaded, 16)

            def ada_load(n, c0=None, count=None):
                if n >= 2:
                    sp.wait_ge(ada_summed, n - 1 if count is None else count)
                sp.dma_start(ada[n % 2][:, :, :],
                             k_tiles(a["ada_w_2"][0], 0, KD, n * P if c0 is None else c0, P)).then_inc(ada_in[n % 2], 16)

            for n in range(2, S_OUT // 2 + 1):
                unit(n)
            sp.wait_ge(tile_done, S_CONV)
            for n in range(2):
                ada_load(n)
            for n in range(S_OUT // 2 + 1, S_OUT // 2 + 4):
                unit(n)
            for n in range(3):
                ada_load(2 * n + 2)
                unit(S_UP // 2 + n)
                ada_load(2 * n + 3)
            unit(S_UP // 2 + 3)
            w = a["ffn_w_up"][0]
            with sp.Fori(0, FT // 2 - 2) as i:
                for half in range(2):
                    n = S_UP // 2 + 4 + half
                    sp.wait_ge(lo_done, i * 4 + (2 * n - 2))
                    sp.dma_start(raw[n % 2][:, :].rearrange("p (k n) -> p k n", k=KD),
                                 k_tiles(w, 0, KD, i * 256 + (512 + half * FFN))).then_inc(raw_in[n % 2], 16)
                    n = ADA_EARLY + 2 + half
                    ada_load(n, i * 256 + n * P, i * 2 + (n - 1))
            n = ADA_EARLY + ADA_UP - 2
            for m in range(4):
                unit(S_DOWN // 2 + m)
                ada_load(n + m)
            for m in range(24):
                if m % 2:
                    unit((S_DOWN + 7 + m) // 2)
                if n + 4 + m < NMOD * KD:
                    ada_load(n + 4 + m)
            for n in range((S_FH + 8) // 2, S_UP2 // 2):
                unit(n)
            w = a["w_up_2"][0]
            u0 = S_UP2 // 2
            with sp.Fori(0, FT // 2) as i:
                for half in range(2):
                    n = u0 + half
                    sp.wait_ge(lo_done, i * 4 + (2 * n - 2))
                    sp.dma_start(raw[n % 2][:, :].rearrange("p (k n) -> p k n", k=KD),
                                 k_tiles(w, 0, KD, i * 256 + half * FFN)).then_inc(raw_in[n % 2], 16)
            for n in range(S_DOWN2 // 2, S_END // 2):
                unit(n)
            for t in range(QT):
                for half in range(2):
                    sp.wait_ge(y_copied[half], t + 1)
                sp.dma_start(out[0, t * P:(t + 1) * P, :], y_out[:, t, :]).then_inc(stored, 16)
            sp.wait_ge(stored, 16 * QT)

        @block.gpsimd
        def _(pool):
            chain = [0]

            def link(ins):
                chain[0] += 1
                ins.then_inc(pool_chain, 1)
                pool.wait_ge(pool_chain, chain[0])

            link(pool.memset(ident[:, :], 0.0))
            link(pool.affine_select(out=ident[:, :], in_=ident[:, :], compare_op=ALU.not_equal, fill=1.0,
                                    base=0, pattern=[[-1, P]], channel_multiplier=1))
            pool.memset(eps_t[:, :], EPS)
            pool.memset(ones[:, :], 1.0).then_inc(consts, 1)
            link(pool.memset(rows[:, NSM - 1, :], 0.0))
            small_dmas(pool)
            link(pool.iota(dist[:, :], [[-1, T]], base=T - P, channel_multiplier=1,
                           allow_small_or_imprecise_dtypes=True))
            link(pool.affine_select(out=dist[:, :], in_=dist[:, :], compare_op=ALU.is_ge, fill=MASKED,
                                    base=T - P, pattern=[[-1, T]], channel_multiplier=1))
            cpat = [[P, QT], [-CMP_STRIDE, 32]]
            link(pool.iota(cdist[:, :, :], cpat, base=1 - CMP_BLOCK, channel_multiplier=1,
                           allow_small_or_imprecise_dtypes=True))
            link(pool.affine_select(out=cdist[:, :, :], in_=cdist[:, :, :], compare_op=ALU.is_ge, fill=MASKED,
                                    base=1 - CMP_BLOCK, pattern=cpat, channel_multiplier=1))
            link(pool.memset(cvalid[:, :, :], 1.0))
            pool.affine_select(out=cvalid[:, :, :], in_=cvalid[:, :, :], compare_op=ALU.is_ge, fill=0.0,
                               base=1 - CMP_BLOCK, pattern=cpat, channel_multiplier=1).then_inc(consts, 1)
            pool.memset(z[:, :, 0:PAD], 0.0).then_inc(consts, 1)

            def lo(s, slot=None, count=None):
                pool.wait_ge(hi_done, s + 1 if count is None else count)
                slot = s if slot is None else slot
                nk = 8 if count is not None else DEPTH_OF[s]
                part = raw[slot // 2 % 2][:, 0:nk * 256].rearrange("p (k n) -> p k n", k=nk)
                pool.tensor_tensor(w_lo[slot % 4][:, 0:nk, :], part[:, :, slot % 2 * P:(slot % 2 + 1) * P],
                                   w_hi[slot % 4][:, 0:nk, :].bitcast(F32), ALU.subtract).then_inc(lo_done, 1)

            def norm_lo(norm):
                for k in range(1, KD, 2):
                    pool.wait_ge(n_hi, HN_BASE[norm] + k + 1)
                    pool.tensor_tensor(h_lo[:, k, :], hn[:, 1, :], h_hi[:, k, :].bitcast(F32),
                                       ALU.subtract).then_inc(n_lo[1], 1)

            for s in range(S_UP + 4):
                lo(s)
                if s == 3:
                    norm_lo(0)
            norm_lo(1)
            with pool.Fori(0, FT // 2 - 1) as i:
                for j in range(4):
                    lo(None, S_UP + j, i * 4 + (S_UP + j + 5))
            for s in range(S_DOWN, S_Q2):
                lo(s)
                if s == S_FH + 3:
                    norm_lo(3)
                    tables2(pool, link)
            hgrn_pool(pool, lo)
            norm_lo(4)
            with pool.Fori(0, FT // 2 - 1) as i:
                for j in range(4):
                    lo(None, S_UP2 + j, i * 4 + (S_UP2 + j + 5))
            for s in range(S_DOWN2, S_END):
                lo(s)

        @block.scalar
        def _(act):
            chain = [0]

            def link(ins):
                chain[0] += 1
                ins.then_inc(act_chain, 1)
                act.wait_ge(act_chain, chain[0])

            def hi(s):
                if s >= S_END:
                    return
                u = s // 2
                act.wait_ge(raw_in[u % 2], RAW_COUNT[u])
                if s >= 4:
                    act.wait_ge(tile_done, s - 3)
                nk = DEPTH_OF[s]
                part = raw[u % 2][:, 0:nk * 256].rearrange("p (k n) -> p k n", k=nk)
                act.activation(w_hi[s % 4][:, 0:nk, :], part[:, :, s % 2 * P:(s % 2 + 1) * P],
                               ACT.Copy).then_inc(hi_done, 1)

            def evac(s, dst, func=ACT.Copy, src=None, **kw):
                act.wait_ge(tile_done, s + 1)
                act.activation(dst, ps[BANK[s]][:, :] if src is None else src, func, **kw).then_inc(freed["act"], 1)

            def square(norm, k):
                x_ready(act, norm, k)
                if k >= 2:
                    act.wait_ge(summed, SQ_BASE[norm] + k - 1)
                act.activation(sq[:, k % 2, :], xT[:, k, :], ACT.Square).then_inc(squared, 1)

            def root(norm):
                act.wait_ge(summed, SQ_BASE[norm] + KD)
                act.activation(rstd[:, :], ps[7][:, :], ACT.Sqrt, scale=1.0 / D, bias=eps_t[:, 0:1]).then_inc(rooted, 1)

            def norm_hi(norm, shift=None):
                for k in range(KD):
                    act.wait_ge(normed, HN_BASE[norm] + k + 1)
                    t = hn[:, k % 2, :]
                    if shift is None:
                        act.activation(h_hi[:, k, :], t, ACT.Copy).then_inc(n_hi, 1)
                    elif k % 2 == 0:
                        act.activation(h_hi[:, k, :], t, ACT.Identity, bias=shift(k)).then_inc(n_hi, 1)
                    else:
                        act.activation(t, t, ACT.Identity, bias=shift(k)).then_inc(shifted, 1)
                        act.wait_ge(shifted, (HN_BASE[norm] - HN_BASE[3] + k) // 2 + 1)
                        act.activation(h_hi[:, k, :], t, ACT.Copy).then_inc(n_hi, 1)

            act.dma_start(w2[:, 0, :], a["cmp_k_w2"][0]).then_inc(misc_loaded, 16)
            act.dma_start(w2[:, 1, :], a["cmp_v_w2"][0]).then_inc(misc_loaded, 16)
            act.dma_start(sinks[:, 0, :], a["attn_sinks_2"].to_broadcast([P, HEADS])).then_inc(misc_loaded, 16)
            act.dma_start(wg[:, :, :], k_tiles(w_in, 0, KD, 1280, 24)).then_inc(wg_loaded, 16)
            for s in range(2):
                hi(s)
            for k in range(KD):
                square(0, k)
            root(0)
            for s in range(2, 4):
                hi(s)
            norm_hi(0)
            act.wait_ge(small_ready, 1)
            act.activation(cond[:, :], col("c_2", 0, KD), ACT.Silu).then_inc(cond_ready, 1)
            act.activation(nq_bias[:, :], col("bq", 0, PAIRS), ACT.Copy, scale=-SCALE).then_inc(cond_ready, 1)
            act.wait_ge(lb_max, 1)
            act.activation(lower[:, 0:2, :], lower[:, 0:2, :], ACT.Exp).then_inc(lb_exp, 1)
            act.wait_ge(consts, 3)
            for h in range(HEADS):
                g, i = divmod(h, PAIRS)
                dst = cbias[:, g * 16:(g + 1) * 16, :].rearrange("p (t i) n -> p t i n", i=PAIRS)[:, :, i, :]
                act.activation(dst, cdist[:, :, :], ACT.Copy, scale=SLOPES[h]).then_inc(cbias_ready, 1)

            act.wait_ge(wg_loaded, 16)
            act.activation(wg_hi[:, :, :], wg[:, :, :], ACT.Copy).then_inc(wg_split_hi, 1)
            for s in range(S_CMP, S_U):
                hi(s + 4)
                if s < S_Q:
                    continue
                if s < S_K:
                    evac(s, qT[:, s - S_Q, :], scale=-SCALE)
                elif s < S_V:
                    evac(s, kT[:, s - S_K, :])
                else:
                    evac(s, sq[:, s - S_V, :])
            act.wait_ge(gate_done, 1)
            act.activation(hn[0:24, 0, :], ps[2][0:24, :], ACT.Sigmoid).then_inc(gate_ready, 1)
            for n in range(2):
                act.wait_ge(v_turned, n + 1)
                act.activation(vN[:, n, :, :].rearrange("p t n -> p (t n)"), ps[6 + n][:, :], ACT.Copy).then_inc(v_copied, 1)
            for s in range(S_U, S_MERGE):
                if s == S_U + 1:
                    act.wait_ge(gelu_parts, 1)
                    act.activation(hc[:, 1, :, :, 0:NCMP], hc[:, 1, :, :, 0:NCMP], ACT.Tanh).then_inc(gelu_done, 1)
                hi(s + 4)
                n = s - S_U
                if n % 4 >= 2:
                    j = n // 4 * 2 + n % 2
                    if j == 0:
                        act.wait_ge(sig_turned, 1)
                        act.wait_ge(hid_turned, 1)
                    if j >= 2:
                        act.wait_ge(freed["dve"], FREED[S_U + (n // 4 - 1) * 4 + n % 2][1])
                    act.wait_ge(tile_done, s + 1)
                    act.activation(sgt[j % 2], ps[BANK[s]][:, :], ACT.Sigmoid).then_inc(freed["act"], 1)
            for c in range(2):
                act.wait_ge(cx_ready, c + 1)
                x = cp[:, c * 16:(c + 1) * 16, 0:NCMP]
                act.activation(x, x, ACT.Exp, scale=-1.0).then_inc(cexp_done, 1)

            def head_bias(n):
                i, g, _ = ITEMS[n * QT]
                if n >= 2:
                    act.wait_ge(scores_ready, 2 * QT * (n - 1))
                act.activation(hbias[n % 2], dist[:, :], ACT.Copy, scale=SLOPES[i + 4 * g]).then_inc(hbias_ready, 1)

            head_bias(0)
            for j in range(NI + 2):
                if j < NI:
                    i, g, t = ITEMS[j]
                    if t == 0 and j // QT + 1 < HEADS:
                        head_bias(j // QT + 1)
                    L = (t + 1) * P
                    for b in range(2):
                        act.wait_ge(scores_ready, 2 * j + b + 1)
                        x = sc[:, j % 2, b, 0:L]
                        act.activation(x, x, ACT.Exp, scale=-1.0, bias=stat[:, 2 * (j % 2) + b:2 * (j % 2) + b + 1],
                                       accum_out=stat[:, 4 + 2 * (j % 2) + b:5 + 2 * (j % 2) + b]).then_inc(exp_done, 1)
                if j < NI and j % 2 == 0:
                    hi(S_MERGE + j // 2 + 4)
                    if j >= 2:
                        s = S_MERGE + j // 2 - 1
                        evac(s, mg[:, s - S_MERGE, :])
                if 1 <= j <= NI:
                    m = j - 1
                    L = (ITEMS[m][2] + 1) * P
                    act.wait_ge(pc_turned, m + 1)
                    if m >= 2:
                        act.wait_ge(pv_done, m - 1)
                    act.activation(pcT[0:NCMP, m % 2, :], ps[3][0:NCMP, 0:P], ACT.Copy).then_inc(pc_copied, 1)
                    act.wait_ge(ps_turned, m + 1)
                    act.activation(pT[:, m % 2, 0, 0:L], ps[6][:, 0:L], ACT.Copy).then_inc(ps_copied, 1)
                if j >= 2 and (j - 1) % (2 * QT) == 0:
                    i = (j - 1) // (2 * QT) - 1
                    act.wait_ge(pv_done, 2 * QT * (i + 1))
                    act.activation(qT[:, i, :], ps[2][:, :], ACT.Copy).then_inc(o_copied, 1)
                    act.wait_ge(o_copied, i + 1)
            evac(S_ATTN - 1, mg[:, 2 * KD - 1, :])

            for i in range(PAIRS):
                act.activation(att_hi[:, i, :], qT[:, i, :], ACT.Copy).then_inc(att_hi_done, 1)
            for c in range(2):
                x = mg[:, c * 4:(c + 1) * 4, :]
                act.wait_ge(freed["act"], FREED[S_MERGE + 4 * c + 3][1])
                act.activation(x, x, ACT.Sigmoid).then_inc(gate_sig, 1)
            for c in range(CC):
                act.wait_ge(ln_centred, c + 1)
                if c >= 2:
                    act.wait_ge(ln_sqsum, c - 1)
                act.activation(sq[:, c % 2, :], acc[:, c, :], ACT.Square).then_inc(ln_sq, 1)
            hi(S_ATTN + 4)
            for c in range(2, 4):
                x = mg[:, c * 4:(c + 1) * 4, :]
                act.wait_ge(freed["act"], FREED[S_MERGE + 4 * c + 3][1])
                act.activation(x, x, ACT.Sigmoid).then_inc(gate_sig, 1)
            hi(S_ATTN + 5)
            act.wait_ge(ln_sqsum, CC)
            act.activation(rstd[:, :], ps[5][:, :], ACT.Sqrt, scale=1.0 / CONV_CH, bias=eps_t[:, 0:1]).then_inc(ln_root, 1)
            hi(S_ATTN + 6)
            for c in range(CC):
                act.wait_ge(ln_norm, c + 1)
                act.activation(acc[:, c, :], acc[:, c, :], ACT.Silu, scale=col("conv_ln_g", c),
                               bias=col("conv_ln_b", c)).then_inc(cv_ready, 1)
                act.wait_ge(cv_ready, c + 1)
                act.activation(cv_hi[:, c, :], acc[:, c, :], ACT.Copy).then_inc(cv_hi_done, 1)
            hi(S_ATTN + 7)
            for s in range(S_ATTN + 4, S_CONV):
                hi(s + 4)
            for s in range(S_CONV, S_OUT):
                hi(s + 4)
                m = s - S_CONV
                act.wait_ge(merged, m + 1)
                act.activation(h_hi[:, m, :], mg[:, m, :], ACT.Copy).then_inc(m_hi, 1)

            for k in range(KD):
                hi(S_OUT + k + 4)
                square(1, k)
            root(1)
            norm_hi(1)

            def ffn_act(s0, second):
                wname, bname = ("conv_w_2", "conv_b_2") if second else ("ffn_dw_w", "ffn_dw_b")
                wide = FT if second else 2 * FT
                done0 = FREED[s0][1]
                with act.Fori(0, FT // 2) as i:
                    for j in range(4):
                        half, t = j // 2, j % 2
                        s = s0 + 4 + j
                        u = s // 2
                        act.wait_ge(raw_in[u % 2], i * 16 + RAW_COUNT[u])
                        act.wait_ge(tile_done, i * 4 + (s - 3))
                        part = raw[u % 2][:, :].rearrange("p (k n) -> p k n", k=KD)
                        act.activation(w_hi[s % 4][:, :, :], part[:, :, s % 2 * P:(s % 2 + 1) * P],
                                       ACT.Copy).then_inc(hi_done, 1)
                        if half == 0 or not second:
                            act.wait_ge(g_lo_done, i * 2 + (second * (FT + 2) + t + 1))
                            act.wait_ge(tile_done, i * 4 + (s0 + j + 1))
                            m = i * 2 + (half * FT + t)
                            act.activation((ua, uv)[half][:, t, :], ps[BANK[s0 + j]][:, :], ACT.Identity,
                                           scale=col(wname, m + 2 * wide), bias=col(bname, m)).then_inc(biased, 1)
                        if half == 1:
                            act.wait_ge(freed["dve"], i * 4 + (done0 + t))
                            act.activation(ua[:, t, :], ua[:, t, :], ACT.Silu).then_inc(silu_done, 1)
                    for t in range(2):
                        act.wait_ge(prod_done, i * 2 + (second * FT + t + 1))
                        act.activation(g_hi[:, bass.ds(i * 2 + t, 1), :].rearrange("p a n -> p (a n)"),
                                       uv[:, t, :], ACT.Copy).then_inc(g_hi_done, 1)

            def act_down(s0, norm):
                for n in range(25):
                    if n >= 5 and n % 6 in (5, 0):
                        k = (n - 5) // 6 * 2 + (n % 6 == 0)
                        square(norm, k)
                        if norm == 2:
                            act.wait_ge(g_lo_done, FT + 2)
                            if k >= 2:
                                act.wait_ge(summed2, k - 1)
                            act.activation(hn[:, k % 2, :], xT[:, k, :], ACT.Square,
                                           scale=col("final_g", k)).then_inc(squared2, 1)
                    if n < 24:
                        hi(s0 + n + 4)

            ffn_act(S_UP, 0)
            act_down(S_DOWN, 2)

            act.wait_ge(mean_ready, 2)
            act.activation(rstd[:, :], rstd[:, :], ACT.Sqrt).then_inc(rooted, 1)
            act.activation(sq[:, 1, :], ps[7][:, :], ACT.Sqrt, scale=1.0 / D, bias=eps_t[:, 0:1]).then_inc(rooted, 1)
            norm_hi(3, lambda k: mod[:, k:k + 1])

            def stage_values(n, s, bias, c):
                act.wait_ge(x2_ready, KD)
                if n >= 2:
                    act.wait_ge(values_turned, n - 1)
                evac(s, sq[:, n % 2, :], ACT.Identity, bias=col(bias, c))

            for s in range(S_FH, S_GH):
                hi(s + 4)
                if s < S_QH:
                    evac(s, hf[:, s - S_FH, :], ACT.Sigmoid, bias=col("bfh", s - S_FH))
                elif s < S_IH:
                    evac(s, hq[:, s - S_QH, :], ACT.Silu, bias=col("bqh", s - S_QH))
                elif s < S_Q2:
                    stage_values(s - S_IH, s, "bih", s - S_IH)
                elif s < S_KV2:
                    evac(s, q2T[:, s - S_Q2, :], ACT.Identity, scale=-SCALE, bias=nq_bias[:, s - S_Q2:s - S_Q2 + 1])
                elif s == S_KV2:
                    evac(s, k2T[:, :], ACT.Identity, bias=col("bk"))
                else:
                    stage_values(HG, s, "bv", 0)
            for j in range(NI + 2):
                if j < NI:
                    i, g, t = ITEMS[j]
                    L = P if t == 0 else 2 * P
                    r = j % 2
                    act.wait_ge(s2_ready, j + 1)
                    act.activation(sc2[:, r, 0:L], sc2[:, r, 0:L], ACT.Exp, scale=-1.0, bias=stat[:, 18 + r:19 + r],
                                   accum_out=stat[:, 20 + r:21 + r]).then_inc(e2_done, 1)
                    h = i + 4 * g
                    act.activation(stat[:, 22 + r:23 + r], stat[:, 18 + r:19 + r], ACT.Exp,
                                   bias=sinks[:, 0, h:h + 1]).then_inc(e2_done, 1)
                if 1 <= j <= NI:
                    m = j - 1
                    L = P if ITEMS[m][2] == 0 else 2 * P
                    act.wait_ge(t2_done, m + 1)
                    if m >= 2:
                        act.wait_ge(pv2_done, m - 1)
                    act.activation(pT2[:, m % 2, 0:L], ps[6][:, 0:L], ACT.Copy).then_inc(t2_copied, 1)
                c = off_chunk_at(j - 1)
                if c is not None:
                    heads, _ = CHUNKS[c][1:]
                    act.wait_ge(chunk_done, c + 1)
                    bank = ps[CHUNK_BANK[c % 2]]
                    if CHUNKS[c][0] == 128:
                        dst = off[:, heads[0]:heads[0] + 2, 0:256]
                        src = bank[:, :].rearrange("p (h n) -> p h n", h=2)
                    else:
                        dst, src = off[:, heads[0], 256:768], bank[:, :]
                    act.activation(dst, src, ACT.Copy).then_inc(off_copied, 1)
                hd = av_at(j - 1)
                if hd is not None:
                    act.wait_ge(av_done, hd + 1)
                    act.activation(hq[:, hd, :], ps[CHUNK_BANK[hd % 2]][:, :], ACT.Copy).then_inc(av_copied, 1)
                    act.wait_ge(av_copied, hd + 1)
                    act.wait_ge(values_turned, HG + 1)
                    if hd >= 2:
                        act.wait_ge(r_sum, hd - 1)
                    act.activation(sq[:, hd % 2, :], hq[:, hd, :], ACT.Square).then_inc(r_sq, 1)
                n = gh_at(j)
                if n is not None:
                    hi(S_GH + n + 4)
                n = gh_at(j - 1)
                if n is not None:
                    act.wait_ge(q_scaled, len(ALL))
                    evac(S_GH + n, hgo[:, n, :], ACT.Identity, bias=col("bgh", n))
                if j >= 2 and (j - 1) % (2 * QT) == 0:
                    i = (j - 1) // (2 * QT) - 1
                    act.wait_ge(pv2_done, 2 * QT * (i + 1))
                    act.activation(q2T[:, i, :], ps[2][:, :], ACT.Copy).then_inc(o2_copied, 1)
            act.wait_ge(r_sum, HG)
            for i in range(PAIRS):
                act.wait_ge(o2_copied, i + 1)
                if i >= 2:
                    act.wait_ge(n2_sum, i - 1)
                act.activation(sq[:, i % 2, :], q2T[:, i, :], ACT.Square).then_inc(n2_sq, 1)
            act.wait_ge(r_inv, HG)
            act.activation(kd[:, :, :], kd[:, :, :], ACT.Sqrt).then_inc(r_root, 1)
            act.wait_ge(n2_sum, PAIRS)
            act.activation(rstd[:, :], ps[7][:, :], ACT.Sqrt, scale=1.0 / CONV_CH, bias=eps_t[:, 0:1]).then_inc(n2_root, 1)
            act.wait_ge(freed["act"], FREED[S_GH + 3][1])
            act.activation(hgo[:, :, :], hgo[:, :, :], ACT.Silu).then_inc(gate2_silu, 1)
            for hd in range(HG):
                act.wait_ge(r_norm, hd + 1)
                act.activation(h_hi[:, PAIRS + hd, :], hq[:, hd, :], ACT.Copy).then_inc(r_hi, 1)
            for i in range(PAIRS):
                act.wait_ge(n2_norm, i + 1)
                act.activation(h_hi[:, i, :], q2T[:, i, :], ACT.Copy).then_inc(n2_hi, 1)
            for k in range(KD):
                hi(S_OUT2 + k + 4)
                square(4, k)
            root(4)
            norm_hi(4, lambda k: mod[:, 3 * KD + k:3 * KD + k + 1])
            ffn_act(S_UP2, 1)
            act_down(S_DOWN2, 5)
            root(5)
            for t in range(QT):
                act.wait_ge(y_turned, t + 1)
                act.activation(y_out[:, t, 0:512], ps[t][:, :], ACT.Copy).then_inc(y_copied[0], 1)

        @block.vector
        def _(dve):
            chain = [0]

            def link(ins):
                chain[0] += 1
                ins.then_inc(dve_chain, 1)
                dve.wait_ge(dve_chain, chain[0])

            def norm(n, gain, shift=None):
                dve.wait_ge(rooted, ROOT[n])
                dve.reciprocal(rstd[:, :], rstd[:, :]).then_inc(inverted, 1)
                dve.wait_ge(inverted, ROOT[n])
                if n == 5:
                    for k in range(KD):
                        dve.scalar_tensor_tensor(out=xT[:, k, :], in0=xT[:, k, :], scalar=gain(k), in1=rstd[:, :],
                                                 op0=ALU.mult, op1=ALU.mult).then_inc(y_ready, 1)
                    return
                b = HN_BASE[n]
                for k in range(KD + 1):
                    if k < KD:
                        if k >= 2:
                            lo_ready(dve, n, k - 2)
                        dve.scalar_tensor_tensor(out=hn[:, k % 2, :], in0=xT[:, k, :], scalar=gain(k), in1=rstd[:, :],
                                                 op0=ALU.mult, op1=ALU.mult).then_inc(normed, 1)
                    m = k - 1
                    if m >= 0 and m % 2 == 0:
                        dve.wait_ge(n_hi, b + m + 1)
                        if shift is None:
                            ins = dve.tensor_tensor(h_lo[:, m, :], hn[:, m % 2, :], h_hi[:, m, :].bitcast(F32),
                                                    ALU.subtract)
                        else:
                            ins = dve.scalar_tensor_tensor(out=h_lo[:, m, :], in0=hn[:, m % 2, :], scalar=shift(m),
                                                           in1=h_hi[:, m, :].bitcast(F32), op0=ALU.add,
                                                           op1=ALU.subtract)
                        ins.then_inc(n_lo[0], 1)

            for k in range(KD):
                dve.wait_ge(x_turned, k + 1)
                dve.tensor_copy(xT[:, k, :], ps[k % 4][:, :]).then_inc(x_copied, 1)
            dve.wait_ge(small_turned, 1)
            n = min(512, NSM * P)
            dve.tensor_copy(sm[:, 0:n], ps[4][:, 0:n])
            link(dve.tensor_copy(sm[:, n:NSM * P], ps[5][:, 0:NSM * P - n]))
            dve.sem_inc(small_ready, 1)
            norm(0, lambda k: col("norm1_g", k))

            l0, l1 = col("hgrn_lb_logits_2", 0, HG), col("hgrn_lb_logits_2", HG, HG)
            link(dve.tensor_tensor(lower[:, 2, :], l0, l1, ALU.max))
            dve.tensor_tensor(lower[:, 0, :], l0, lower[:, 2, :], ALU.subtract)
            dve.tensor_tensor(lower[:, 1, :], l1, lower[:, 2, :], ALU.subtract).then_inc(lb_max, 1)
            dve.wait_ge(misc_loaded, 48)
            dve.tensor_scalar(sinks[:, 1, :], sinks[:, 0, :], -1.0, None, ALU.mult).then_inc(cond_ready, 1)
            dve.wait_ge(lb_exp, 1)
            link(dve.tensor_tensor(lower[:, 2, :], lower[:, 0, :], lower[:, 1, :], ALU.add))
            link(dve.reciprocal(lower[:, 2, :], lower[:, 2, :]))
            link(dve.tensor_tensor(lower[:, 2, :], lower[:, 0, :], lower[:, 2, :], ALU.mult))
            dve.tensor_scalar(lower[:, 3, :], lower[:, 2, :], -1.0, 1.0, ALU.mult, ALU.add).then_inc(lb_ready, 1)

            dve.wait_ge(wg_split_hi, 1)
            dve.tensor_tensor(wg_lo[:, :, :], wg[:, :, :], wg_hi[:, :, :].bitcast(F32), ALU.subtract).then_inc(wg_split, 1)
            for n in range(2):
                dve.wait_ge(tile_done, n + 1)
                src = ps[BANK[n]]
                pe_v = col(("pe_k", "pe_v")[n], 0, CMP_BLOCK)
                for half in range(2):
                    b = blk[:, n, half * 16:(half + 1) * 16, :]
                    tok = src[:, half * 16:half * 16 + NCMP * CMP_STRIDE].rearrange("p (m i) -> p i m", i=CMP_STRIDE)
                    ins = dve.tensor_tensor(b, tok, pe_v[:, half * 16:(half + 1) * 16].unsqueeze(2)
                                            .to_broadcast([P, 16, NCMP]), ALU.add)
                ins.then_inc(freed["dve"], 1)
            dve.wait_ge(hid_done, 1)
            H = lambda n: hc[:, n, :, :, 0:NCMP]
            for g in range(2):
                dve.tensor_copy(hn[0:NCMP, 1, g * 256:(g + 1) * 256], ps[3 + g][0:NCMP, 0:256]).then_inc(hid_rows, 1)
            dve.wait_ge(sig_turned, 1)
            dve.tensor_copy(gates[:, :, :].rearrange("p t n -> p (t n)"), ps[2][:, 0:QT * 24]).then_inc(sig_ready, 1)
            dve.wait_ge(hid_turned, 1)
            link(dve.tensor_copy(H(0), ps[4][:, 0:128].rearrange("p (g n m) -> p n g m", n=2, g=2)[:, :, :, 0:NCMP]))
            link(dve.tensor_tensor(H(1), H(0), H(0), ALU.mult))
            link(dve.tensor_scalar(H(1), H(1), 0.044715 * GELU_C, GELU_C, ALU.mult, ALU.add))
            dve.tensor_tensor(H(1), H(1), H(0), ALU.mult).then_inc(gelu_parts, 1)

            def glu(n):
                s = S_U + n // 2 * 4 + n % 2
                dve.wait_ge(freed["act"], FREED[s + 2][1])
                dve.tensor_tensor(z[:, n, PAD:PAD + T], ps[BANK[s]][:, :], sgt[n % 2], ALU.mult).then_inc(freed["dve"], 1)

            dve.wait_ge(gelu_done, 1)
            link(dve.scalar_tensor_tensor(out=H(2), in0=H(1), scalar=1.0, in1=H(0), op0=ALU.add, op1=ALU.mult))
            dve.tensor_scalar(H(2), H(2), 0.5, None, ALU.mult).then_inc(hid_copied, 1)
            dve.wait_ge(cmp_kv_done, 1)
            dve.tensor_copy(kcT[:, 0:NCMP], ps[5][:, 0:NCMP])
            dve.tensor_copy(vcN[0:NCMP, :], ps[5][0:NCMP, 64:64 + P]).then_inc(cmp_kv_copied, 1)
            glu(0)
            glu(1)
            for g in range(2):
                x = cp[:, g * 16:(g + 1) * 16, 0:NCMP]
                dve.wait_ge(cqk_done, g + 1)
                dve.wait_ge(cbias_ready, HEADS)
                link(dve.tensor_tensor(x, ps[4 + g][:, :].rearrange("p (n m) -> p n m", m=32)[:, :, 0:NCMP],
                                       cbias[:, g * 16:(g + 1) * 16, 0:NCMP], ALU.add))
                low = stat[:, 32:48]
                link(dve.tensor_reduce(low, x, AX.X, ALU.min))
                dve.tensor_tensor(x, x, low.unsqueeze(2).to_broadcast([P, 16, NCMP]), ALU.subtract).then_inc(cx_ready, 1)
                dve.wait_ge(cexp_done, g + 1)
                link(dve.tensor_reduce(low, x, AX.X, ALU.add))
                link(dve.reciprocal(low, low))
                dve.wait_ge(sig_ready, 1)
                r = stat[:, 48:64]
                gc = gates[:, :, 12 * g:12 * g + 12].rearrange("p t (i c) -> p t i c", c=3)[:, :, :, 0]
                link(dve.tensor_tensor(r.rearrange("p (t i) -> p t i", t=QT), low.rearrange("p (t i) -> p t i", t=QT),
                                       gc, ALU.mult))
                link(dve.tensor_tensor(x, x, r.unsqueeze(2).to_broadcast([P, 16, NCMP]), ALU.mult))
                for t in range(QT):
                    xt = cp[:, g * 16 + t * 4:g * 16 + t * 4 + 4, 0:NCMP]
                    v = cvalid[:, t, 0:NCMP].unsqueeze(1).to_broadcast([P, 4, NCMP])
                    ins = dve.tensor_tensor(xt, xt, v, ALU.mult)
                ins.then_inc(cp_ready, 1)
            glu(2)
            glu(3)
            dve.wait_ge(freed["dve"], FREED[S_U + 5][1])

            def tap(n):
                c, m = n % CC, n // CC
                src = z[:, c, m:m + T]
                w = col("conv_dw_w", 4 * m + c)
                if m == 0:
                    ins = dve.tensor_scalar(acc[:, c, :], src, w, col("conv_dw_b", c), ALU.mult, ALU.add)
                else:
                    dve.wait_ge(tap_done, n - CC + 1)
                    ins = dve.scalar_tensor_tensor(out=acc[:, c, :], in0=src, scalar=w, in1=acc[:, c, :],
                                                   op0=ALU.mult, op1=ALU.add)
                ins.then_inc(tap_done, 1)

            for j in range(NI + 1):
                if j < NI:
                    i, g, t = ITEMS[j]
                    L = (t + 1) * P
                    hn_ = j // QT
                    for b in range(2):
                        if b == 0 and t == 0:
                            dve.wait_ge(hbias_ready, hn_ + 1)
                        dve.wait_ge(qk_done, 2 * j + b + 1)
                        if j >= 2:
                            dve.wait_ge((ps_turned, pw_turned)[b], j - 1)
                        q = 2 * (j % 2) + b
                        dve.tensor_tensor_reduce(out=sc[:, j % 2, b, 0:L], in0=ps[4 + b][:, 0:L],
                                                 in1=hbias[hn_ % 2][:, (QT - 1 - t) * P:T], scale=1.0, scalar=3.0e38,
                                                 op0=ALU.add, op1=ALU.min, accum_out=stat[:, q:q + 1])\
                           .then_inc(scores_ready, 1)
                for n in range(4 * j, min(4 * j + 2, CC * CONV_W)):
                    tap(n)
                if j >= 1:
                    m = j - 1
                    L2 = (ITEMS[m][2] + 1) * P
                    dve.wait_ge(pw_turned, m + 1)
                    if m >= 2:
                        dve.wait_ge(pv_done, m - 1)
                    dve.tensor_copy(pT[:, m % 2, 1, 0:L2], ps[7][:, 0:L2]).then_inc(pw_copied, 1)
                for n in range(4 * j + 2, min(4 * j + 4, CC * CONV_W)):
                    tap(n)
                if j < NI:
                    q = 2 * (j % 2)
                    dve.wait_ge(exp_done, 2 * j + 2)
                    link(dve.reciprocal(stat[:, 8 + q:10 + q], stat[:, 4 + q:6 + q]))
                    h = i + 4 * g
                    link(dve.tensor_tensor(stat[:, 8 + q:10 + q], stat[:, 8 + q:10 + q],
                                           gates[:, t, 3 * h + 1:3 * h + 3], ALU.mult))
                    for b in range(2):
                        x = sc[:, j % 2, b, 0:L]
                        ins = dve.tensor_scalar(x, x, stat[:, 8 + q + b:9 + q + b], None, ALU.mult)
                    ins.then_inc(p_ready, 1)

            for i in range(PAIRS):
                dve.wait_ge(att_hi_done, i + 1)
                dve.tensor_tensor(att_lo[:, i, :], qT[:, i, :], att_hi[:, i, :].bitcast(F32),
                                  ALU.subtract).then_inc(att_lo_done, 1)
            dve.wait_ge(ln_sum, 1)
            for c in range(CC):
                dve.scalar_tensor_tensor(out=acc[:, c, :], in0=ps[4][:, :], scalar=-1.0 / CONV_CH, in1=acc[:, c, :],
                                         op0=ALU.mult, op1=ALU.add).then_inc(ln_centred, 1)

            def gated_attention(m):
                s = S_ATTN + m
                dve.wait_ge(gate_sig, m // 4 + 1)
                dve.wait_ge(tile_done, s + 1)
                dve.tensor_tensor(mg[:, m, :], ps[BANK[s]][:, :], mg[:, m, :], ALU.mult).then_inc(freed["dve"], 1)

            gated_attention(0)
            gated_attention(1)
            dve.wait_ge(ln_root, 1)
            link(dve.reciprocal(rstd[:, :], rstd[:, :]))
            for c in range(CC):
                dve.tensor_tensor(acc[:, c, :], acc[:, c, :], rstd[:, :], ALU.mult).then_inc(ln_norm, 1)
            for c in range(CC):
                dve.wait_ge(cv_hi_done, c + 1)
                dve.tensor_tensor(cv_lo[:, c, :], acc[:, c, :], cv_hi[:, c, :].bitcast(F32),
                                  ALU.subtract).then_inc(cv_lo_done, 1)
            for m in range(2, KD):
                gated_attention(m)
            for m in range(KD + 1):
                if m < KD:
                    s = S_CONV + m
                    dve.wait_ge(gate_sig, 3 + m // 4)
                    dve.wait_ge(tile_done, s + 1)
                    dve.tensor_tensor(mg[:, KD + m, :], ps[BANK[s]][:, :], mg[:, KD + m, :], ALU.mult)\
                       .then_inc(freed["dve"], 1)
                    dve.wait_ge(freed["dve"], FREED[s][1])
                    dve.tensor_tensor(mg[:, m, :], mg[:, m, :], mg[:, KD + m, :], ALU.add).then_inc(merged, 1)
                if m:
                    dve.wait_ge(m_hi, m)
                    dve.tensor_tensor(h_lo[:, m - 1, :], mg[:, m - 1, :], h_hi[:, m - 1, :].bitcast(F32),
                                      ALU.subtract).then_inc(m_lo, 1)

            def ada_reduce(n, loaded, i=None):
                buf = n % 2
                count = lambda v: v if i is None else i * 2 + v
                dve.wait_ge(ada_in[buf], loaded)
                dve.tensor_tensor(ada[buf][:, :, :], ada[buf][:, :, :],
                                  cond[:, :].unsqueeze(2).to_broadcast([P, KD, P]), ALU.mult).then_inc(ada_scaled, 1)
                dve.wait_ge(ada_scaled, count(n + 1))
                if n >= 2:
                    dve.wait_ge(ada_done, count(n - 1))
                dve.tensor_reduce(ada_sum[buf][:, :], ada[buf][:, :, :].rearrange("p k n -> p n k"), AX.X,
                                  ALU.add).then_inc(ada_summed, 1)

            dve.wait_ge(cond_ready, 1)
            for k in range(KD):
                s = S_OUT + k
                dve.wait_ge(tile_done, s + 1)
                dve.tensor_tensor(xT[:, k, :], ps[BANK[s]][:, :], xT[:, k, :], ALU.add).then_inc(freed["dve"], 1)
                if k < ADA_EARLY:
                    ada_reduce(k, 16 * (k // 2 + 1))
            norm(1, lambda k: col("norm2_g", k))

            def ffn_dve(s0, second):
                wname = "conv_w_2" if second else "ffn_dw_w"
                wide = FT if second else 2 * FT
                per = 2 if second else 4
                dve.sem_inc(g_lo_done, 2)
                with dve.Fori(0, FT // 2) as i:
                    for j in range(4):
                        half, t = j // 2, j % 2
                        src = ps[BANK[s0 + j]]
                        if half and second:
                            dve.wait_ge(silu_done, i * 2 + (FT + t + 1))
                            dve.wait_ge(tile_done, i * 4 + (s0 + j + 1))
                            dve.tensor_tensor(uv[:, t, :], src[:, :], ua[:, t, :], ALU.mult).then_inc(freed["dve"], 1)
                            continue
                        u = (ua, uv)[half]
                        n = i * per + (second * 2 * FT + j + 1)
                        m = i * 2 + (half * FT + t)
                        dve.wait_ge(biased, n)
                        dve.scalar_tensor_tensor(out=u[:, t, 1:T], in0=src[:, 0:T - 1], scalar=col(wname, m + wide),
                                                 in1=u[:, t, 1:T], op0=ALU.mult, op1=ALU.add).then_inc(tap1_done, 1)
                        dve.wait_ge(tap1_done, n)
                        dve.scalar_tensor_tensor(out=u[:, t, 2:T], in0=src[:, 0:T - 2], scalar=col(wname, m),
                                                 in1=u[:, t, 2:T], op0=ALU.mult, op1=ALU.add).then_inc(freed["dve"], 1)
                        if j == 1 and not second:
                            ada_reduce(ADA_EARLY, i * 16 + 16 * (ADA_EARLY // 2 + 1), i)
                    for t in range(2):
                        if second:
                            dve.wait_ge(freed["dve"], i * 4 + (FREED[s0][1] + 2 + t))
                            dve.sem_inc(prod_done, 1)
                        else:
                            dve.wait_ge(silu_done, i * 2 + (t + 1))
                            dve.wait_ge(freed["dve"], i * 4 + (FREED[s0][1] + 2 + t))
                            dve.tensor_tensor(uv[:, t, :], uv[:, t, :], ua[:, t, :], ALU.mult).then_inc(prod_done, 1)
                    for t in range(2):
                        k = i * 2 + t
                        dve.wait_ge(g_hi_done, i * 2 + (second * FT + t + 1))
                        dve.tensor_tensor(g_lo[:, bass.ds(k, 1), :].rearrange("p a n -> p (a n)"), uv[:, t, :],
                                          g_hi[:, bass.ds(k, 1), :].rearrange("p a n -> p (a n)").bitcast(F32),
                                          ALU.subtract).then_inc(g_lo_done, 1)
                    if not second:
                        ada_reduce(ADA_EARLY + 1, i * 16 + 16 * (ADA_EARLY // 2 + 1), i)

            ffn_dve(S_UP, 0)
            for n in range(24):
                if n % 6 >= 4:
                    k = n // 6 * 2 + n % 2
                    dve.wait_ge(tile_done, S_DOWN + n + 1)
                    dve.tensor_tensor(xT[:, k, :], ps[BANK[S_DOWN + n]][:, :], xT[:, k, :],
                                      ALU.add).then_inc(freed["dve"], 1)
                m = ADA_EARLY + ADA_UP + n
                if m < NMOD * KD:
                    ada_reduce(m, 16 * (m // 2 + 1))
            dve.wait_ge(ada_done, NMOD * KD)
            link(dve.tensor_tensor(mod[:, :], ps[6][:, 0:NMOD * KD], col("ada_b_2", 0, NMOD * KD), ALU.add))
            for n, (name, c) in enumerate((("mix_norm_g_2", KD), ("ffn_norm_g_2", 4 * KD))):
                link(dve.tensor_scalar(gain2[:, n, :], mod[:, c:c + KD], 1.0, None, ALU.add))
                link(dve.tensor_tensor(gain2[:, n, :], gain2[:, n, :], col(name, 0, KD), ALU.mult))
            link(dve.tensor_tensor(gain2[:, 0, :], gain2[:, 0, :], col("final_g", 0, KD), ALU.mult))
            dve.wait_ge(summed, SQ_BASE[2] + KD)
            dve.wait_ge(summed2, KD)
            dve.tensor_scalar(sq[:, 0, :], ps[7][:, :], EPS / D, EPS * EPS, ALU.mult, ALU.add).then_inc(mean_ready, 1)
            dve.wait_ge(mean_ready, 1)
            dve.scalar_tensor_tensor(out=rstd[:, :], in0=ps[5][:, :], scalar=1.0 / D, in1=sq[:, 0, :],
                                     op0=ALU.mult, op1=ALU.add).then_inc(mean_ready, 1)
            norm(3, lambda k: gain2[:, 0, k:k + 1], lambda k: mod[:, k:k + 1])
            dve.wait_ge(rooted, ROOT[2])
            dve.reciprocal(sq[:, 1, :], sq[:, 1, :]).then_inc(inverted, 1)
            dve.wait_ge(inverted, ROOT[2])
            for k in range(KD):
                dve.scalar_tensor_tensor(out=xT[:, k, :], in0=xT[:, k, :], scalar=col("final_g", k), in1=sq[:, 1, :],
                                         op0=ALU.mult, op1=ALU.mult).then_inc(x2_ready, 1)

            for h in range(HG):
                dve.wait_ge(freed["act"], FREED[S_FH + h][1])
                dve.tensor_scalar(hf[:, h, :], hf[:, h, :], lower[:, 3, h:h + 1], lower[:, 2, h:h + 1],
                                  ALU.mult, ALU.add).then_inc(f_ready, 1)
                dve.wait_ge(f_ready, 2 * h + 1)
                dve.tensor_scalar(hk[:, h, :], hf[:, h, :], -1.0, 1.0, ALU.mult, ALU.add).then_inc(f_ready, 1)

            def take_values(n, dst):
                dve.wait_ge(values_turned, n + 1)
                dve.tensor_copy(dst, ps[V_BANK[n]][:, :].rearrange("p (t n) -> p t n", t=QT)).then_inc(values_copied, 1)

            for h in range(HG - 1):
                take_values(h, iN[:, :, h * P:(h + 1) * P])
            dve.wait_ge(freed["act"], FREED[S_QH + 3][1])

            def scale_queries(n):
                b = ALL[n]
                if n:
                    dve.wait_ge(lvl_done, n)
                dst = qd[:, :, :].rearrange("p h t -> p (h t)").rearrange("p (m c) -> p m c", c=b)
                dve.tensor_tensor(dst, pairs_of(hq, b)[:, :, 1, :], pairs_of(hf, b)[:, :, 1, :],
                                  ALU.mult).then_inc(q_scaled, 1)

            def merge_decays(n):
                b = ALL[n]
                dve.wait_ge(g_merged, n + 1)
                f = pairs_of(hf, b)
                dve.tensor_tensor(f[:, :, 1, :], f[:, :, 1, :],
                                  f[:, :, 0, b - 1:b].to_broadcast([P, HG * T // (2 * b), b]),
                                  ALU.mult).then_inc(f_merged, 1)
                dve.wait_ge(f_merged, n + 1)

            def take_scores(c):
                kind, heads, n = CHUNKS[c]
                if n is not None and kind > 64:
                    return
                dve.wait_ge(chunk_done, c + 1)
                if n is None:
                    in_tiles = lambda x: x.rearrange("p (t n) -> p t n", t=QT)
                    dve.copy_predicated(in_tiles(hs[:, heads[0], :]), eye8[:, :].unsqueeze(1).to_broadcast([P, QT, P]),
                                        in_tiles(ps[CHUNK_BANK[c % 2]][:, :])).then_inc(sel_done, 1)
                else:
                    half = HG * T // (2 * kind) // 2
                    m0 = half * (heads[0] // 2)
                    by_tile = lambda x: x.rearrange("p (r m) c -> p r m c", m=DH // kind)
                    sel = mask[:, n, :].rearrange("p (m c) -> p m c", c=kind).unsqueeze(1)
                    dve.copy_predicated(by_tile(pairs_of(hs, kind)[:, m0:m0 + half, 1, :]),
                                        sel.to_broadcast([P, T // DH, DH // kind, kind]),
                                        by_tile(ps[CHUNK_BANK[c % 2]][:, :].rearrange("p (m c) -> p m c", c=kind)))\
                       .then_inc(sel_done, 1)

            def hgrn_step(c):
                take_scores(c)
                nxt = CHUNKS[c + 1][2] if c + 1 < len(CHUNKS) else None
                if nxt is not None and nxt != CHUNKS[c][2]:
                    if nxt:
                        merge_decays(nxt - 1)
                    scale_queries(nxt)

            dve.wait_ge(setup2, 1)
            for s in range(S_Q2, S_GH):
                if s == S_Q2:
                    take_values(HG - 1, iN[:, :, (HG - 1) * P:HG * P])
                hgrn_step(s - S_Q2)
            take_values(HG, v2N[:, :, :])
            for j in range(NI + 1):
                if j < NI:
                    i, g, t = ITEMS[j]
                    h = i + 4 * g
                    L = P if t == 0 else 2 * P
                    r = j % 2
                    dve.wait_ge(qk2_done, j + 1)
                    if j >= 2:
                        dve.wait_ge(t2_done, j - 1)
                    if j == 0:
                        dve.wait_ge(cond_ready, 3)
                    link(dve.tensor_tensor_reduce(out=sc2[:, r, 0:L], in0=ps[4 + r][:, 0:L], in1=dist2[:, 2 * P - L:],
                                                  scale=1.0, scalar=3.0e38, op0=ALU.add, op1=ALU.min,
                                                  accum_out=stat[:, 16 + r:17 + r]))
                    dve.tensor_scalar(stat[:, 18 + r:19 + r], stat[:, 16 + r:17 + r], sinks[:, 1, h:h + 1], None,
                                      ALU.min).then_inc(s2_ready, 1)
                c = chunk_at(j)
                if c is not None:
                    hgrn_step(c)
                hd = av_at(j - 1)
                if hd is not None:
                    dve.wait_ge(r_sum, hd + 1)
                    dve.tensor_scalar(kd[:, hd, :], ps[R_BANK][:, :], 1.0 / P, EPS, ALU.mult,
                                      ALU.add).then_inc(r_var, 1)
                    dve.wait_ge(r_var, hd + 1)
                    dve.reciprocal(kd[:, hd, :], kd[:, hd, :]).then_inc(r_inv, 1)
                if j < NI:
                    dve.wait_ge(e2_done, 2 * j + 2)
                    link(dve.tensor_tensor(stat[:, 24 + r:25 + r], stat[:, 20 + r:21 + r], stat[:, 22 + r:23 + r], ALU.add))
                    link(dve.reciprocal(stat[:, 24 + r:25 + r], stat[:, 24 + r:25 + r]))
                    dve.tensor_scalar(sc2[:, r, 0:L], sc2[:, r, 0:L], stat[:, 24 + r:25 + r], None,
                                      ALU.mult).then_inc(p2_ready, 1)
            dve.wait_ge(r_root, 1)
            for hd in range(HG):
                dve.wait_ge(av_copied, hd + 1)
                link(dve.tensor_tensor(hq[:, hd, :], hq[:, hd, :], kd[:, hd, :], ALU.mult))
            dve.wait_ge(n2_root, 1)
            link(dve.reciprocal(rstd[:, :], rstd[:, :]))
            for i in range(PAIRS):
                dve.scalar_tensor_tensor(out=q2T[:, i, :], in0=q2T[:, i, :], scalar=col("attn_out_g_2", i),
                                         in1=rstd[:, :], op0=ALU.mult, op1=ALU.mult).then_inc(n2_norm, 1)
            dve.wait_ge(gate2_silu, 1)
            for hd in range(HG):
                dve.scalar_tensor_tensor(out=hq[:, hd, :], in0=hq[:, hd, :], scalar=col("hgrn_out_g_2", hd),
                                         in1=hgo[:, hd, :], op0=ALU.mult, op1=ALU.mult).then_inc(r_norm, 1)
            for i in range(PAIRS):
                dve.wait_ge(n2_hi, i + 1)
                dve.tensor_tensor(h_lo[:, i, :], q2T[:, i, :], h_hi[:, i, :].bitcast(F32), ALU.subtract).then_inc(n2_lo, 1)
            for hd in range(HG):
                dve.wait_ge(r_hi, hd + 1)
                dve.tensor_tensor(h_lo[:, PAIRS + hd, :], hq[:, hd, :], h_hi[:, PAIRS + hd, :].bitcast(F32),
                                  ALU.subtract).then_inc(r_lo, 1)

            def gated_residual(s, k, gate):
                dve.wait_ge(tile_done, s + 1)
                dve.scalar_tensor_tensor(out=xT[:, k, :], in0=ps[BANK[s]][:, :], scalar=mod[:, gate * KD + k:gate * KD + k + 1],
                                         in1=xT[:, k, :], op0=ALU.mult, op1=ALU.add).then_inc(freed["dve"], 1)

            dve.wait_ge(x2_ready, KD)
            for k in range(KD):
                gated_residual(S_OUT2 + k, k, 2)
            norm(4, lambda k: gain2[:, 1, k:k + 1], lambda k: mod[:, 3 * KD + k:3 * KD + k + 1])
            ffn_dve(S_UP2, 1)
            for k in range(KD):
                gated_residual(S_DOWN2 + k // 2 * 6 + 4 + k % 2, k, 5)
            norm(5, lambda k: col("final_norm_g_2", k))
            for t in range(QT):
                dve.wait_ge(y_turned, QT + t + 1)
                dve.tensor_copy(y_out[:, t, 512:D], ps[4 + t][:, :]).then_inc(y_copied[1], 1)

        @block.tensor
        def _(pe):
            def split_product(out_ap, w, wl, x, xl, first, last):
                pe.matmul(out_ap, w, x, start=first, stop=False)
                pe.matmul(out_ap, w, xl, start=False, stop=False)
                return pe.matmul(out_ap, wl, x, start=False, stop=last)

            def tile(s, x, xl, k0=0, first=True, last=True, part=(0, None), ready=None, signal=True):
                nk = DEPTH_OF[s]
                lo_k, hi_k = part[0], nk if part[1] is None else part[1]
                if lo_k == 0:
                    pe.wait_ge(lo_done, s + 1)
                    if first:
                        wait_bank(pe, s)
                for k in range(lo_k, hi_k):
                    if ready is not None:
                        ready(k0 + k)
                    ins = split_product(ps[BANK[s]][:, :], w_hi[s % 4][:, k, :], w_lo[s % 4][:, k, :],
                                        x[:, k0 + k, :], xl[:, k0 + k, :], first and k == 0, last and k == nk - 1)
                if hi_k == nk and signal:
                    ins.then_inc(tile_done, 1)

            def norm_sum(n, k):
                pe.wait_ge(squared, SQ_BASE[n] + k + 1)
                pe.matmul(ps[7][:, :], ones[:, :], sq[:, k % 2, :], start=k == 0, stop=k == KD - 1).then_inc(summed, 1)

                if n == 2:
                    pe.wait_ge(squared2, k + 1)
                    pe.matmul(ps[5][:, :], ones[:, :], hn[:, k % 2, :], start=k == 0, stop=k == KD - 1).then_inc(summed2, 1)

            def parts(sem, base=0):
                return lambda k: pe.wait_ge(sem, base + k + 1)

            def normed_parts(norm):
                return lambda k: lo_ready(pe, norm, k)

            pe.wait_ge(consts, 1)
            pe.wait_ge(x_loaded, 16 * QT)
            for k in range(KD):
                if k >= 4:
                    pe.wait_ge(x_copied, k - 3)
                for t in range(QT):
                    ins = pe.transpose(ps[k % 4][:, t * P:(t + 1) * P], x_in[:, t, k * P:(k + 1) * P], ident[:, :])
                ins.then_inc(x_turned, 1)
            for k in range(KD):
                norm_sum(0, k)
            pe.wait_ge(small_loaded, small_total[0])
            for m in range(NSM):
                ins = pe.transpose(ps[4 + m // 4][:, m % 4 * P:(m % 4 + 1) * P], rows[:, m, :], ident[:, :])
            ins.then_inc(small_turned, 1)
            pe.wait_ge(x_copied, KD)
            for s in range(S_CMP, S_V):
                tile(s, h_hi, h_lo, ready=normed_parts(0) if s == 0 else None)
            for s in range(S_V, S_U):
                tile(s, h_hi, h_lo)
            pe.wait_ge(wg_split, 1)
            for k in range(KD):
                ins = split_product(ps[2][0:24, :], wg_hi[:, k, :], wg_lo[:, k, :], h_hi[:, k, :], h_lo[:, k, :],
                                    k == 0, k == KD - 1)
            ins.then_inc(gate_done, 1)
            for n in range(2):
                pe.wait_ge(freed["act"], FREED[S_V + n][1])
                for t in range(QT):
                    ins = pe.transpose(ps[6 + n][:, t * P:(t + 1) * P], sq[:, n, t * P:(t + 1) * P], ident[:, :])
                ins.then_inc(v_turned, 1)
            pe.wait_ge(w1_loaded, 64)
            pe.wait_ge(freed["dve"], FREED[1][1])
            for g in range(2):
                for n in range(2):
                    for m in range(CMP_BLOCK):
                        ins = pe.matmul(ps[3 + g][0:NCMP, n * P:(n + 1) * P], blk[g * DH:(g + 1) * DH, n, m, :],
                                        w1[n][g * DH:(g + 1) * DH, m, :], start=m == 0, stop=m == CMP_BLOCK - 1)
            ins.then_inc(hid_done, 1)
            pe.wait_ge(gate_ready, 1)
            for t in range(QT):
                ins = pe.transpose(ps[2][:, t * 24:(t + 1) * 24], hn[0:24, 0, t * P:(t + 1) * P], ident[0:24, 0:24])
            ins.then_inc(sig_turned, 1)
            for s in range(S_U, S_MERGE):
                if s == S_U + 2:
                    pe.wait_ge(v_copied, 2)
                tile(s, h_hi, h_lo)
                if s == S_U:
                    pe.wait_ge(hid_rows, 2)
                    for m in range(4):
                        ins = pe.transpose(ps[4][:, m * 32:m * 32 + NCMP], hn[0:NCMP, 1, m * P:(m + 1) * P],
                                           ident[0:NCMP, 0:NCMP])
                    ins.then_inc(hid_turned, 1)
                if s == S_U + 1:
                    pe.wait_ge(hid_copied, 1)
                    pe.wait_ge(misc_loaded, 48)
                    for g in range(2):
                        pe.matmul(ps[5][g * DH:(g + 1) * DH, 0:NCMP], w2[:, 0, :], hc[:, 2, 0, g, 0:NCMP],
                                  start=True, stop=True)
                    for g in range(2):
                        ins = pe.matmul(ps[5][0:NCMP, 64 + g * DH:64 + (g + 1) * DH], hc[:, 2, 1, g, 0:NCMP],
                                        w2[:, 1, :], start=True, stop=True)
                    ins.then_inc(cmp_kv_done, 1)
                if s == S_U + 3:
                    pe.wait_ge(cmp_kv_copied, 1)
                    pe.wait_ge(freed["act"], FREED[S_U - 1][1])
                    for g in range(2):
                        for t in range(QT):
                            for i in range(PAIRS):
                                n = (t * PAIRS + i) * 32
                                ins = pe.matmul(ps[4 + g][:, n:n + NCMP], qT[g * DH:(g + 1) * DH, i, t * P:(t + 1) * P],
                                                kcT[g * DH:(g + 1) * DH, 0:NCMP], start=True, stop=True)
                        ins.then_inc(cqk_done, 1)
            pe.wait_ge(cx_ready, 2)
            pe.wait_ge(sig_ready, 1)
            pe.wait_ge(freed["act"], FREED[S_MERGE - 1][1])
            for j in range(NI + 2):
                if j < NI:
                    i, g, t = ITEMS[j]
                    L = (t + 1) * P
                    grp = slice(g * DH, (g + 1) * DH)
                    for b in range(2):
                        if j:
                            pe.wait_ge(scores_ready, 2 * j + b - 1)
                        pe.matmul(ps[4 + b][:, 0:L], qT[grp, i, t * P:(t + 1) * P], kT[grp, b, 0:L],
                                  start=True, stop=True).then_inc(qk_done, 1)
                    tile(S_MERGE + j // 2, h_hi, h_lo, part=(4 * (j % 2), 4 * (j % 2) + 4))
                if 1 <= j <= NI:
                    m = j - 1
                    i, g, t = ITEMS[m]
                    pe.wait_ge(p_ready, m + 1)
                    pe.wait_ge(cp_ready, 2)
                    if m:
                        pe.wait_ge(pc_copied, m)
                    pe.transpose(ps[3][0:NCMP, 0:P], cp[:, g * 16 + t * 4 + i, 0:NCMP], ident[:, :]).then_inc(pc_turned, 1)
                    for b in range(2):
                        if m:
                            pe.wait_ge((ps_copied, pw_copied)[b], m)
                        for kt in range(t + 1):
                            ins = pe.transpose(ps[6 + b][:, kt * P:(kt + 1) * P], sc[:, m % 2, b, kt * P:(kt + 1) * P],
                                               ident[:, :])
                        ins.then_inc((ps_turned, pw_turned)[b], 1)
                if j >= 2:
                    m = j - 2
                    i, g, t = ITEMS[m]
                    pe.wait_ge(pc_copied, m + 1)
                    pe.wait_ge(ps_copied, m + 1)
                    pe.wait_ge(pw_copied, m + 1)
                    if m and m % (2 * QT) == 0:
                        pe.wait_ge(o_copied, m // (2 * QT))
                    o = ps[2][g * DH:(g + 1) * DH, t * P:(t + 1) * P]
                    for b in range(2):
                        for kt in range(t + 1):
                            pe.matmul(o, vN[:, b, kt, g * DH:(g + 1) * DH], pT[:, m % 2, b, kt * P:(kt + 1) * P],
                                      start=b == 0 and kt == 0, stop=False)
                    pe.matmul(o, vcN[0:NCMP, g * DH:(g + 1) * DH], pcT[0:NCMP, m % 2, :],
                              start=False, stop=True).then_inc(pv_done, 1)
            pe.wait_ge(tap_done, CC * CONV_W)
            for c in range(CC):
                ins = pe.matmul(ps[4][:, :], ones[:, :], acc[:, c, :], start=c == 0, stop=c == CC - 1)
            ins.then_inc(ln_sum, 1)
            tile(S_ATTN, att_hi, att_lo, ready=parts(att_lo_done))
            for c in range(CC):
                pe.wait_ge(ln_sq, c + 1)
                pe.matmul(ps[5][:, :], ones[:, :], sq[:, c % 2, :], start=c == 0, stop=c == CC - 1).then_inc(ln_sqsum, 1)
            for s in range(S_ATTN + 1, S_CONV):
                tile(s, att_hi, att_lo)
            for s in range(S_CONV, S_OUT):
                tile(s, cv_hi, cv_lo, ready=parts(cv_lo_done) if s == S_CONV else None)

            def ada_tile(n, buf, count):
                pe.wait_ge(ada_summed, count)
                pe.matmul(ps[6][:, bass.ds(n, 1)] if not isinstance(n, int) else ps[6][:, n:n + 1],
                          ada_sum[buf][:, :], ones[:, 0:1], start=True, stop=True).then_inc(ada_done, 1)

            for s in range(S_OUT, S_UP):
                tile(s, h_hi, h_lo, ready=parts(m_lo) if s == S_OUT else None)
                if s > S_OUT:
                    norm_sum(1, s - S_OUT - 1)
                n = s - S_OUT - 2
                if 0 <= n < ADA_EARLY - 1:
                    ada_tile(n, n % 2, n + 1)
            norm_sum(1, KD - 1)

            def ffn_pe(s0, norm):
                with pe.Fori(0, FT // 2) as i:
                    for j in range(4):
                        s = s0 + j
                        pe.wait_ge(lo_done, i * 4 + (s + 1))
                        pe.wait_ge(freed["dve"], i * 4 + (FREED[s][1] - 4))
                        for k in range(KD):
                            if j == 0:
                                lo_ready(pe, norm, k)
                            ins = split_product(ps[BANK[s]][:, :], w_hi[s % 4][:, k, :], w_lo[s % 4][:, k, :],
                                                h_hi[:, k, :], h_lo[:, k, :], k == 0, k == KD - 1)
                        ins.then_inc(tile_done, 1)
                        if norm == 1 and j % 2:
                            n = ADA_EARLY - 1 + j // 2
                            ada_tile(i * 2 + n, n % 2, i * 2 + (n + 1))

            ffn_pe(S_UP, 1)

            def down(s0, second):
                norm = 5 if second else 2
                for n in range(24):
                    k0, nk = PARTS[n // 2 % 3]
                    if n >= 6 and n % 6 in (0, 1):
                        norm_sum(norm, (n // 6 - 1) * 2 + n % 6)
                    s = s0 + n
                    tile(s, g_hi, g_lo, k0, first=n // 2 % 3 == 0, last=n // 2 % 3 == 2,
                         ready=parts(g_lo_done, second * (FT + 2) + 2) if n in (0, 2, 4) else None)
                    m = ADA_EARLY + ADA_UP - 2 + n
                    if not second and n and m < NMOD * KD:
                        ada_tile(m, m % 2, m + 1)
                for k in range(KD - 2, KD):
                    norm_sum(norm, k)

            down(S_DOWN, 0)
            for s in range(S_FH, S_IH):
                tile(s, h_hi, h_lo, ready=normed_parts(3) if s == S_FH else None)

            def turn_values(n):
                pe.wait_ge(freed["act"], FREED[S_IH + n if n < HG else S_KV2 + 1][1])
                if n >= 2:
                    pe.wait_ge(values_copied, n - 1)
                for t in range(QT):
                    ins = pe.transpose(ps[V_BANK[n]][:, t * P:(t + 1) * P], sq[:, n % 2, t * P:(t + 1) * P], ident[:, :])
                ins.then_inc(values_turned, 1)

            for n in range(HG):
                tile(S_IH + n, h_hi, h_lo)
                if n:
                    turn_values(n - 1)

            def chunk(c):
                kind, heads, n = CHUNKS[c]
                bank = ps[CHUNK_BANK[c % 2]]
                if c >= 2:
                    if c - 2 < N_SEL:
                        pe.wait_ge(sel_done, c - 1)
                    else:
                        pe.wait_ge(off_copied, c - 1 - N_SEL)
                if n is None:
                    pe.wait_ge(f_ready, 2 * HG)
                    pe.wait_ge(freed["act"], FREED[S_QH + 3][1])
                    for t in range(QT):
                        tk = slice(t * P, (t + 1) * P)
                        ins = pe.matmul(bank[:, tk], hk[:, heads[0], tk], hq[:, heads[0], tk], start=True, stop=True)
                    ins.then_inc(chunk_done, 1)
                    return
                pe.wait_ge(q_scaled, n + 1)
                if n:
                    pe.wait_ge(k_scaled, n)
                keys = kd if n else hk
                for hd in heads:
                    if kind == 256:
                        todo = [(m * 256, m, 0, 256) for m in range(2)]
                    elif kind == 128:
                        todo = [(hd % 2 * 256 + m * P, 2 * m, m * P, P) for m in range(2)]
                    else:
                        todo = [(hd % 2 * 256 + t * 64, t, t * 64, 64) for t in range(QT)]
                    for at, t, q0, nq in todo:
                        ins = pe.matmul(bank[:, at:at + nq], keys[:, hd, t * P:(t + 1) * P], qd[:, hd, q0:q0 + nq],
                                        start=True, stop=True)
                ins.then_inc(chunk_done, 1)
                if c + 1 == len(CHUNKS) or CHUNKS[c + 1][2] != n:
                    pe.wait_ge(chunk_done, c + 1)
                    pe.sem_inc(lvl_done, 1)

            for s in range(S_Q2, S_GH):
                tile(s, h_hi, h_lo)
                if s == S_Q2:
                    turn_values(HG - 1)
                chunk(s - S_Q2)
            turn_values(HG)
            pe.wait_ge(values_copied, HG + 1)
            for j in range(NI + 2):
                if j < NI:
                    i, g, t = ITEMS[j]
                    L = P if t == 0 else 2 * P
                    grp = slice(g * DH, (g + 1) * DH)
                    if j >= 2:
                        pe.wait_ge(s2_ready, j - 1)
                    pe.matmul(ps[4 + j % 2][:, 0:L], q2T[grp, i, t * P:(t + 1) * P], k2T[grp, (t + 1) * P - L:(t + 1) * P],
                              start=True, stop=True).then_inc(qk2_done, 1)
                c = chunk_at(j)
                if c is not None:
                    chunk(c)
                hd = av_at(j)
                if hd is not None:
                    pe.wait_ge(sel_done, N_SEL)
                    pe.wait_ge(off_copied, len(CHUNKS) - N_SEL)
                    if hd >= 2:
                        pe.wait_ge(av_copied, hd - 1)
                    for t in range(QT):
                        for k in range(t + 1):
                            if k == t:
                                w = hs[:, hd, t * P:(t + 1) * P]
                            elif (k, t) in OFF_AT:
                                w = off[:, hd, OFF_AT[k, t]:OFF_AT[k, t] + P]
                            ins = pe.matmul(ps[CHUNK_BANK[hd % 2]][:, t * P:(t + 1) * P], iN[:, k, hd * P:(hd + 1) * P],
                                            w, start=k == 0, stop=k == t)
                    ins.then_inc(av_done, 1)
                n = gh_at(j)
                if n is not None:
                    tile(S_GH + n, h_hi, h_lo)
                if 1 <= j <= NI:
                    m = j - 1
                    nk = 1 if ITEMS[m][2] == 0 else 2
                    pe.wait_ge(p2_ready, m + 1)
                    if m:
                        pe.wait_ge(t2_copied, m)
                    for kt in range(nk):
                        ins = pe.transpose(ps[6][:, kt * P:(kt + 1) * P], sc2[:, m % 2, kt * P:(kt + 1) * P], ident[:, :])
                    ins.then_inc(t2_done, 1)
                if j >= 2:
                    m = j - 2
                    i, g, t = ITEMS[m]
                    nk = 1 if t == 0 else 2
                    pe.wait_ge(t2_copied, m + 1)
                    if m and m % (2 * QT) == 0:
                        pe.wait_ge(o2_copied, m // (2 * QT))
                    for n in range(nk):
                        ins = pe.matmul(ps[2][g * DH:(g + 1) * DH, t * P:(t + 1) * P],
                                        v2N[:, t + 1 - nk + n, g * DH:(g + 1) * DH], pT2[:, m % 2, n * P:(n + 1) * P],
                                        start=n == 0, stop=n == nk - 1)
                    ins.then_inc(pv2_done, 1)
                hd = av_at(j - 1)
                if hd is not None:
                    pe.wait_ge(r_sq, hd + 1)
                    if hd:
                        pe.wait_ge(r_var, hd)
                    pe.matmul(ps[R_BANK][:, :], ones[:, :], sq[:, hd % 2, :], start=True, stop=True).then_inc(r_sum, 1)
            pe.wait_ge(av_copied, HG)
            for i in range(PAIRS):
                pe.wait_ge(n2_sq, i + 1)
                pe.matmul(ps[7][:, :], ones[:, :], sq[:, i % 2, :], start=i == 0, stop=i == PAIRS - 1).then_inc(n2_sum, 1)
            mixed_parts = lambda k: pe.wait_ge(n2_lo if k < PAIRS else r_lo, k % PAIRS + 1)
            for s in range(S_OUT2, S_UP2):
                tile(s, h_hi, h_lo, ready=mixed_parts if s == S_OUT2 else None)
                if s > S_OUT2:
                    norm_sum(4, s - S_OUT2 - 1)
            norm_sum(4, KD - 1)
            ffn_pe(S_UP2, 4)
            down(S_DOWN2, 1)
            pe.wait_ge(rooted, 6)
            for half in range(2):
                for t in range(QT):
                    for k in range(4 * half, 4 * half + 4):
                        if t == 0:
                            pe.wait_ge(y_ready, k + 1)
                        ins = pe.transpose(ps[4 * half + t][:, k % 4 * P:(k % 4 + 1) * P], xT[:, k, t * P:(t + 1) * P],
                                           ident[:, :])
                    ins.then_inc(y_turned, 1)


INPUTS = ["x", "norm1_g", "w_in", "cmp_pe_k", "cmp_pe_v", "cmp_k_w1", "cmp_k_w2", "cmp_v_w1", "cmp_v_w2",
          "w_attn_br", "conv_dw_w", "conv_dw_b", "conv_ln_g", "conv_ln_b", "w_conv_br", "w_out", "norm2_g",
          "ffn_w_up", "ffn_dw_w", "ffn_dw_b", "ffn_w_down", "final_g", "c_2", "ada_w_2", "ada_b_2",
          "mix_norm_g_2", "w_in_2", "b_in_2", "attn_sinks_2", "attn_out_g_2", "hgrn_lb_logits_2",
          "hgrn_out_g_2", "w_out_2", "ffn_norm_g_2", "w_up_2", "conv_w_2", "conv_b_2", "w_down_2",
          "final_norm_g_2"]


def kernel(**inputs):
    import concourse.bacc as bacc
    from concourse.bass_utils import run_bass_kernel_spmd as run

    nc = bacc.Bacc("TRN2", target_bir_lowering=False, num_devices=1)
    arrays, aps = {}, {}
    for name in INPUTS:
        arrays[f"in_{name}"] = np.ascontiguousarray(inputs[name])
        aps[name] = nc.dram_tensor(f"in_{name}", arrays[f"in_{name}"].shape, F32, kind="ExternalInput").ap()
    out = nc.dram_tensor("out", (1, T, D), F32, kind="ExternalOutput").ap()
    build(nc, aps, out)
    return run(nc, [arrays], core_ids=[0]).results[0]["out"]
```

```python
import numpy as np
import concourse.bass as bass
from concourse import mybir
from contextlib import ExitStack

F32 = mybir.dt.float32
F32R = mybir.dt.float32r
U8 = mybir.dt.uint8
ALU = mybir.AluOpType
ACT = mybir.ActivationFunctionType
AX = mybir.AxisListType

P = 128
D = 1024
T = 512
KD = D // P
QT = T // P
HEADS = 8
DH = 64
PAIRS = HEADS // 2
CMP_BLOCK, CMP_STRIDE = 32, 16
NCMP = (T - CMP_BLOCK) // CMP_STRIDE + 1
CONV_CH, CONV_W = 512, 31
CC = CONV_CH // P
PAD = CONV_W - 1
FFN = 2816
FT = FFN // P
PARTS = [(0, 8), (8, 7), (15, 7)]
MASKED = 1.0e30
EPS = 1e-6
SLOPES = [2.0 ** -(h + 1) for h in range(HEADS)]
SCALE = DH ** -0.5
HG = 4
NMOD = 6
LEVELS = [1, 2, 4, 8, 16, 32, 64]

S_CMP, S_Q, S_K, S_V, S_U, S_MERGE = 0, 2, 6, 8, 10, 18
S_ATTN, S_CONV, S_OUT, S_UP, S_DOWN = 34, 42, 50, 58, 102
S_FH, S_QH, S_IH, S_Q2, S_KV2, S_GH = 126, 130, 134, 138, 142, 144
S_OUT2, S_UP2, S_DOWN2, S_END = 148, 156, 200, 224

ADA_EARLY = 6
ADA_UP = FT


ALL = LEVELS + [128, 256]
GELU_C = 0.7978845608028654

CHUNKS = [(1, (h,), None) for h in range(HG)]
CHUNKS += [(b, (2 * c, 2 * c + 1), n) for n, b in enumerate(ALL[:-1]) for c in range(2)]
CHUNKS += [(256, (h,), len(ALL) - 1) for h in range(HG)]
SUMMED_CHUNKS = HG + 2
N_SEL = HG + 2 * len(LEVELS)
CHUNK_BANK = [3, 7]
R_BANK = 1
V_BANK = [2, 4, 2, 4, 5]
OFF_AT = {(0, 1): 0, (2, 3): 128, (0, 2): 256, (0, 3): 384, (1, 2): 512, (1, 3): 640}
EARLY_CHUNKS = S_GH - S_Q2


def chunk_at(j):
    return j + EARLY_CHUNKS if 0 <= j < len(CHUNKS) - EARLY_CHUNKS else None


def off_chunk_at(j):
    c = chunk_at(j)
    return c if c is not None and c >= N_SEL else None


def av_at(j):
    return (j - 20) // 3 if j >= 20 and (j - 20) % 3 == 0 and (j - 20) // 3 < HG else None


def gh_at(j):
    return (j - 19) // 3 if j >= 19 and (j - 19) % 3 == 0 and (j - 19) // 3 < HG else None


def small_rows():
    sizes = [("norm1_g", 8), ("norm2_g", 8), ("final_g", 8), ("mix_norm_g_2", 8), ("ffn_norm_g_2", 8),
             ("final_norm_g_2", 8), ("c_2", 8), ("conv_dw_b", 4), ("conv_ln_g", 4), ("conv_ln_b", 4),
             ("ada_b_2", 48), ("hgrn_out_g_2", 4), ("hgrn_lb_logits_2", 8), ("conv_dw_w", 124),
             ("ffn_dw_w", 132), ("ffn_dw_b", 44), ("conv_w_2", 66), ("conv_b_2", 22),
             ("bq", 4), ("attn_out_g_2", 4), ("bk", 1), ("bv", 1), ("bqh", 4), ("bfh", 4), ("bih", 4), ("bgh", 4),
             ("pe_k", 32), ("pe_v", 32)]
    at, where = 0, {}
    for name, n in sizes:
        where[name] = (at, n)
        at += n
    return where, at


def evacuations():
    bank, freed = {}, {}
    count = {"act": 0, "dve": 0}

    def out(s, who):
        count[who] += 1
        freed[s] = (who, count[who])

    for s in range(S_END):
        if s < S_OUT or S_FH <= s < S_OUT2:
            bank[s] = s % 2 if s < S_GH else 0
            if S_U <= s < S_MERGE and (s - S_U) % 4 >= 2:
                bank[s] = 6 + s % 2
        elif S_DOWN <= s < S_FH or s >= S_DOWN2:
            n = s - (S_DOWN if s < S_FH else S_DOWN2)
            bank[s] = (n // 6 * 2 + n % 2) % 4
        else:
            bank[s] = s % 4
    for s in range(S_END):
        if s < S_Q:
            out(s, "dve")
        elif s < S_U:
            out(s, "act")
        elif s < S_MERGE:
            out(s, "dve" if (s - S_U) % 4 < 2 else "act")
        elif s < S_ATTN:
            out(s, "act")
        elif s < S_DOWN:
            out(s, "dve")
        elif s < S_FH:
            if (s - S_DOWN) % 6 >= 4:
                out(s, "dve")
        elif s < S_OUT2:
            out(s, "act")
        elif s < S_DOWN2:
            out(s, "dve")
        elif (s - S_DOWN2) % 6 >= 4:
            out(s, "dve")
    return bank, freed


def build(nc, a, out):
    where, n_small = small_rows()
    BANK, FREED = evacuations()
    NSM = (n_small + P - 1) // P

    ctx = ExitStack()
    with ctx:
        base = (nc.sbuf_base + 63) // 64 * 64
        end = nc.sbuf_usable_end
        offset = [base]

        def sb(name, shape, dtype=F32, at=None):
            size = int(np.prod(shape[1:])) * (1 if dtype == U8 else 4)
            if at is None:
                at = offset[0]
                offset[0] += (size + 31) // 32 * 32
            assert at + size <= end, (name, at, size, end)
            return nc.alloc_sbuf_tensor_at(name, list(shape), dtype, offset=at)

        def sem(name):
            return nc.alloc_semaphore(name)

        raw = [sb(f"raw{i}", [P, 2048]) for i in range(2)]
        w_hi = [sb(f"w_hi{i}", [P, 8, P], F32R) for i in range(4)]
        w_lo = [sb(f"w_lo{i}", [P, 8, P], F32R) for i in range(4)]
        xT = sb("xT", [P, KD, T])
        h_hi = sb("h_hi", [P, KD, T], F32R)
        h_lo = sb("h_lo", [P, KD, T], F32R)
        ident = sb("ident", [P, P])
        ones = sb("ones", [P, P])
        small = sb("small", [P, NSM, P])
        sm = small[:, :, :].rearrange("p a b -> p (a b)")
        rstd = sb("rstd", [P, T])
        sq = sb("sq", [P, 2, T])
        hn = sb("hn", [P, 2, T])
        mod = sb("mod", [P, NMOD * KD])
        gain2 = sb("gain2", [P, 2, KD])
        cond = sb("cond", [P, KD])
        lower = sb("lower", [P, 4, HG])
        nq_bias = sb("nq_bias", [P, PAIRS])
        sinks = sb("sinks", [P, 2, HEADS])
        eps_t = sb("eps_t", [P, 1])
        scratch = sb("scratch", [P, 1])
        stat = sb("stat", [P, 64])
        gates = sb("gates", [P, QT, 24])

        G0 = offset[0]

        qT = sb("qT", [P, PAIRS, T])
        kT = sb("kT", [P, 2, T])
        vN = sb("vN", [P, 2, QT, P])
        mg_at = offset[0]
        mg = sb("mg", [P, 2 * KD, T])
        w1 = [sb(f"w1_{n}", [P, CMP_BLOCK, P], at=mg_at + n * 16384) for n in range(2)]
        z = sb("z", [P, CC, PAD + T])
        acc_at = offset[0]
        acc = sb("acc", [P, CC, T])
        rows = sb("rows", [P, NSM, P], at=acc_at)
        wg = sb("wg", [P, KD, 24], at=acc_at + 4096)
        wg_hi = sb("wg_hi", [P, KD, 24], F32R, at=acc_at + 5120)
        wg_lo = sb("wg_lo", [P, KD, 24], F32R, at=acc_at + 6144)
        dist = sb("dist", [P, T])
        cdist = sb("cdist", [P, QT, 32])
        cvalid = sb("cvalid", [P, QT, 32])
        cbias = sb("cbias", [P, QT * HEADS, 32])
        cp = sb("cp", [P, QT * HEADS, 32])
        w2 = sb("w2", [P, 2, DH])
        hc = sb("hc", [P, 3, 2, 2, 32])
        kcT = sb("kcT", [P, 32])
        vcN = sb("vcN", [32, P])
        pcT = sb("pcT", [32, 2, P])
        sc_at = offset[0]
        sc = sb("sc", [P, 2, 2, T])
        pT = sb("pT", [P, 2, 2, T])
        x_in = sb("x_in", [P, QT, D], at=sc_at)
        blk = sb("blk", [P, 2, CMP_BLOCK, NCMP], at=sc_at + 8192)
        att_hi = sb("att_hi", [P, PAIRS, T], F32R, at=sc_at)
        att_lo = sb("att_lo", [P, PAIRS, T], F32R, at=sc_at + 8192)
        z_at = acc_at - 4 * CC * (PAD + T)
        z_at = (z_at + 31) // 32 * 32
        cv_hi = sb("cv_hi", [P, CC, T], F32R, at=z_at)
        kv_at = G0 + 4 * PAIRS * T
        cv_lo = sb("cv_lo", [P, CC, T], F32R, at=kv_at)
        hbias = [sq[:, n, :] for n in range(2)]
        sgt = [hn[:, n, :] for n in range(2)]
        top1 = offset[0]

        offset[0] = G0
        g_hi = sb("g_hi", [P, FT, T], F32R)
        g_lo = sb("g_lo", [P, FT, T], F32R)
        ada_at = offset[0]
        ada = [sb(f"ada{n}", [P, KD, P], at=ada_at + 4096 * n) for n in range(2)]
        ada_sum = [sb(f"ada_sum{n}", [P, P], at=ada_at + 8192 + 512 * n) for n in range(2)]
        ua = sq
        uv = hn
        assert max(top1, ada_at + 9216) <= end

        offset[0] = G0
        q2T = sb("q2T", [P, PAIRS, T])
        k2T = sb("k2T", [P, T])
        v2N = sb("v2N", [P, QT, P])
        hq = sb("hq", [P, HG, T])
        hk = sb("hk", [P, HG, T])
        f_at = offset[0]
        hf = sb("hf", [P, HG, T])
        hgo = sb("hgo", [P, HG, T], at=f_at)
        hg = sb("hg", [P, HG, T])
        iN = sb("iN", [P, QT, T])
        qd = [sb(f"qd{n}", [P, HG, T // 2]) for n in range(2)]
        kd = sb("kd", [P, HG, T])
        hs = sb("hs", [P, HG, T])
        off_at = offset[0]
        off = sb("off", [P, HG, 768])
        mask = sb("mask", [P, len(LEVELS), DH], U8)
        eye8 = sb("eye8", [P, P], U8)
        dist2 = sb("dist2", [P, 2 * P])
        sc2 = sb("sc2", [P, 2, 2 * P])
        pT2 = sb("pT2", [P, 2, 2 * P])
        msk_f = sb("msk_f", [P, P], at=off_at + 8192)
        kd_odd = sb("kd_odd", [P, HG, T], at=off_at)
        keys_at = [None if n == 0 else kd_odd if n in (1, 3, 5) else kd for n in range(len(ALL))]
        assert offset[0] <= end, (offset[0], end)
        offset[0] = G0
        y_out = sb("y_out", [P, QT, D])
        Y_BANK = [[4, 5, 6, 0], [1, 2, 3, 7]]

        ps = [nc.alloc_psum_tensor(f"ps{i}", [P, 512], F32) for i in range(8)]

        raw_in = [sem(f"raw_in{i}") for i in range(2)]
        hi_done, lo_done, tile_done = sem("hi_done"), sem("lo_done"), sem("tile_done")
        freed = {"act": sem("freed_by_act"), "dve": sem("freed_by_dve")}
        x_loaded = [sem(f"x_loaded{t}") for t in range(QT)]
        w1_loaded, wg_loaded = sem("w1_loaded"), sem("wg_loaded")
        small_loaded = [sem("small_loaded_by_act"), sem("small_loaded_by_pool")]
        misc_loaded = sem("misc_loaded")
        consts = sem("consts")
        x_turned, x_copied = sem("x_turned"), sem("x_copied")
        small_turned, small_ready = sem("small_turned"), sem("small_ready")
        squared, summed, rooted, inverted = sem("squared"), sem("summed"), sem("rooted"), sem("inverted")
        normed, n_hi = sem("normed"), sem("n_hi")
        n_lo = [sem("n_lo_even"), sem("n_lo_odd")]
        squared2, summed2, mean_ready, shifted = sem("squared2"), sem("summed2"), sem("mean_ready"), sem("shifted")
        hid_done, hid_copied, gelu_parts, gelu_done = (
            sem("hid_done"), sem("hid_copied"), sem("gelu_parts"), sem("gelu_done"))
        cmp_kv_done, cmp_kv_copied = sem("cmp_kv_done"), sem("cmp_kv_copied")
        wg_split_hi, wg_split, gate_done, gate_ready = sem("wg_split_hi"), sem("wg_split"), sem("gate_done"), sem("gate_ready")
        sig_ready, cbias_ready = sem("sig_ready"), sem("cbias_ready")
        cqk_done, cx_ready, cexp_done, cp_ready = sem("cqk_done"), sem("cx_ready"), sem("cexp_done"), sem("cp_ready")
        hbias_ready, qk_done, scores_ready, exp_done, p_ready = (
            sem("hbias_ready"), sem("qk_done"), sem("scores_ready"), sem("exp_done"), sem("p_ready"))
        pc_turned, ps_turned, pw_turned = sem("pc_turned"), sem("ps_turned"), sem("pw_turned")
        pc_copied, ps_copied, pw_copied = sem("pc_copied"), sem("ps_copied"), sem("pw_copied")
        pv_done, o_copied = sem("pv_done"), sem("o_copied")
        tap_done, ln_sum, ln_centred, ln_sq, ln_sqsum, ln_root, ln_norm, cv_ready, cv_hi_done, cv_lo_done = (
            sem("tap_done"), sem("ln_sum"), sem("ln_centred"), sem("ln_sq"), sem("ln_sqsum"), sem("ln_root"),
            sem("ln_norm"), sem("cv_ready"), sem("cv_hi_done"), sem("cv_lo_done"))
        att_hi_done, att_lo_done, gate_sig = sem("att_hi_done"), sem("att_lo_done"), sem("gate_sig")
        merged, m_hi, m_lo = sem("merged"), sem("m_hi"), sem("m_lo")
        biased, tap1_done, silu_done, prod_done, g_hi_done, g_lo_done = (
            sem("biased"), sem("tap1_done"), sem("silu_done"), sem("prod_done"), sem("g_hi_done"), sem("g_lo_done"))
        ada_in = [sem(f"ada_in{i}") for i in range(2)]
        ada_scaled, ada_summed, ada_done, cond_ready = sem("ada_scaled"), sem("ada_summed"), sem("ada_done"), sem("cond_ready")
        x2_ready = sem("x2_ready")
        lb_max, lb_exp, lb_ready = sem("lb_max"), sem("lb_exp"), sem("lb_ready")
        f_ready, k_scaled, q_scaled, chunk_done, lvl_done, sel_done, off_copied, f_merged, g_merged = (
            sem("f_ready"), sem("k_scaled"), sem("q_scaled"), sem("chunk_done"), sem("lvl_done"),
            sem("sel_done"), sem("off_copied"), sem("f_merged"), sem("g_merged"))
        setup2 = sem("setup2")
        qk2_done, s2_ready, e2_done, p2_ready, t2_done, t2_copied, pv2_done, o2_copied = (
            sem("qk2_done"), sem("s2_ready"), sem("e2_done"), sem("p2_ready"), sem("t2_done"),
            sem("t2_copied"), sem("pv2_done"), sem("o2_copied"))
        n2_sq, n2_sum, n2_root, n2_norm, n2_hi, n2_lo = (
            sem("n2_sq"), sem("n2_sum"), sem("n2_root"), sem("n2_norm"), sem("n2_hi"), sem("n2_lo"))
        av_done, av_copied, r_sq, r_sum, r_var, r_inv, r_root, r_norm, r_hi, r_lo, gate2_silu = (
            sem("av_done"), sem("av_copied"), sem("r_sq"), sem("r_sum"), sem("r_var"), sem("r_inv"), sem("r_root"),
            sem("r_norm"), sem("r_hi"), [sem("r_lo_by_pool"), sem("r_lo_by_dve")], sem("gate2_silu"))
        y_ready, y_turned, stored = sem("y_ready"), sem("y_turned"), sem("stored")
        squares_added, y_sum, y_root, y_inv = sem("squares_added"), sem("y_sum"), sem("y_root"), sem("y_inv")
        y_copied = [sem("y_copied_act"), sem("y_copied_dve")]
        v_turned, v_copied, hid_rows, hid_turned, sig_turned = (
            sem("v_turned"), sem("v_copied"), sem("hid_rows"), sem("hid_turned"), sem("sig_turned"))
        r_scaled, multiplied = sem("r_scaled"), sem("multiplied")
        values_turned, values_copied = sem("values_turned"), sem("values_copied")
        act_chain, dve_chain, pool_chain = sem("act_chain"), sem("dve_chain"), sem("pool_chain")

        def col(name, i=0, n=1):
            at = where[name][0]
            return sm[:, at + i:at + i + n] if isinstance(i, int) else sm[:, bass.ds(i + at, n)]

        def k_tiles(w, rows_from, nk, c0, n=2 * P):
            return w[rows_from:rows_from + nk * P, bass.ds(c0, n)].rearrange("(k p) n -> p k n", p=P)

        def standard(w, c0, u, nk=KD, r0=0):
            return [(raw[u % 2][:, 0:nk * 256].rearrange("p (k n) -> p k n", k=nk), k_tiles(w, r0, nk, c0))]

        def two_columns(w, cols, u, width=P):
            dst = raw[u % 2][:, :].rearrange("p (k n) -> p k n", k=KD)
            return [(dst[:, :, n * width:(n + 1) * width], k_tiles(w, 0, KD, c, width)) for n, c in enumerate(cols)]

        def paired_columns(w, c0, i, u):
            return two_columns(w, [c0 + g * 256 + (i + m) * DH for m in range(2) for g in range(2)], u, DH)

        def paired_rows(w, c0, u, nk_dst=PAIRS, more=None):
            dst = raw[u % 2][:, 0:nk_dst * 256].rearrange("p (k n) -> p k n", k=nk_dst)
            got = [(dst[g * DH:(g + 1) * DH, 0:PAIRS, :],
                    w[g * 256:(g + 1) * 256, c0:c0 + 256].rearrange("(i d) n -> d i n", d=DH)) for g in range(2)]
            if more is not None:
                got.append((dst[:, PAIRS:nk_dst, :], k_tiles(w, PAIRS * P, nk_dst - PAIRS, c0)))
            return got

        w_in, w_in2 = a["w_in"][0], a["w_in_2"][0]
        LOADS = {}
        for n in range(S_END // 2):
            s = 2 * n
            if s < S_Q:
                LOADS[n] = standard(w_in, 512, n)
            elif s < S_K:
                LOADS[n] = paired_columns(w_in, 0, s - S_Q, n)
            elif s < S_V:
                LOADS[n] = two_columns(w_in, [768, 1024], n)
            elif s < S_U:
                LOADS[n] = two_columns(w_in, [896, 1152], n)
            elif s < S_MERGE:
                m = (s - S_U) // 2
                LOADS[n] = standard(w_in, 1304 + (m % 2) * CONV_CH + (m // 2) * 256, n)
            elif s < S_ATTN:
                LOADS[n] = standard(w_in, 2328 + (s - S_MERGE) * P, n)
            elif s < S_CONV:
                LOADS[n] = paired_rows(a["w_attn_br"][0], (s - S_ATTN) * P, n)
            elif s < S_OUT:
                LOADS[n] = standard(a["w_conv_br"][0], (s - S_CONV) * P, n, CC)
            elif s < S_UP:
                LOADS[n] = standard(a["w_out"][0], (s - S_OUT) * P, n)
            elif s < S_DOWN:
                m = (s - S_UP) // 2
                LOADS[n] = standard(a["ffn_w_up"][0], (m % 2) * FFN + (m // 2) * 256, n)
            elif s < S_FH or s >= S_DOWN2:
                w = a["ffn_w_down"][0] if s < S_FH else a["w_down_2"][0]
                m = (s - (S_DOWN if s < S_FH else S_DOWN2)) // 2
                k0, nk = PARTS[m % 3]
                LOADS[n] = standard(w, m // 3 * 256, n, nk, k0 * P)
            elif s < S_QH:
                LOADS[n] = standard(w_in2, 1280 + (s - S_FH) * P, n)
            elif s < S_IH:
                LOADS[n] = standard(w_in2, 768 + (s - S_QH) * P, n)
            elif s < S_Q2:
                LOADS[n] = standard(w_in2, 1792 + (s - S_IH) * P, n)
            elif s < S_KV2:
                LOADS[n] = paired_columns(w_in2, 0, s - S_Q2, n)
            elif s < S_GH:
                LOADS[n] = standard(w_in2, 512, n)
            elif s < S_OUT2:
                LOADS[n] = standard(w_in2, 2304 + (s - S_GH) * P, n)
            elif s < S_UP2:
                LOADS[n] = paired_rows(a["w_out_2"][0], (s - S_OUT2) * P, n, KD, True)
            else:
                m = (s - S_UP2) // 2
                LOADS[n] = standard(a["w_up_2"][0], (m % 2) * FFN + (m // 2) * 256, n)
        RAW_COUNT, total = {}, [0, 0]
        for n in range(S_END // 2):
            total[n % 2] += 16 * len(LOADS[n])
            RAW_COUNT[n] = total[n % 2]
        DEPTH_OF = {s: (4 if S_ATTN <= s < S_OUT else
                        PARTS[(s - (S_DOWN if s < S_FH else S_DOWN2)) // 2 % 3][1]
                        if S_DOWN <= s < S_FH or s >= S_DOWN2 else KD) for s in range(S_END)}

        def wait_bank(eng, s, shift=0):
            prev = max((t for t in range(s) if BANK[t] == BANK[s] and t in FREED), default=None)
            if prev is not None:
                who, n = FREED[prev]
                eng.wait_ge(freed[who], n + shift)

        def x_ready(eng, norm, k):
            if norm == 0:
                eng.wait_ge(x_copied, k + 1)
            else:
                s = {1: S_OUT + k, 4: S_OUT2 + k,
                     2: S_DOWN + k // 2 * 6 + 4 + k % 2, 5: S_DOWN2 + k // 2 * 6 + 4 + k % 2}[norm]
                eng.wait_ge(freed["dve"], FREED[s][1])

        SQ_BASE = {0: 0, 1: 8, 2: 16, 4: 24, 5: 32}
        HN_BASE = {0: 0, 1: 8, 3: 16, 4: 24}
        ROOT = {0: 1, 1: 2, 3: 3, 2: 4, 4: 5, 5: 6}

        def normed_tile(norm, k):
            return hn[:, k % 2, :] if norm == 3 else (hn, sq)[k // 2 % 2][:, k % 2, :]

        def lo_ready(eng, norm, k):
            eng.wait_ge(n_lo[k % 2], (HN_BASE[norm] + k) // 2 + 1)

        ITEMS = [(i, g, t) for i in range(PAIRS) for g in range(2) for t in range(QT)]
        NI = len(ITEMS)
        FIRST_KEYS = [max(0, t - 1) for t in range(QT)]

        def small_dmas(eng, which):
            flat = rows[:, :, :]

            def put(name, rows_ap, c0=0, c1=P, n=None):
                at, n = where[name][0], n or where[name][1]
                done = 0
                while done < n:
                    r, m = (at + done) % P, (at + done) // P
                    take = min(n - done, P - r)
                    mine = 1 if m == NSM - 1 or (r + m) % 4 else 0
                    if mine == which:
                        eng.dma_start(flat[r:r + take, m, c0:c1],
                                      rows_ap[done:done + take, :]).then_inc(small_loaded[which], 16)
                        small_total[which] += 16
                    done += take

            as_rows = lambda v, n: v.rearrange("a (r c) -> (a r) c", c=n)
            for name in ("norm1_g", "norm2_g", "mix_norm_g_2", "ffn_norm_g_2", "c_2", "conv_dw_b", "conv_ln_g",
                         "conv_ln_b", "ada_b_2", "hgrn_out_g_2", "hgrn_lb_logits_2", "ffn_dw_b", "conv_b_2"):
                put(name, as_rows(a[name], P))
            for name in ("final_g", "final_norm_g_2"):
                put(name, a[name].rearrange("(r c) -> r c", c=P))
            for name in ("conv_dw_w", "ffn_dw_w", "conv_w_2"):
                put(name, as_rows(a[name][0], P))
            b = a["b_in_2"]
            put("bk", as_rows(b[:, 512:], P), n=18)
            for g in range(2):
                put("bq", as_rows(b[:, g * 256:(g + 1) * 256], DH), g * DH, (g + 1) * DH)
                put("attn_out_g_2", as_rows(a["attn_out_g_2"][:, g * 256:(g + 1) * 256], DH), g * DH, (g + 1) * DH)
                put("pe_k", a["cmp_pe_k"][0], g * DH, (g + 1) * DH)
                put("pe_v", a["cmp_pe_v"][0], g * DH, (g + 1) * DH)
        small_total = [0, 0]

        def tables2(pool, link, m):
            if m == 0:
                link(pool.memset(dist2[:, :], 0.0))
                link(pool.affine_select(out=dist2[:, :], in_=dist2[:, :], compare_op=ALU.is_ge, fill=MASKED,
                                        base=P, pattern=[[-1, 2 * P]], channel_multiplier=1))
                link(pool.affine_select(out=dist2[:, :], in_=dist2[:, :], compare_op=ALU.is_ge, fill=MASKED,
                                        base=-1, pattern=[[1, 2 * P]], channel_multiplier=-1))
                link(pool.memset(msk_f[:, :], 0.0))
                link(pool.affine_select(out=msk_f[:, :], in_=msk_f[:, :], compare_op=ALU.not_equal, fill=1.0, base=0,
                                        pattern=[[-1, P]], channel_multiplier=1))
                link(pool.tensor_copy(eye8[:, :], msk_f[:, :]))
                return
            start = {4: (hg, 1.0), 5: (hs, 0.0), 6: (kd, 0.0), 7: (kd_odd, 0.0)}
            if m in start:
                link(pool.memset(start[m][0][:, :, :], start[m][1]))
            b = LEVELS[m - 1]
            nb = P // (2 * b)
            v = msk_f[:, 0:DH].rearrange("p (m c) -> p m c", m=nb)
            link(pool.memset(msk_f[:, 0:DH], 1.0))
            link(pool.affine_select(out=v, in_=v, compare_op=ALU.is_ge, fill=0.0, base=0,
                                    pattern=[[-2 * b, nb], [0, b]], channel_multiplier=1))
            link(pool.affine_select(out=v, in_=v, compare_op=ALU.is_ge, fill=0.0, base=b - 1,
                                    pattern=[[2 * b, nb], [0, b]], channel_multiplier=-1))
            ins = pool.tensor_copy(mask[:, m - 1, :], msk_f[:, 0:DH])
            if m < len(LEVELS):
                link(ins)
            else:
                ins.then_inc(setup2, 1)

        def pairs_of(x, b):
            return x[:, :, :].rearrange("p h t -> p (h t)").rearrange("p (m e c) -> p m e c", e=2, c=b)

        def hgrn_pool(pool, lo):
            s = S_Q2
            pool.wait_ge(f_ready, 2 * HG)
            for n, b in enumerate(ALL):
                g, f, k = pairs_of(hg, b), pairs_of(hf, b), pairs_of(hk, b)
                if n:
                    kk = pairs_of(keys_at[n], b)
                    before = [m for m in range(1, n) if keys_at[m] is keys_at[n]]
                    if before:
                        pool.wait_ge(lvl_done, before[-1] + 1)
                    pool.tensor_tensor(kk[:, :, 0, :], k[:, :, 0, :], g[:, :, 0, :], ALU.mult).then_inc(k_scaled, 1)
                if n < len(ALL) - 1:
                    if n:
                        pool.wait_ge(f_merged, n)
                    pool.tensor_tensor(g[:, :, 0, :], g[:, :, 0, :],
                                       f[:, :, 1, b - 1:b].to_broadcast([P, HG * T // (2 * b), b]),
                                       ALU.mult).then_inc(g_merged, 1)
                    pool.wait_ge(g_merged, n + 1)
                while s < (S_GH, S_GH + 4)[n > 0]:
                    lo(s)
                    s += 1
            for s in range(s, S_OUT2 + 4):
                lo(s)
            pool.wait_ge(r_root, 1)
            for hd in range(HG):
                pool.wait_ge(av_copied, hd + 1)
                pool.tensor_tensor(hq[:, hd, :], hq[:, hd, :], kd[:, hd, :], ALU.mult).then_inc(r_scaled, 1)
            for hd in range(2):
                pool.wait_ge(r_hi, hd + 1)
                pool.tensor_tensor(h_lo[:, PAIRS + hd, :], hq[:, hd, :], h_hi[:, PAIRS + hd, :].bitcast(F32),
                                   ALU.subtract).then_inc(r_lo[0], 1)
            for s in range(S_OUT2 + 4, S_UP2 + 4):
                lo(s)

        block = ctx.enter_context(nc.Block())

        @block.sync
        def _(sp):
            for t in range(QT):
                sp.dma_start(x_in[:, t, :], a["x"][0, t * P:(t + 1) * P, :]).then_inc(x_loaded[t], 16)

            def unit(n):
                if n >= 2:
                    sp.wait_ge(lo_done, 2 * n - 2)
                for dst, src in LOADS[n]:
                    sp.dma_start(dst, src).then_inc(raw_in[n % 2], 16)

            unit(0)
            unit(1)
            def ada_load(n, c0=None, count=None):
                if n >= 2:
                    sp.wait_ge(ada_summed, n - 1 if count is None else count)
                sp.dma_start(ada[n % 2][:, :, :],
                             k_tiles(a["ada_w_2"][0], 0, KD, n * P if c0 is None else c0, P)).then_inc(ada_in[n % 2], 16)

            unit(2)
            for n, w in enumerate(("cmp_k_w1", "cmp_v_w1")):
                for g in range(2):
                    sp.dma_start(w1[n][g * DH:(g + 1) * DH, :, :],
                                 a[w][0].rearrange("(i d) n -> d i n", d=DH)).then_inc(w1_loaded, 16)
            for n in range(3, S_OUT // 2 + 1):
                unit(n)
            sp.wait_ge(tile_done, S_CONV)
            for n in range(2):
                ada_load(n)
            for n in range(S_OUT // 2 + 1, S_OUT // 2 + 4):
                unit(n)
            for n in range(3):
                ada_load(2 * n + 2)
                unit(S_UP // 2 + n)
                ada_load(2 * n + 3)
            unit(S_UP // 2 + 3)
            w = a["ffn_w_up"][0]
            with sp.Fori(0, FT // 2 - 2) as i:
                for half in range(2):
                    n = S_UP // 2 + 4 + half
                    sp.wait_ge(lo_done, i * 4 + (2 * n - 2))
                    sp.dma_start(raw[n % 2][:, :].rearrange("p (k n) -> p k n", k=KD),
                                 k_tiles(w, 0, KD, i * 256 + (512 + half * FFN))).then_inc(raw_in[n % 2], 16)
                    n = ADA_EARLY + 2 + half
                    ada_load(n, i * 256 + n * P, i * 2 + (n - 1))
            n = ADA_EARLY + ADA_UP - 2
            for m in range(4):
                unit(S_DOWN // 2 + m)
                ada_load(n + m)
            for m in range(24):
                if m % 2:
                    unit((S_DOWN + 7 + m) // 2)
                if n + 4 + m < NMOD * KD:
                    ada_load(n + 4 + m)
            for n in range((S_FH + 8) // 2, S_UP2 // 2):
                unit(n)
            w = a["w_up_2"][0]
            u0 = S_UP2 // 2
            with sp.Fori(0, FT // 2) as i:
                for half in range(2):
                    n = u0 + half
                    sp.wait_ge(lo_done, i * 4 + (2 * n - 2))
                    sp.dma_start(raw[n % 2][:, :].rearrange("p (k n) -> p k n", k=KD),
                                 k_tiles(w, 0, KD, i * 256 + half * FFN)).then_inc(raw_in[n % 2], 16)
            for n in range(S_DOWN2 // 2, S_END // 2):
                unit(n)
            for t in range(QT):
                for half in range(2):
                    sp.wait_ge(y_copied[half], t + 1)
                sp.dma_start(out[0, t * P:(t + 1) * P, :], y_out[:, t, :]).then_inc(stored, 16)
            sp.wait_ge(stored, 16 * QT)

        @block.gpsimd
        def _(pool):
            chain = [0]

            def link(ins):
                chain[0] += 1
                ins.then_inc(pool_chain, 1)
                pool.wait_ge(pool_chain, chain[0])

            link(pool.memset(ident[:, :], 0.0))
            link(pool.affine_select(out=ident[:, :], in_=ident[:, :], compare_op=ALU.not_equal, fill=1.0,
                                    base=0, pattern=[[-1, P]], channel_multiplier=1))
            pool.memset(eps_t[:, :], EPS)
            pool.memset(ones[:, :], 1.0).then_inc(consts, 1)
            link(pool.memset(rows[:, NSM - 1, :], 0.0))
            small_dmas(pool, 1)
            link(pool.iota(dist[:, :], [[-1, T]], base=T - P, channel_multiplier=1,
                           allow_small_or_imprecise_dtypes=True))
            link(pool.affine_select(out=dist[:, :], in_=dist[:, :], compare_op=ALU.is_ge, fill=MASKED,
                                    base=T - P, pattern=[[-1, T]], channel_multiplier=1))
            cpat = [[P, QT], [-CMP_STRIDE, 32]]
            link(pool.iota(cdist[:, :, :], cpat, base=1 - CMP_BLOCK, channel_multiplier=1,
                           allow_small_or_imprecise_dtypes=True))
            link(pool.affine_select(out=cdist[:, :, :], in_=cdist[:, :, :], compare_op=ALU.is_ge, fill=MASKED,
                                    base=1 - CMP_BLOCK, pattern=cpat, channel_multiplier=1))
            link(pool.memset(cvalid[:, :, :], 1.0))
            pool.affine_select(out=cvalid[:, :, :], in_=cvalid[:, :, :], compare_op=ALU.is_ge, fill=0.0,
                               base=1 - CMP_BLOCK, pattern=cpat, channel_multiplier=1).then_inc(consts, 1)
            pool.memset(z[:, :, 0:PAD], 0.0).then_inc(consts, 1)

            def lo(s, slot=None, count=None):
                pool.wait_ge(hi_done, s + 1 if count is None else count)
                slot = s if slot is None else slot
                nk = 8 if count is not None else DEPTH_OF[s]
                part = raw[slot // 2 % 2][:, 0:nk * 256].rearrange("p (k n) -> p k n", k=nk)
                pool.tensor_tensor(w_lo[slot % 4][:, 0:nk, :], part[:, :, slot % 2 * P:(slot % 2 + 1) * P],
                                   w_hi[slot % 4][:, 0:nk, :].bitcast(F32), ALU.subtract).then_inc(lo_done, 1)

            def norm_lo(norm):
                for k in range(1, KD, 2):
                    pool.wait_ge(n_hi, HN_BASE[norm] + k + 1)
                    pool.tensor_tensor(h_lo[:, k, :], normed_tile(norm, k), h_hi[:, k, :].bitcast(F32),
                                       ALU.subtract).then_inc(n_lo[1], 1)

            for s in range(S_UP + 4):
                lo(s)
                if s == 1:
                    norm_lo(0)
            norm_lo(1)
            with pool.Fori(0, FT // 2 - 1) as i:
                for j in range(4):
                    lo(None, S_UP + j, i * 4 + (S_UP + j + 5))
            for s in range(S_DOWN, S_Q2):
                lo(s)
                if s == S_FH + 3:
                    norm_lo(3)
                if s >= S_FH + 4:
                    tables2(pool, link, s - S_FH - 4)
            hgrn_pool(pool, lo)
            norm_lo(4)
            with pool.Fori(0, FT // 2 - 1) as i:
                for j in range(4):
                    lo(None, S_UP2 + j, i * 4 + (S_UP2 + j + 5))
            for s in range(S_DOWN2, S_END):
                lo(s)

        @block.scalar
        def _(act):
            chain = [0]

            def link(ins):
                chain[0] += 1
                ins.then_inc(act_chain, 1)
                act.wait_ge(act_chain, chain[0])

            def hi(s):
                if s >= S_END:
                    return
                u = s // 2
                act.wait_ge(raw_in[u % 2], RAW_COUNT[u])
                if s >= 4:
                    act.wait_ge(tile_done, s - 3)
                nk = DEPTH_OF[s]
                part = raw[u % 2][:, 0:nk * 256].rearrange("p (k n) -> p k n", k=nk)
                act.activation(w_hi[s % 4][:, 0:nk, :], part[:, :, s % 2 * P:(s % 2 + 1) * P],
                               ACT.Copy).then_inc(hi_done, 1)

            def evac(s, dst, func=ACT.Copy, src=None, **kw):
                act.wait_ge(tile_done, s + 1)
                act.activation(dst, ps[BANK[s]][:, :] if src is None else src, func, **kw).then_inc(freed["act"], 1)

            def load_sqrt():
                act.activation(scratch[:, :], eps_t[:, :], ACT.Sqrt)

            def square(norm, k):
                x_ready(act, norm, k)
                if k >= 2 and norm == 5:
                    act.wait_ge(squares_added, k - 1)
                elif k >= 2:
                    act.wait_ge(summed, SQ_BASE[norm] + k - 1)
                act.activation(sq[:, k % 2, :], xT[:, k, :], ACT.Square).then_inc(squared, 1)

            def root(norm):
                act.wait_ge(summed, SQ_BASE[norm] + KD)
                act.activation(rstd[:, :], ps[7][:, :], ACT.Sqrt, scale=1.0 / D, bias=eps_t[:, 0:1]).then_inc(rooted, 1)

            def norm_hi(norm, shift=None):
                for k in range(KD):
                    act.wait_ge(normed, HN_BASE[norm] + k + 1)
                    t = normed_tile(norm, k)
                    if shift is None:
                        act.activation(h_hi[:, k, :], t, ACT.Copy).then_inc(n_hi, 1)
                    elif k % 2 == 0:
                        act.activation(h_hi[:, k, :], t, ACT.Identity, bias=shift(k)).then_inc(n_hi, 1)
                    else:
                        act.activation(t, t, ACT.Identity, bias=shift(k)).then_inc(shifted, 1)
                        act.wait_ge(shifted, (HN_BASE[norm] - HN_BASE[3] + k) // 2 + 1)
                        act.activation(h_hi[:, k, :], t, ACT.Copy).then_inc(n_hi, 1)

            small_dmas(act, 0)
            act.dma_start(w2[:, 0, :], a["cmp_k_w2"][0]).then_inc(misc_loaded, 16)
            act.dma_start(w2[:, 1, :], a["cmp_v_w2"][0]).then_inc(misc_loaded, 16)
            act.dma_start(sinks[:, 0, :], a["attn_sinks_2"].to_broadcast([P, HEADS])).then_inc(misc_loaded, 16)
            act.dma_start(wg[:, :, :], k_tiles(w_in, 0, KD, 1280, 24)).then_inc(wg_loaded, 16)
            act.wait_ge(consts, 1)
            load_sqrt()
            for k in range(KD):
                square(0, k)
            root(0)
            for s in range(4):
                hi(s)
            norm_hi(0)
            act.wait_ge(small_ready, 1)
            act.activation(cond[:, :], col("c_2", 0, KD), ACT.Silu).then_inc(cond_ready, 1)
            act.activation(nq_bias[:, :], col("bq", 0, PAIRS), ACT.Copy, scale=-SCALE).then_inc(cond_ready, 1)
            act.wait_ge(lb_max, 1)
            act.activation(lower[:, 0:2, :], lower[:, 0:2, :], ACT.Exp).then_inc(lb_exp, 1)
            act.wait_ge(consts, 3)
            for h in range(HEADS):
                g, i = divmod(h, PAIRS)
                dst = cbias[:, g * 16:(g + 1) * 16, :].rearrange("p (t i) n -> p t i n", i=PAIRS)[:, :, i, :]
                act.activation(dst, cdist[:, :, :], ACT.Copy, scale=SLOPES[h]).then_inc(cbias_ready, 1)

            act.wait_ge(wg_loaded, 16)
            act.activation(wg_hi[:, :, :], wg[:, :, :], ACT.Copy).then_inc(wg_split_hi, 1)
            for s in range(S_CMP, S_U):
                hi(s + 4)
                if s < S_Q:
                    continue
                if s < S_K:
                    evac(s, qT[:, s - S_Q, :], scale=-SCALE)
                elif s < S_V:
                    evac(s, kT[:, s - S_K, :])
                else:
                    evac(s, sq[:, s - S_V, :])
            act.wait_ge(gate_done, 1)
            act.activation(hn[0:24, 0, :], ps[2][0:24, :], ACT.Sigmoid).then_inc(gate_ready, 1)
            for n in range(2):
                act.wait_ge(v_turned, n + 1)
                act.activation(vN[:, n, :, :].rearrange("p t n -> p (t n)"), ps[6 + n][:, :], ACT.Copy).then_inc(v_copied, 1)
            for s in range(S_U, S_MERGE):
                if s == S_U + 1:
                    act.wait_ge(gelu_parts, 1)
                    act.activation(hc[:, 1, :, :, 0:NCMP], hc[:, 1, :, :, 0:NCMP], ACT.Tanh).then_inc(gelu_done, 1)
                hi(s + 4)
                n = s - S_U
                if n % 4 >= 2:
                    j = n // 4 * 2 + n % 2
                    if j == 0:
                        act.wait_ge(sig_turned, 1)
                        act.wait_ge(hid_turned, 1)
                    if j >= 2:
                        act.wait_ge(freed["dve"], FREED[S_U + (n // 4 - 1) * 4 + n % 2][1])
                    act.wait_ge(tile_done, s + 1)
                    act.activation(sgt[j % 2], ps[BANK[s]][:, :], ACT.Sigmoid).then_inc(freed["act"], 1)
            for c in range(2):
                act.wait_ge(cx_ready, c + 1)
                x = cp[:, c * 16:(c + 1) * 16, 0:NCMP]
                act.activation(x, x, ACT.Exp, scale=-1.0).then_inc(cexp_done, 1)

            def head_bias(n):
                i, g, _ = ITEMS[n * QT]
                if n >= 2:
                    act.wait_ge(scores_ready, 2 * QT * (n - 1))
                act.activation(hbias[n % 2], dist[:, :], ACT.Copy, scale=SLOPES[i + 4 * g]).then_inc(hbias_ready, 1)

            head_bias(0)
            for j in range(NI + 2):
                if j < NI:
                    i, g, t = ITEMS[j]
                    if t == 0 and j // QT + 1 < HEADS:
                        head_bias(j // QT + 1)
                    L = (t + 1) * P
                    for b in range(2):
                        act.wait_ge(scores_ready, 2 * j + b + 1)
                        x = sc[:, j % 2, b, 0:L]
                        act.activation(x, x, ACT.Exp, scale=-1.0, bias=stat[:, 2 * (j % 2) + b:2 * (j % 2) + b + 1],
                                       accum_out=stat[:, 4 + 2 * (j % 2) + b:5 + 2 * (j % 2) + b]).then_inc(exp_done, 1)
                if 1 <= j <= NI:
                    m = j - 1
                    L = (ITEMS[m][2] + 1) * P
                    act.wait_ge(pc_turned, m + 1)
                    if m >= 2:
                        act.wait_ge(pv_done, m - 1)
                    act.activation(pcT[0:NCMP, m % 2, :], ps[3][0:NCMP, 0:P], ACT.Copy).then_inc(pc_copied, 1)
                    act.wait_ge(ps_turned, m + 1)
                    act.activation(pT[:, m % 2, 0, 0:L], ps[6][:, 0:L], ACT.Copy).then_inc(ps_copied, 1)
                if j < NI and j % 2 == 0:
                    hi(S_MERGE + j // 2 + 4)
                    if j >= 2:
                        s = S_MERGE + j // 2 - 1
                        evac(s, mg[:, s - S_MERGE, :])
                if j >= 2 and (j - 1) % (2 * QT) == 0:
                    i = (j - 1) // (2 * QT) - 1
                    act.wait_ge(pv_done, 2 * QT * (i + 1))
                    act.activation(qT[:, i, :], ps[2][:, :], ACT.Copy).then_inc(o_copied, 1)
                    act.wait_ge(o_copied, i + 1)
            evac(S_ATTN - 1, mg[:, 2 * KD - 1, :])

            for i in range(PAIRS):
                act.activation(att_hi[:, i, :], qT[:, i, :], ACT.Copy).then_inc(att_hi_done, 1)
            for c in range(2):
                x = mg[:, c * 4:(c + 1) * 4, :]
                act.wait_ge(freed["act"], FREED[S_MERGE + 4 * c + 3][1])
                act.activation(x, x, ACT.Sigmoid).then_inc(gate_sig, 1)
            load_sqrt()
            for c in range(CC):
                act.wait_ge(ln_centred, c + 1)
                if c >= 2:
                    act.wait_ge(ln_sqsum, c - 1)
                act.activation(sq[:, c % 2, :], acc[:, c, :], ACT.Square).then_inc(ln_sq, 1)
            hi(S_ATTN + 4)
            act.wait_ge(ln_sqsum, CC)
            act.activation(rstd[:, :], ps[5][:, :], ACT.Sqrt, scale=1.0 / CONV_CH, bias=eps_t[:, 0:1]).then_inc(ln_root, 1)
            for s in range(S_ATTN + 5, S_ATTN + 8):
                hi(s)
            for c in range(CC):
                act.wait_ge(ln_norm, c + 1)
                act.activation(acc[:, c, :], acc[:, c, :], ACT.Silu, scale=col("conv_ln_g", c),
                               bias=col("conv_ln_b", c)).then_inc(cv_ready, 1)
                act.wait_ge(cv_ready, c + 1)
                act.activation(cv_hi[:, c, :], acc[:, c, :], ACT.Copy).then_inc(cv_hi_done, 1)
                hi(S_CONV + c)
            for c in range(2, 4):
                x = mg[:, c * 4:(c + 1) * 4, :]
                act.wait_ge(freed["act"], FREED[S_MERGE + 4 * c + 3][1])
                act.activation(x, x, ACT.Sigmoid).then_inc(gate_sig, 1)
            for s in range(S_CONV, S_OUT):
                hi(s + 4)
                m = s - S_CONV
                act.wait_ge(merged, m + 1)
                act.activation(h_hi[:, m, :], mg[:, m, :], ACT.Copy).then_inc(m_hi, 1)

            for k in range(KD):
                if k == KD - 1:
                    load_sqrt()
                hi(S_OUT + k + 4)
                square(1, k)
            root(1)
            norm_hi(1)

            def ffn_act(s0, second):
                wname, bname = ("conv_w_2", "conv_b_2") if second else ("ffn_dw_w", "ffn_dw_b")
                wide = FT if second else 2 * FT
                done0 = FREED[s0][1]
                with act.Fori(0, FT // 2) as i:
                    act.activation(scratch[:, :], eps_t[:, :], ACT.Silu)
                    for j in range(4):
                        half, t = j // 2, j % 2
                        s = s0 + 4 + j
                        u = s // 2
                        act.wait_ge(raw_in[u % 2], i * 16 + RAW_COUNT[u])
                        act.wait_ge(tile_done, i * 4 + (s - 3))
                        part = raw[u % 2][:, :].rearrange("p (k n) -> p k n", k=KD)
                        act.activation(w_hi[s % 4][:, :, :], part[:, :, s % 2 * P:(s % 2 + 1) * P],
                                       ACT.Copy).then_inc(hi_done, 1)
                        if half == 0 or not second:
                            act.wait_ge(g_lo_done, i * 2 + (second * (FT + 2) + t + 1))
                            act.wait_ge(tile_done, i * 4 + (s0 + j + 1))
                            m = i * 2 + (half * FT + t)
                            act.activation((ua, uv)[half][:, t, :], ps[BANK[s0 + j]][:, :], ACT.Identity,
                                           scale=col(wname, m + 2 * wide), bias=col(bname, m)).then_inc(biased, 1)
                        if half == 1:
                            act.wait_ge(freed["dve"], i * 4 + (done0 + t))
                            act.activation(ua[:, t, :], ua[:, t, :], ACT.Silu).then_inc(silu_done, 1)
                    for t in range(2):
                        act.wait_ge(prod_done, i * 2 + (second * FT + t + 1))
                        act.activation(g_hi[:, bass.ds(i * 2 + t, 1), :].rearrange("p a n -> p (a n)"),
                                       uv[:, t, :], ACT.Copy).then_inc(g_hi_done, 1)

            def act_down(s0, norm):
                for n in range(25):
                    if n >= 5 and n % 6 in (5, 0):
                        k = (n - 5) // 6 * 2 + (n % 6 == 0)
                        square(norm, k)
                        if norm == 2:
                            act.wait_ge(g_lo_done, FT + 2)
                            if k >= 2:
                                act.wait_ge(summed2, k - 1)
                            act.activation(hn[:, k % 2, :], xT[:, k, :], ACT.Square,
                                           scale=col("final_g", k)).then_inc(squared2, 1)
                    if n == 23:
                        load_sqrt()
                    if n < 24:
                        hi(s0 + n + 4)

            ffn_act(S_UP, 0)
            act_down(S_DOWN, 2)

            act.wait_ge(mean_ready, 2)
            act.activation(rstd[:, :], rstd[:, :], ACT.Sqrt).then_inc(rooted, 1)
            act.activation(sq[:, 1, :], ps[7][:, :], ACT.Sqrt, scale=1.0 / D, bias=eps_t[:, 0:1]).then_inc(rooted, 1)
            norm_hi(3, lambda k: mod[:, k:k + 1])

            def stage_values(n, s, bias, c):
                act.wait_ge(x2_ready, KD)
                if n >= 2:
                    act.wait_ge(values_turned, n - 1)
                evac(s, sq[:, n % 2, :], ACT.Identity, bias=col(bias, c))

            for s in range(S_FH, S_GH):
                hi(s + 4)
                if s < S_QH:
                    evac(s, hf[:, s - S_FH, :], ACT.Sigmoid, bias=col("bfh", s - S_FH))
                elif s < S_IH:
                    evac(s, hq[:, s - S_QH, :], ACT.Silu, bias=col("bqh", s - S_QH))
                elif s < S_Q2:
                    stage_values(s - S_IH, s, "bih", s - S_IH)
                elif s < S_KV2:
                    evac(s, q2T[:, s - S_Q2, :], ACT.Identity, scale=-SCALE, bias=nq_bias[:, s - S_Q2:s - S_Q2 + 1])
                elif s == S_KV2:
                    evac(s, k2T[:, :], ACT.Identity, bias=col("bk"))
                else:
                    stage_values(HG, s, "bv", 0)
            for j in range(NI + 2):
                if j < NI:
                    i, g, t = ITEMS[j]
                    L = P if t == 0 else 2 * P
                    r = j % 2
                    act.wait_ge(s2_ready, j + 1)
                    act.activation(sc2[:, r, 0:L], sc2[:, r, 0:L], ACT.Exp, scale=-1.0, bias=stat[:, 18 + r:19 + r],
                                   accum_out=stat[:, 20 + r:21 + r]).then_inc(e2_done, 1)
                    h = i + 4 * g
                    act.activation(stat[:, 22 + r:23 + r], stat[:, 18 + r:19 + r], ACT.Exp,
                                   bias=sinks[:, 0, h:h + 1]).then_inc(e2_done, 1)
                if 1 <= j <= NI:
                    m = j - 1
                    L = P if ITEMS[m][2] == 0 else 2 * P
                    act.wait_ge(t2_done, m + 1)
                    if m >= 2:
                        act.wait_ge(pv2_done, m - 1)
                    act.activation(pT2[:, m % 2, 0:L], ps[6][:, 0:L], ACT.Copy).then_inc(t2_copied, 1)
                c = off_chunk_at(j - 1)
                if c is not None:
                    heads, _ = CHUNKS[c][1:]
                    act.wait_ge(chunk_done, c + 1)
                    bank = ps[CHUNK_BANK[c % 2]]
                    if CHUNKS[c][0] == 128:
                        dst = off[:, heads[0]:heads[0] + 2, 0:256]
                        src = bank[:, :].rearrange("p (h n) -> p h n", h=2)
                    else:
                        dst, src = off[:, heads[0], 256:768], bank[:, :]
                    act.activation(dst, src, ACT.Copy).then_inc(off_copied, 1)
                hd = av_at(j - 1)
                if hd is not None:
                    act.wait_ge(av_done, hd + 1)
                    act.activation(hq[:, hd, :], ps[CHUNK_BANK[hd % 2]][:, :], ACT.Copy).then_inc(av_copied, 1)
                    act.wait_ge(av_copied, hd + 1)
                    act.wait_ge(values_turned, HG + 1)
                    if hd >= 2:
                        act.wait_ge(r_sum, hd - 1)
                    act.activation(sq[:, hd % 2, :], hq[:, hd, :], ACT.Square).then_inc(r_sq, 1)
                n = gh_at(j)
                if n is not None:
                    hi(S_GH + n + 4)
                n = gh_at(j - 1)
                if n is not None:
                    act.wait_ge(q_scaled, len(ALL))
                    evac(S_GH + n, hgo[:, n, :], ACT.Identity, bias=col("bgh", n))
                if j >= 2 and (j - 1) % (2 * QT) == 0:
                    i = (j - 1) // (2 * QT) - 1
                    act.wait_ge(pv2_done, 2 * QT * (i + 1))
                    act.activation(q2T[:, i, :], ps[2][:, :], ACT.Copy).then_inc(o2_copied, 1)
                    if i < 2:
                        act.wait_ge(o2_copied, i + 1)
                        act.wait_ge(chunk_done, SUMMED_CHUNKS)
                        act.activation(hn[:, i, :], q2T[:, i, :], ACT.Square).then_inc(n2_sq, 1)
            act.wait_ge(r_sum, HG)
            for i in range(2, PAIRS):
                act.wait_ge(o2_copied, i + 1)
                act.activation(sq[:, i % 2, :], q2T[:, i, :], ACT.Square).then_inc(n2_sq, 1)
            load_sqrt()
            act.wait_ge(n2_sum, PAIRS)
            act.activation(rstd[:, :], ps[7][:, :], ACT.Sqrt, scale=1.0 / CONV_CH, bias=eps_t[:, 0:1]).then_inc(n2_root, 1)
            act.wait_ge(r_inv, 2 * HG)
            act.activation(kd[:, :, :], kd[:, :, :], ACT.Sqrt).then_inc(r_root, 1)
            act.wait_ge(freed["act"], FREED[S_GH + 3][1])
            act.activation(hgo[:, :, :], hgo[:, :, :], ACT.Silu).then_inc(gate2_silu, 1)
            for i in range(PAIRS):
                act.wait_ge(n2_norm, i + 1)
                act.activation(h_hi[:, i, :], q2T[:, i, :], ACT.Copy).then_inc(n2_hi, 1)
            for hd in range(HG):
                act.wait_ge(r_norm, hd + 1)
                act.activation(h_hi[:, PAIRS + hd, :], hq[:, hd, :], ACT.Copy).then_inc(r_hi, 1)
            for k in range(KD):
                if k == KD - 1:
                    load_sqrt()
                hi(S_OUT2 + k + 4)
                square(4, k)
            root(4)
            norm_hi(4, lambda k: mod[:, 3 * KD + k:3 * KD + k + 1])
            ffn_act(S_UP2, 1)
            act_down(S_DOWN2, 5)
            act.wait_ge(y_sum, 1)
            act.activation(stat[:, 0:QT], ps[7][:, 0:QT], ACT.Sqrt, scale=1.0 / D, bias=eps_t[:, 0:1]).then_inc(y_root, 1)
            act.wait_ge(y_inv, 1)
            act.wait_ge(y_turned, 1)
            for t in range(QT):
                act.activation(y_out[:, t, 0:512], ps[Y_BANK[0][t]][:, :], ACT.Copy,
                               scale=stat[:, QT + t:QT + t + 1]).then_inc(y_copied[0], 1)

        @block.vector
        def _(dve):
            chain = [0]

            def link(ins):
                chain[0] += 1
                ins.then_inc(dve_chain, 1)
                dve.wait_ge(dve_chain, chain[0])

            def norm(n, gain, shift=None, first=None):
                dve.wait_ge(rooted, ROOT[n])
                dve.reciprocal(rstd[:, :], rstd[:, :]).then_inc(inverted, 1)
                dve.wait_ge(inverted, ROOT[n])
                if first is not None:
                    first()
                b = HN_BASE[n]
                back = 2 if n == 3 else 4
                for k in range(KD + back // 2):
                    if k < KD:
                        if k >= back:
                            lo_ready(dve, n, k - back)
                        dve.scalar_tensor_tensor(out=normed_tile(n, k), in0=xT[:, k, :], scalar=gain(k), in1=rstd[:, :],
                                                 op0=ALU.mult, op1=ALU.mult).then_inc(normed, 1)
                    m = k - back // 2
                    if m >= 0 and m % 2 == 0:
                        dve.wait_ge(n_hi, b + m + 1)
                        if shift is None:
                            ins = dve.tensor_tensor(h_lo[:, m, :], normed_tile(n, m), h_hi[:, m, :].bitcast(F32),
                                                    ALU.subtract)
                        else:
                            ins = dve.scalar_tensor_tensor(out=h_lo[:, m, :], in0=normed_tile(n, m), scalar=shift(m),
                                                           in1=h_hi[:, m, :].bitcast(F32), op0=ALU.add,
                                                           op1=ALU.subtract)
                        ins.then_inc(n_lo[0], 1)

            for k in range(KD):
                dve.wait_ge(x_turned, k + 1)
                dve.tensor_copy(xT[:, k, :], ps[k % (KD - 1)][:, :]).then_inc(x_copied, 1)

            def take_small():
                dve.wait_ge(small_turned, 1)
                n = min(512, NSM * P)
                dve.tensor_copy(sm[:, 0:n], ps[4][:, 0:n])
                link(dve.tensor_copy(sm[:, n:NSM * P], ps[5][:, 0:NSM * P - n]))
                dve.sem_inc(small_ready, 1)

            norm(0, lambda k: col("norm1_g", k), first=take_small)

            l0, l1 = col("hgrn_lb_logits_2", 0, HG), col("hgrn_lb_logits_2", HG, HG)
            link(dve.tensor_tensor(lower[:, 2, :], l0, l1, ALU.max))
            dve.tensor_tensor(lower[:, 0, :], l0, lower[:, 2, :], ALU.subtract)
            dve.tensor_tensor(lower[:, 1, :], l1, lower[:, 2, :], ALU.subtract).then_inc(lb_max, 1)
            dve.wait_ge(misc_loaded, 48)
            dve.tensor_scalar(sinks[:, 1, :], sinks[:, 0, :], -1.0, None, ALU.mult).then_inc(cond_ready, 1)
            dve.wait_ge(lb_exp, 1)
            link(dve.tensor_tensor(lower[:, 2, :], lower[:, 0, :], lower[:, 1, :], ALU.add))
            link(dve.reciprocal(lower[:, 2, :], lower[:, 2, :]))
            link(dve.tensor_tensor(lower[:, 2, :], lower[:, 0, :], lower[:, 2, :], ALU.mult))
            dve.tensor_scalar(lower[:, 3, :], lower[:, 2, :], -1.0, 1.0, ALU.mult, ALU.add).then_inc(lb_ready, 1)

            dve.wait_ge(wg_split_hi, 1)
            dve.tensor_tensor(wg_lo[:, :, :], wg[:, :, :], wg_hi[:, :, :].bitcast(F32), ALU.subtract).then_inc(wg_split, 1)
            for n in range(2):
                dve.wait_ge(tile_done, n + 1)
                src = ps[BANK[n]]
                pe_v = col(("pe_k", "pe_v")[n], 0, CMP_BLOCK)
                for half in range(2):
                    b = blk[:, n, half * 16:(half + 1) * 16, :]
                    tok = src[:, half * 16:half * 16 + NCMP * CMP_STRIDE].rearrange("p (m i) -> p i m", i=CMP_STRIDE)
                    ins = dve.tensor_tensor(b, tok, pe_v[:, half * 16:(half + 1) * 16].unsqueeze(2)
                                            .to_broadcast([P, 16, NCMP]), ALU.add)
                ins.then_inc(freed["dve"], 1)
            dve.wait_ge(hid_done, 1)
            H = lambda n: hc[:, n, :, :, 0:NCMP]
            for g in range(2):
                dve.tensor_copy(hn[0:NCMP, 1, g * 256:(g + 1) * 256], ps[3 + g][0:NCMP, 0:256]).then_inc(hid_rows, 1)
            dve.wait_ge(sig_turned, 1)
            dve.tensor_copy(gates[:, :, :].rearrange("p t n -> p (t n)"), ps[2][:, 0:QT * 24]).then_inc(sig_ready, 1)
            dve.wait_ge(hid_turned, 1)
            link(dve.tensor_copy(H(0), ps[4][:, 0:128].rearrange("p (g n m) -> p n g m", n=2, g=2)[:, :, :, 0:NCMP]))
            link(dve.tensor_tensor(H(1), H(0), H(0), ALU.mult))
            link(dve.tensor_scalar(H(1), H(1), 0.044715 * GELU_C, GELU_C, ALU.mult, ALU.add))
            dve.tensor_tensor(H(1), H(1), H(0), ALU.mult).then_inc(gelu_parts, 1)

            def glu(n):
                s = S_U + n // 2 * 4 + n % 2
                dve.wait_ge(freed["act"], FREED[s + 2][1])
                dve.tensor_tensor(z[:, n, PAD:PAD + T], ps[BANK[s]][:, :], sgt[n % 2], ALU.mult).then_inc(freed["dve"], 1)

            dve.wait_ge(gelu_done, 1)
            link(dve.scalar_tensor_tensor(out=H(2), in0=H(1), scalar=1.0, in1=H(0), op0=ALU.add, op1=ALU.mult))
            dve.tensor_scalar(H(2), H(2), 0.5, None, ALU.mult).then_inc(hid_copied, 1)
            dve.wait_ge(cmp_kv_done, 1)
            dve.tensor_copy(kcT[:, 0:NCMP], ps[5][:, 0:NCMP])
            dve.tensor_copy(vcN[0:NCMP, :], ps[5][0:NCMP, 64:64 + P]).then_inc(cmp_kv_copied, 1)
            glu(0)
            glu(1)
            for g in range(2):
                x = cp[:, g * 16:(g + 1) * 16, 0:NCMP]
                dve.wait_ge(cqk_done, g + 1)
                dve.wait_ge(cbias_ready, HEADS)
                link(dve.tensor_tensor(x, ps[4 + g][:, :].rearrange("p (n m) -> p n m", m=32)[:, :, 0:NCMP],
                                       cbias[:, g * 16:(g + 1) * 16, 0:NCMP], ALU.add))
                low = stat[:, 32 + 16 * g:48 + 16 * g]
                link(dve.tensor_reduce(low, x, AX.X, ALU.min))
                dve.tensor_tensor(x, x, low.unsqueeze(2).to_broadcast([P, 16, NCMP]), ALU.subtract).then_inc(cx_ready, 1)
            glu(2)
            glu(3)

            def compressed_weights(g):
                x = cp[:, g * 16:(g + 1) * 16, 0:NCMP]
                low = stat[:, 32 + 16 * g:48 + 16 * g]
                dve.wait_ge(cexp_done, g + 1)
                link(dve.tensor_reduce(low, x, AX.X, ALU.add))
                link(dve.reciprocal(low, low))
                dve.wait_ge(sig_ready, 1)
                gc = gates[:, :, 12 * g:12 * g + 12].rearrange("p t (i c) -> p t i c", c=3)[:, :, :, 0]
                by_tile = low.rearrange("p (t i) -> p t i", t=QT)
                link(dve.tensor_tensor(by_tile, by_tile, gc, ALU.mult))
                link(dve.tensor_tensor(x, x, low.unsqueeze(2).to_broadcast([P, 16, NCMP]), ALU.mult))
                for t in range(QT):
                    xt = cp[:, g * 16 + t * 4:g * 16 + t * 4 + 4, 0:NCMP]
                    v = cvalid[:, t, 0:NCMP].unsqueeze(1).to_broadcast([P, 4, NCMP])
                    ins = dve.tensor_tensor(xt, xt, v, ALU.mult)
                ins.then_inc(cp_ready, 1)

            dve.wait_ge(freed["dve"], FREED[S_U + 5][1])

            def tap(n):
                c, m = n % CC, n // CC
                src = z[:, c, m:m + T]
                w = col("conv_dw_w", 4 * m + c)
                if m == 0:
                    ins = dve.tensor_scalar(acc[:, c, :], src, w, col("conv_dw_b", c), ALU.mult, ALU.add)
                else:
                    dve.wait_ge(tap_done, n - CC + 1)
                    ins = dve.scalar_tensor_tensor(out=acc[:, c, :], in0=src, scalar=w, in1=acc[:, c, :],
                                                   op0=ALU.mult, op1=ALU.add)
                ins.then_inc(tap_done, 1)

            for j in range(NI + 1):
                if j < NI:
                    i, g, t = ITEMS[j]
                    L = (t + 1) * P
                    hn_ = j // QT
                    for b in range(2):
                        if b == 0 and t == 0:
                            dve.wait_ge(hbias_ready, hn_ + 1)
                        dve.wait_ge(qk_done, 2 * j + b + 1)
                        if j >= 2:
                            dve.wait_ge((ps_turned, pw_turned)[b], j - 1)
                        q = 2 * (j % 2) + b
                        dve.tensor_tensor_reduce(out=sc[:, j % 2, b, 0:L], in0=ps[4 + b][:, 0:L],
                                                 in1=hbias[hn_ % 2][:, (QT - 1 - t) * P:T], scale=1.0, scalar=3.0e38,
                                                 op0=ALU.add, op1=ALU.min, accum_out=stat[:, q:q + 1])\
                           .then_inc(scores_ready, 1)
                if j < 2:
                    compressed_weights(j)
                for n in range(max(0, 4 * j - 4), min(max(0, 4 * j - 2), CC * CONV_W)):
                    tap(n)
                if j >= 1:
                    m = j - 1
                    L2 = (ITEMS[m][2] + 1) * P
                    dve.wait_ge(pw_turned, m + 1)
                    if m >= 2:
                        dve.wait_ge(pv_done, m - 1)
                    dve.tensor_copy(pT[:, m % 2, 1, 0:L2], ps[7][:, 0:L2]).then_inc(pw_copied, 1)
                for n in range(max(0, 4 * j - 2), min(4 * j, CC * CONV_W)):
                    tap(n)
                if j < NI:
                    q = 2 * (j % 2)
                    dve.wait_ge(exp_done, 2 * j + 2)
                    link(dve.reciprocal(stat[:, 8 + q:10 + q], stat[:, 4 + q:6 + q]))
                    h = i + 4 * g
                    link(dve.tensor_tensor(stat[:, 8 + q:10 + q], stat[:, 8 + q:10 + q],
                                           gates[:, t, 3 * h + 1:3 * h + 3], ALU.mult))
                    for b in range(2):
                        x = sc[:, j % 2, b, 0:L]
                        ins = dve.tensor_scalar(x, x, stat[:, 8 + q + b:9 + q + b], None, ALU.mult)
                    ins.then_inc(p_ready, 1)

            for i in range(PAIRS):
                dve.wait_ge(att_hi_done, i + 1)
                dve.tensor_tensor(att_lo[:, i, :], qT[:, i, :], att_hi[:, i, :].bitcast(F32),
                                  ALU.subtract).then_inc(att_lo_done, 1)
            dve.wait_ge(ln_sum, 1)
            for c in range(CC):
                dve.scalar_tensor_tensor(out=acc[:, c, :], in0=ps[4][:, :], scalar=-1.0 / CONV_CH, in1=acc[:, c, :],
                                         op0=ALU.mult, op1=ALU.add).then_inc(ln_centred, 1)

            def gated_attention(m):
                s = S_ATTN + m
                dve.wait_ge(gate_sig, m // 4 + 1)
                dve.wait_ge(tile_done, s + 1)
                dve.tensor_tensor(mg[:, m, :], ps[BANK[s]][:, :], mg[:, m, :], ALU.mult).then_inc(freed["dve"], 1)

            gated_attention(0)
            gated_attention(1)
            dve.wait_ge(ln_root, 1)
            link(dve.reciprocal(rstd[:, :], rstd[:, :]))
            gated_attention(2)
            gated_attention(3)
            for c in range(CC):
                dve.tensor_tensor(acc[:, c, :], acc[:, c, :], rstd[:, :], ALU.mult).then_inc(ln_norm, 1)
            for c in range(CC):
                dve.wait_ge(cv_hi_done, c + 1)
                dve.tensor_tensor(cv_lo[:, c, :], acc[:, c, :], cv_hi[:, c, :].bitcast(F32),
                                  ALU.subtract).then_inc(cv_lo_done, 1)
                gated_attention(4 + c)
            for m in range(KD + 1):
                if m < KD:
                    s = S_CONV + m
                    dve.wait_ge(gate_sig, 3 + m // 4)
                    dve.wait_ge(tile_done, s + 1)
                    dve.tensor_tensor(mg[:, KD + m, :], ps[BANK[s]][:, :], mg[:, KD + m, :], ALU.mult)\
                       .then_inc(freed["dve"], 1)
                    dve.wait_ge(freed["dve"], FREED[s][1])
                    dve.tensor_tensor(mg[:, m, :], mg[:, m, :], mg[:, KD + m, :], ALU.add).then_inc(merged, 1)
                if m:
                    dve.wait_ge(m_hi, m)
                    dve.tensor_tensor(h_lo[:, m - 1, :], mg[:, m - 1, :], h_hi[:, m - 1, :].bitcast(F32),
                                      ALU.subtract).then_inc(m_lo, 1)

            def ada_reduce(n, loaded, i=None):
                buf = n % 2
                count = lambda v: v if i is None else i * 2 + v
                dve.wait_ge(ada_in[buf], loaded)
                dve.tensor_tensor(ada[buf][:, :, :], ada[buf][:, :, :],
                                  cond[:, :].unsqueeze(2).to_broadcast([P, KD, P]), ALU.mult).then_inc(ada_scaled, 1)
                dve.wait_ge(ada_scaled, count(n + 1))
                if n >= 2:
                    dve.wait_ge(ada_done, count(n - 1))
                dve.tensor_reduce(ada_sum[buf][:, :], ada[buf][:, :, :].rearrange("p k n -> p n k"), AX.X,
                                  ALU.add).then_inc(ada_summed, 1)

            dve.wait_ge(cond_ready, 1)
            for k in range(KD):
                s = S_OUT + k
                dve.wait_ge(tile_done, s + 1)
                dve.tensor_tensor(xT[:, k, :], ps[BANK[s]][:, :], xT[:, k, :], ALU.add).then_inc(freed["dve"], 1)
                if k < ADA_EARLY:
                    ada_reduce(k, 16 * (k // 2 + 1))
            norm(1, lambda k: col("norm2_g", k))

            def ffn_dve(s0, second):
                wname = "conv_w_2" if second else "ffn_dw_w"
                wide = FT if second else 2 * FT
                per = 2 if second else 4
                dve.sem_inc(g_lo_done, 2)
                with dve.Fori(0, FT // 2) as i:
                    for j in range(4):
                        half, t = j // 2, j % 2
                        src = ps[BANK[s0 + j]]
                        if half and second:
                            dve.wait_ge(silu_done, i * 2 + (FT + t + 1))
                            dve.wait_ge(tile_done, i * 4 + (s0 + j + 1))
                            dve.tensor_tensor(uv[:, t, :], src[:, :], ua[:, t, :], ALU.mult).then_inc(freed["dve"], 1)
                            continue
                        u = (ua, uv)[half]
                        n = i * per + (second * 2 * FT + j + 1)
                        m = i * 2 + (half * FT + t)
                        dve.wait_ge(biased, n)
                        dve.scalar_tensor_tensor(out=u[:, t, 1:T], in0=src[:, 0:T - 1], scalar=col(wname, m + wide),
                                                 in1=u[:, t, 1:T], op0=ALU.mult, op1=ALU.add).then_inc(tap1_done, 1)
                        dve.wait_ge(tap1_done, n)
                        dve.scalar_tensor_tensor(out=u[:, t, 2:T], in0=src[:, 0:T - 2], scalar=col(wname, m),
                                                 in1=u[:, t, 2:T], op0=ALU.mult, op1=ALU.add).then_inc(freed["dve"], 1)
                        if j == 1 and not second:
                            ada_reduce(ADA_EARLY, i * 16 + 16 * (ADA_EARLY // 2 + 1), i)
                    for t in range(2):
                        if second:
                            dve.wait_ge(freed["dve"], i * 4 + (FREED[s0][1] + 2 + t))
                            dve.sem_inc(prod_done, 1)
                        else:
                            dve.wait_ge(silu_done, i * 2 + (t + 1))
                            dve.wait_ge(freed["dve"], i * 4 + (FREED[s0][1] + 2 + t))
                            dve.tensor_tensor(uv[:, t, :], uv[:, t, :], ua[:, t, :], ALU.mult).then_inc(prod_done, 1)
                    for t in range(2):
                        k = i * 2 + t
                        dve.wait_ge(g_hi_done, i * 2 + (second * FT + t + 1))
                        dve.tensor_tensor(g_lo[:, bass.ds(k, 1), :].rearrange("p a n -> p (a n)"), uv[:, t, :],
                                          g_hi[:, bass.ds(k, 1), :].rearrange("p a n -> p (a n)").bitcast(F32),
                                          ALU.subtract).then_inc(g_lo_done, 1)
                    if not second:
                        ada_reduce(ADA_EARLY + 1, i * 16 + 16 * (ADA_EARLY // 2 + 1), i)

            ffn_dve(S_UP, 0)
            for n in range(24):
                if n % 6 >= 4:
                    k = n // 6 * 2 + n % 2
                    dve.wait_ge(tile_done, S_DOWN + n + 1)
                    dve.tensor_tensor(xT[:, k, :], ps[BANK[S_DOWN + n]][:, :], xT[:, k, :],
                                      ALU.add).then_inc(freed["dve"], 1)
                m = ADA_EARLY + ADA_UP + n
                if m < NMOD * KD:
                    ada_reduce(m, 16 * (m // 2 + 1))
            dve.wait_ge(ada_done, NMOD * KD)
            link(dve.tensor_tensor(mod[:, :], ps[6][:, 0:NMOD * KD], col("ada_b_2", 0, NMOD * KD), ALU.add))
            for n, (name, c) in enumerate((("mix_norm_g_2", KD), ("ffn_norm_g_2", 4 * KD))):
                link(dve.tensor_scalar(gain2[:, n, :], mod[:, c:c + KD], 1.0, None, ALU.add))
                link(dve.tensor_tensor(gain2[:, n, :], gain2[:, n, :], col(name, 0, KD), ALU.mult))
            link(dve.tensor_tensor(gain2[:, 0, :], gain2[:, 0, :], col("final_g", 0, KD), ALU.mult))
            dve.wait_ge(summed, SQ_BASE[2] + KD)
            dve.tensor_scalar(sq[:, 0, :], ps[7][:, :], EPS / D, EPS * EPS, ALU.mult, ALU.add).then_inc(mean_ready, 1)
            dve.wait_ge(summed2, KD)
            dve.wait_ge(mean_ready, 1)
            dve.scalar_tensor_tensor(out=rstd[:, :], in0=ps[5][:, :], scalar=1.0 / D, in1=sq[:, 0, :],
                                     op0=ALU.mult, op1=ALU.add).then_inc(mean_ready, 1)
            norm(3, lambda k: gain2[:, 0, k:k + 1], lambda k: mod[:, k:k + 1])
            dve.wait_ge(rooted, ROOT[2])
            dve.reciprocal(sq[:, 1, :], sq[:, 1, :]).then_inc(inverted, 1)
            dve.wait_ge(inverted, ROOT[2])
            for k in range(KD):
                dve.scalar_tensor_tensor(out=xT[:, k, :], in0=xT[:, k, :], scalar=col("final_g", k), in1=sq[:, 1, :],
                                         op0=ALU.mult, op1=ALU.mult).then_inc(x2_ready, 1)

            for h in range(HG):
                dve.wait_ge(freed["act"], FREED[S_FH + h][1])
                dve.tensor_scalar(hf[:, h, :], hf[:, h, :], lower[:, 3, h:h + 1], lower[:, 2, h:h + 1],
                                  ALU.mult, ALU.add).then_inc(f_ready, 1)
                dve.wait_ge(f_ready, 2 * h + 1)
                dve.tensor_scalar(hk[:, h, :], hf[:, h, :], -1.0, 1.0, ALU.mult, ALU.add).then_inc(f_ready, 1)

            def take_values(n, dst):
                dve.wait_ge(values_turned, n + 1)
                dve.tensor_copy(dst, ps[V_BANK[n]][:, :].rearrange("p (t n) -> p t n", t=QT)).then_inc(values_copied, 1)

            for h in range(HG - 1):
                take_values(h, iN[:, :, h * P:(h + 1) * P])
            dve.wait_ge(freed["act"], FREED[S_QH + 3][1])

            def scale_queries(n):
                b = ALL[n]
                if n >= 2:
                    dve.wait_ge(lvl_done, n - 1)
                dst = qd[n % 2][:, :, :].rearrange("p h t -> p (h t)").rearrange("p (m c) -> p m c", c=b)
                dve.tensor_tensor(dst, pairs_of(hq, b)[:, :, 1, :], pairs_of(hf, b)[:, :, 1, :],
                                  ALU.mult).then_inc(q_scaled, 1)

            def merge_decays(n):
                b = ALL[n]
                dve.wait_ge(g_merged, n + 1)
                f = pairs_of(hf, b)
                dve.tensor_tensor(f[:, :, 1, :], f[:, :, 1, :],
                                  f[:, :, 0, b - 1:b].to_broadcast([P, HG * T // (2 * b), b]),
                                  ALU.mult).then_inc(f_merged, 1)
                dve.wait_ge(f_merged, n + 1)

            def multiply(c):
                kind, heads, n = CHUNKS[c]
                if c >= 2:
                    dve.wait_ge(chunk_done, c - 1)
                out = hn[:, c % 2, :]
                if n is None:
                    ins = dve.tensor_tensor(out, hq[:, heads[0], :], hk[:, heads[0], :], ALU.mult)
                else:
                    keys = hk[:, heads[0]:heads[0] + 2, :].rearrange("p h (m e) -> p h m e", e=2)[:, :, :, 0]
                    ins = dve.tensor_tensor(out.rearrange("p (h m) -> p h m", h=2),
                                            qd[0][:, heads[0]:heads[0] + 2, :], keys, ALU.mult)
                ins.then_inc(multiplied, 1)

            def take_scores(c):
                kind, heads, n = CHUNKS[c]
                if n is not None and kind > 64:
                    return
                dve.wait_ge(chunk_done, c + 1)
                if n is None:
                    in_tiles = lambda x: x.rearrange("p (t n) -> p t n", t=QT)
                    dve.copy_predicated(in_tiles(hs[:, heads[0], :]), eye8[:, :].unsqueeze(1).to_broadcast([P, QT, P]),
                                        in_tiles(ps[CHUNK_BANK[c % 2]][:, :])).then_inc(sel_done, 1)
                else:
                    half = HG * T // (2 * kind) // 2
                    m0 = half * (heads[0] // 2)
                    by_tile = lambda x: x.rearrange("p (r m) c -> p r m c", m=DH // kind)
                    sel = mask[:, n, :].rearrange("p (m c) -> p m c", c=kind).unsqueeze(1)
                    dve.copy_predicated(by_tile(pairs_of(hs, kind)[:, m0:m0 + half, 1, :]),
                                        sel.to_broadcast([P, T // DH, DH // kind, kind]),
                                        by_tile(ps[CHUNK_BANK[c % 2]][:, :].rearrange("p (m c) -> p m c", c=kind)))\
                       .then_inc(sel_done, 1)

            def hgrn_step(c):
                take_scores(c)
                if c + 2 < SUMMED_CHUNKS:
                    multiply(c + 2)
                n = CHUNKS[c][2]
                if n is not None and n != CHUNKS[c - 1][2] and n + 1 < len(ALL):
                    merge_decays(n)
                    scale_queries(n + 1)

            dve.wait_ge(n_lo[0], (HN_BASE[3] + KD) // 2)
            dve.wait_ge(n_lo[1], (HN_BASE[3] + KD) // 2)
            multiply(0)
            multiply(1)
            scale_queries(0)
            dve.wait_ge(q_scaled, 1)
            dve.wait_ge(setup2, 1)
            for s in range(S_Q2, S_GH):
                if s == S_Q2:
                    take_values(HG - 1, iN[:, :, (HG - 1) * P:HG * P])
                hgrn_step(s - S_Q2)
            take_values(HG, v2N[:, :, :])
            for j in range(NI + 2):
                if j < NI:
                    i, g, t = ITEMS[j]
                    h = i + 4 * g
                    L = P if t == 0 else 2 * P
                    r = j % 2
                    dve.wait_ge(qk2_done, j + 1)
                    if j >= 2:
                        dve.wait_ge(t2_done, j - 1)
                    if j == 0:
                        dve.wait_ge(cond_ready, 3)
                    link(dve.tensor_tensor_reduce(out=sc2[:, r, 0:L], in0=ps[4 + r][:, 0:L], in1=dist2[:, 2 * P - L:],
                                                  scale=1.0, scalar=3.0e38, op0=ALU.add, op1=ALU.min,
                                                  accum_out=stat[:, 16 + r:17 + r]))
                    dve.tensor_scalar(stat[:, 18 + r:19 + r], stat[:, 16 + r:17 + r], sinks[:, 1, h:h + 1], None,
                                      ALU.min).then_inc(s2_ready, 1)
                c = chunk_at(j)
                if c is not None:
                    hgrn_step(c)
                if j < NI:
                    dve.wait_ge(e2_done, 2 * j + 2)
                    link(dve.tensor_tensor(stat[:, 24 + r:25 + r], stat[:, 20 + r:21 + r], stat[:, 22 + r:23 + r], ALU.add))
                    link(dve.reciprocal(stat[:, 24 + r:25 + r], stat[:, 24 + r:25 + r]))
                    dve.tensor_scalar(sc2[:, r, 0:L], sc2[:, r, 0:L], stat[:, 24 + r:25 + r], None,
                                      ALU.mult).then_inc(p2_ready, 1)
                hd = av_at(j - 3)
                if hd is not None:
                    dve.wait_ge(r_sum, hd + 1)
                    dve.tensor_scalar(kd[:, hd, :], ps[R_BANK][:, :], 1.0 / P, EPS, ALU.mult,
                                      ALU.add).then_inc(r_var, 1)
                    dve.wait_ge(r_var, hd + 1)
                    dve.reciprocal(kd[:, hd, 0:256], kd[:, hd, 0:256]).then_inc(r_inv, 1)
                hd = av_at(j - 4)
                if hd is not None:
                    dve.reciprocal(kd[:, hd, 256:T], kd[:, hd, 256:T]).then_inc(r_inv, 1)
            dve.wait_ge(n2_root, 1)
            link(dve.reciprocal(rstd[:, :], rstd[:, :]))
            for i in range(PAIRS + 1):
                if i < PAIRS:
                    dve.scalar_tensor_tensor(out=q2T[:, i, :], in0=q2T[:, i, :], scalar=col("attn_out_g_2", i),
                                             in1=rstd[:, :], op0=ALU.mult, op1=ALU.mult).then_inc(n2_norm, 1)
                if i:
                    dve.wait_ge(n2_hi, i)
                    dve.tensor_tensor(h_lo[:, i - 1, :], q2T[:, i - 1, :], h_hi[:, i - 1, :].bitcast(F32),
                                      ALU.subtract).then_inc(n2_lo, 1)
            dve.wait_ge(gate2_silu, 1)
            for hd in range(HG):
                dve.wait_ge(r_scaled, hd + 1)
                dve.scalar_tensor_tensor(out=hq[:, hd, :], in0=hq[:, hd, :], scalar=col("hgrn_out_g_2", hd),
                                         in1=hgo[:, hd, :], op0=ALU.mult, op1=ALU.mult).then_inc(r_norm, 1)
            for hd in range(2, HG):
                dve.wait_ge(r_hi, hd + 1)
                dve.tensor_tensor(h_lo[:, PAIRS + hd, :], hq[:, hd, :], h_hi[:, PAIRS + hd, :].bitcast(F32),
                                  ALU.subtract).then_inc(r_lo[1], 1)

            def gated_residual(s, k, gate):
                dve.wait_ge(tile_done, s + 1)
                dve.scalar_tensor_tensor(out=xT[:, k, :], in0=ps[BANK[s]][:, :], scalar=mod[:, gate * KD + k:gate * KD + k + 1],
                                         in1=xT[:, k, :], op0=ALU.mult, op1=ALU.add).then_inc(freed["dve"], 1)

            dve.wait_ge(x2_ready, KD)
            for k in range(KD):
                gated_residual(S_OUT2 + k, k, 2)
            norm(4, lambda k: gain2[:, 1, k:k + 1], lambda k: mod[:, 3 * KD + k:3 * KD + k + 1])
            ffn_dve(S_UP2, 1)
            for k in range(KD):
                gated_residual(S_DOWN2 + k // 2 * 6 + 4 + k % 2, k, 5)
                dve.wait_ge(squared, SQ_BASE[5] + k + 1)
                if k:
                    if k >= 2:
                        dve.wait_ge(squares_added, k - 1)
                    dve.tensor_tensor(hn[:, 0, :], sq[:, 0, :] if k == 1 else hn[:, 0, :], sq[:, k % 2, :],
                                      ALU.add).then_inc(squares_added, 1)
                dve.wait_ge(freed["dve"], FREED[S_DOWN2 + k // 2 * 6 + 4 + k % 2][1])
                dve.tensor_scalar(xT[:, k, :], xT[:, k, :], col("final_norm_g_2", k), None, ALU.mult).then_inc(y_ready, 1)
            dve.wait_ge(y_root, 1)
            dve.reciprocal(stat[:, QT:2 * QT], stat[:, 0:QT]).then_inc(y_inv, 1)
            dve.wait_ge(y_inv, 1)
            for t in range(QT):
                dve.wait_ge(y_turned, 2 + t)
                dve.tensor_scalar(y_out[:, t, 512:D], ps[Y_BANK[1][t]][:, :], stat[:, QT + t:QT + t + 1], None,
                                  ALU.mult).then_inc(y_copied[1], 1)

        @block.tensor
        def _(pe):
            def split_product(out_ap, w, wl, x, xl, first, last):
                pe.matmul(out_ap, w, x, start=first, stop=False)
                pe.matmul(out_ap, w, xl, start=False, stop=False)
                return pe.matmul(out_ap, wl, x, start=False, stop=last)

            def tile(s, x, xl, k0=0, first=True, last=True, part=(0, None), ready=None, signal=True):
                nk = DEPTH_OF[s]
                lo_k, hi_k = part[0], nk if part[1] is None else part[1]
                if lo_k == 0:
                    pe.wait_ge(lo_done, s + 1)
                    if first:
                        wait_bank(pe, s)
                for k in range(lo_k, hi_k):
                    if ready is not None:
                        ready(k0 + k)
                    ins = split_product(ps[BANK[s]][:, :], w_hi[s % 4][:, k, :], w_lo[s % 4][:, k, :],
                                        x[:, k0 + k, :], xl[:, k0 + k, :], first and k == 0, last and k == nk - 1)
                if hi_k == nk and signal:
                    ins.then_inc(tile_done, 1)

            def keep_warm(bank, n):
                for _ in range(n):
                    pe.matmul(ps[bank][:, 0:P], ones[:, :], ident[:, :], start=True, stop=True)

            def norm_sum(n, k):
                pe.wait_ge(squared, SQ_BASE[n] + k + 1)
                pe.matmul(ps[7][:, :], ones[:, :], sq[:, k % 2, :], start=k == 0, stop=k == KD - 1).then_inc(summed, 1)

                if n == 2:
                    pe.wait_ge(squared2, k + 1)
                    pe.matmul(ps[5][:, :], ones[:, :], hn[:, k % 2, :], start=k == 0, stop=k == KD - 1).then_inc(summed2, 1)

            def parts(sem, base=0):
                return lambda k: pe.wait_ge(sem, base + k + 1)

            def normed_parts(norm):
                return lambda k: lo_ready(pe, norm, k)

            pe.wait_ge(consts, 1)
            for t in range(QT):
                pe.wait_ge(x_loaded[t], 16)
                for k in range(KD - 1):
                    ins = pe.transpose(ps[k][:, t * P:(t + 1) * P], x_in[:, t, k * P:(k + 1) * P], ident[:, :])
                    if t == QT - 1:
                        ins.then_inc(x_turned, 1)
            pe.wait_ge(x_copied, 1)
            for t in range(QT):
                ins = pe.transpose(ps[0][:, t * P:(t + 1) * P], x_in[:, t, (KD - 1) * P:D], ident[:, :])
            ins.then_inc(x_turned, 1)
            keep_warm(7, 9)
            for k in range(KD):
                norm_sum(0, k)
            for which in range(2):
                pe.wait_ge(small_loaded[which], small_total[which])
            for m in range(NSM):
                ins = pe.transpose(ps[4 + m // 4][:, m % 4 * P:(m % 4 + 1) * P], rows[:, m, :], ident[:, :])
            ins.then_inc(small_turned, 1)
            keep_warm(6, 22)
            pe.wait_ge(x_copied, KD)
            for s in range(S_CMP, S_V):
                tile(s, h_hi, h_lo, ready=normed_parts(0) if s == 0 else None)
            for s in range(S_V, S_U):
                tile(s, h_hi, h_lo)
            pe.wait_ge(wg_split, 1)
            for k in range(KD):
                ins = split_product(ps[2][0:24, :], wg_hi[:, k, :], wg_lo[:, k, :], h_hi[:, k, :], h_lo[:, k, :],
                                    k == 0, k == KD - 1)
            ins.then_inc(gate_done, 1)
            for n in range(2):
                pe.wait_ge(freed["act"], FREED[S_V + n][1])
                for t in range(QT):
                    ins = pe.transpose(ps[6 + n][:, t * P:(t + 1) * P], sq[:, n, t * P:(t + 1) * P], ident[:, :])
                ins.then_inc(v_turned, 1)
            pe.wait_ge(w1_loaded, 64)
            pe.wait_ge(freed["dve"], FREED[1][1])
            for g in range(2):
                for n in range(2):
                    for m in range(CMP_BLOCK):
                        ins = pe.matmul(ps[3 + g][0:NCMP, n * P:(n + 1) * P], blk[g * DH:(g + 1) * DH, n, m, :],
                                        w1[n][g * DH:(g + 1) * DH, m, :], start=m == 0, stop=m == CMP_BLOCK - 1)
            ins.then_inc(hid_done, 1)
            pe.wait_ge(gate_ready, 1)
            for t in range(QT):
                ins = pe.transpose(ps[2][:, t * 24:(t + 1) * 24], hn[0:24, 0, t * P:(t + 1) * P], ident[0:24, 0:24])
            ins.then_inc(sig_turned, 1)
            for s in range(S_U, S_MERGE):
                if s == S_U + 2:
                    pe.wait_ge(v_copied, 2)
                tile(s, h_hi, h_lo)
                if s == S_U:
                    pe.wait_ge(hid_rows, 2)
                    for m in range(4):
                        ins = pe.transpose(ps[4][:, m * 32:m * 32 + NCMP], hn[0:NCMP, 1, m * P:(m + 1) * P],
                                           ident[0:NCMP, 0:NCMP])
                    ins.then_inc(hid_turned, 1)
                if s == S_U + 1:
                    pe.wait_ge(hid_copied, 1)
                    pe.wait_ge(misc_loaded, 48)
                    for g in range(2):
                        pe.matmul(ps[5][g * DH:(g + 1) * DH, 0:NCMP], w2[:, 0, :], hc[:, 2, 0, g, 0:NCMP],
                                  start=True, stop=True)
                    for g in range(2):
                        ins = pe.matmul(ps[5][0:NCMP, 64 + g * DH:64 + (g + 1) * DH], hc[:, 2, 1, g, 0:NCMP],
                                        w2[:, 1, :], start=True, stop=True)
                    ins.then_inc(cmp_kv_done, 1)
                if s == S_U + 3:
                    pe.wait_ge(cmp_kv_copied, 1)
                    pe.wait_ge(freed["act"], FREED[S_U - 1][1])
                    for g in range(2):
                        for t in range(QT):
                            for i in range(PAIRS):
                                n = (t * PAIRS + i) * 32
                                ins = pe.matmul(ps[4 + g][:, n:n + NCMP], qT[g * DH:(g + 1) * DH, i, t * P:(t + 1) * P],
                                                kcT[g * DH:(g + 1) * DH, 0:NCMP], start=True, stop=True)
                        ins.then_inc(cqk_done, 1)
            tile(S_MERGE, h_hi, h_lo, part=(0, 4))
            pe.wait_ge(cx_ready, 2)
            pe.wait_ge(sig_ready, 1)
            pe.wait_ge(freed["act"], FREED[S_MERGE - 1][1])
            for j in range(NI + 2):
                if j < NI:
                    i, g, t = ITEMS[j]
                    L = (t + 1) * P
                    grp = slice(g * DH, (g + 1) * DH)
                    for b in range(2):
                        if j:
                            pe.wait_ge(scores_ready, 2 * j + b - 1)
                        pe.matmul(ps[4 + b][:, 0:L], qT[grp, i, t * P:(t + 1) * P], kT[grp, b, 0:L],
                                  start=True, stop=True).then_inc(qk_done, 1)
                    if j:
                        tile(S_MERGE + j // 2, h_hi, h_lo, part=(4 * (j % 2), 4 * (j % 2) + 4))
                if 1 <= j <= NI:
                    m = j - 1
                    i, g, t = ITEMS[m]
                    pe.wait_ge(p_ready, m + 1)
                    pe.wait_ge(cp_ready, g + 1)
                    if m:
                        pe.wait_ge(pc_copied, m)
                    pe.transpose(ps[3][0:NCMP, 0:P], cp[:, g * 16 + t * 4 + i, 0:NCMP], ident[:, :]).then_inc(pc_turned, 1)
                    for b in range(2):
                        if m:
                            pe.wait_ge((ps_copied, pw_copied)[b], m)
                        for kt in range(t + 1):
                            ins = pe.transpose(ps[6 + b][:, kt * P:(kt + 1) * P], sc[:, m % 2, b, kt * P:(kt + 1) * P],
                                               ident[:, :])
                        ins.then_inc((ps_turned, pw_turned)[b], 1)
                if j >= 2:
                    m = j - 2
                    i, g, t = ITEMS[m]
                    pe.wait_ge(pc_copied, m + 1)
                    pe.wait_ge(ps_copied, m + 1)
                    pe.wait_ge(pw_copied, m + 1)
                    if m and m % (2 * QT) == 0:
                        pe.wait_ge(o_copied, m // (2 * QT))
                    o = ps[2][g * DH:(g + 1) * DH, t * P:(t + 1) * P]
                    for b in range(2):
                        for kt in range(t + 1):
                            pe.matmul(o, vN[:, b, kt, g * DH:(g + 1) * DH], pT[:, m % 2, b, kt * P:(kt + 1) * P],
                                      start=b == 0 and kt == 0, stop=False)
                    pe.matmul(o, vcN[0:NCMP, g * DH:(g + 1) * DH], pcT[0:NCMP, m % 2, :],
                              start=False, stop=True).then_inc(pv_done, 1)
            pe.wait_ge(tap_done, CC * CONV_W)
            for c in range(CC):
                ins = pe.matmul(ps[4][:, :], ones[:, :], acc[:, c, :], start=c == 0, stop=c == CC - 1)
            ins.then_inc(ln_sum, 1)
            tile(S_ATTN, att_hi, att_lo, ready=parts(att_lo_done))
            for c in range(CC):
                pe.wait_ge(ln_sq, c + 1)
                pe.matmul(ps[5][:, :], ones[:, :], sq[:, c % 2, :], start=c == 0, stop=c == CC - 1).then_inc(ln_sqsum, 1)
            for s in range(S_ATTN + 1, S_CONV):
                tile(s, att_hi, att_lo)
            for s in range(S_CONV, S_OUT):
                tile(s, cv_hi, cv_lo, ready=parts(cv_lo_done) if s == S_CONV else None)

            def ada_tile(n, buf, count):
                pe.wait_ge(ada_summed, count)
                pe.matmul(ps[6][:, bass.ds(n, 1)] if not isinstance(n, int) else ps[6][:, n:n + 1],
                          ada_sum[buf][:, :], ones[:, 0:1], start=True, stop=True).then_inc(ada_done, 1)

            for s in range(S_OUT, S_UP):
                tile(s, h_hi, h_lo, ready=parts(m_lo) if s == S_OUT else None)
                if s > S_OUT:
                    norm_sum(1, s - S_OUT - 1)
                n = s - S_OUT - 2
                if 0 <= n < ADA_EARLY - 1:
                    ada_tile(n, n % 2, n + 1)
            norm_sum(1, KD - 1)
            keep_warm(4, 22)

            def ffn_pe(s0, norm):
                with pe.Fori(0, FT // 2) as i:
                    for j in range(4):
                        s = s0 + j
                        pe.wait_ge(lo_done, i * 4 + (s + 1))
                        pe.wait_ge(freed["dve"], i * 4 + (FREED[s][1] - 4))
                        for k in range(KD):
                            if j == 0:
                                lo_ready(pe, norm, k)
                            ins = split_product(ps[BANK[s]][:, :], w_hi[s % 4][:, k, :], w_lo[s % 4][:, k, :],
                                                h_hi[:, k, :], h_lo[:, k, :], k == 0, k == KD - 1)
                        ins.then_inc(tile_done, 1)
                        if norm == 1 and j % 2:
                            n = ADA_EARLY - 1 + j // 2
                            ada_tile(i * 2 + n, n % 2, i * 2 + (n + 1))

            ffn_pe(S_UP, 1)

            def turn_output(half, ks, ts):
                for k in ks:
                    pe.wait_ge(y_ready, k + 1)
                for t in ts:
                    for k in ks:
                        ins = pe.transpose(ps[Y_BANK[half][t]][:, k % 4 * P:(k % 4 + 1) * P], xT[:, k, t * P:(t + 1) * P],
                                           ident[:, :])
                    if ks[-1] % 4 == 3:
                        if half or t == QT - 1:
                            ins.then_inc(y_turned, 1)

            def down(s0, second):
                norm = 5 if second else 2
                for n in range(24):
                    k0, nk = PARTS[n // 2 % 3]
                    if n >= 6 and n % 6 in (0, 1) and not second:
                        norm_sum(norm, (n // 6 - 1) * 2 + n % 6)
                    if second and n == 20:
                        pe.wait_ge(y_ready, 5)
                        turn_output(0, range(4), range(QT))
                    s = s0 + n
                    tile(s, g_hi, g_lo, k0, first=n // 2 % 3 == 0, last=n // 2 % 3 == 2,
                         ready=parts(g_lo_done, second * (FT + 2) + 2) if n in (0, 2, 4) else None)
                    m = ADA_EARLY + ADA_UP - 2 + n
                    if not second and n and m < NMOD * KD:
                        ada_tile(m, m % 2, m + 1)
                if not second:
                    for k in range(KD - 2, KD):
                        norm_sum(norm, k)
                    keep_warm(4, 26)

            down(S_DOWN, 0)
            for s in range(S_FH, S_IH):
                tile(s, h_hi, h_lo, ready=normed_parts(3) if s == S_FH else None)

            def turn_values(n):
                pe.wait_ge(freed["act"], FREED[S_IH + n if n < HG else S_KV2 + 1][1])
                if n >= 2:
                    pe.wait_ge(values_copied, n - 1)
                for t in range(QT):
                    ins = pe.transpose(ps[V_BANK[n]][:, t * P:(t + 1) * P], sq[:, n % 2, t * P:(t + 1) * P], ident[:, :])
                ins.then_inc(values_turned, 1)

            for n in range(HG):
                tile(S_IH + n, h_hi, h_lo)
                if n:
                    turn_values(n - 1)

            def chunk(c):
                kind, heads, n = CHUNKS[c]
                bank = ps[CHUNK_BANK[c % 2]]
                if c >= 2:
                    if c - 2 < N_SEL:
                        pe.wait_ge(sel_done, c - 1)
                    else:
                        pe.wait_ge(off_copied, c - 1 - N_SEL)
                if c < SUMMED_CHUNKS:
                    pe.wait_ge(multiplied, c + 1)
                    ins = pe.matmul(bank[:, :], ones[:, :], hn[:, c % 2, :], start=True, stop=True)
                    heads = ()
                else:
                    pe.wait_ge(q_scaled, n + 1)
                    pe.wait_ge(k_scaled, n)
                    keys = keys_at[n]
                for hd in heads:
                    if kind == 256:
                        todo = [(m * 256, m, 0, 256) for m in range(2)]
                    elif kind == 128:
                        todo = [(hd % 2 * 256 + m * P, 2 * m, m * P, P) for m in range(2)]
                    else:
                        todo = [(hd % 2 * 256 + t * 64, t, t * 64, 64) for t in range(QT)]
                    for at, t, q0, nq in todo:
                        ins = pe.matmul(bank[:, at:at + nq], keys[:, hd, t * P:(t + 1) * P], qd[n % 2][:, hd, q0:q0 + nq],
                                        start=True, stop=True)
                ins.then_inc(chunk_done, 1)
                if n is not None and (c + 1 == len(CHUNKS) or CHUNKS[c + 1][2] != n):
                    pe.wait_ge(chunk_done, c + 1)
                    pe.sem_inc(lvl_done, 1)

            for s in range(S_Q2, S_GH):
                tile(s, h_hi, h_lo)
                if s == S_Q2:
                    turn_values(HG - 1)
                chunk(s - S_Q2)
            turn_values(HG)
            pe.wait_ge(values_copied, HG + 1)

            def scores2(j):
                i, g, t = ITEMS[j]
                L = P if t == 0 else 2 * P
                grp = slice(g * DH, (g + 1) * DH)
                if j >= 2:
                    pe.wait_ge(s2_ready, j - 1)
                pe.matmul(ps[4 + j % 2][:, 0:L], q2T[grp, i, t * P:(t + 1) * P], k2T[grp, (t + 1) * P - L:(t + 1) * P],
                          start=True, stop=True).then_inc(qk2_done, 1)

            scores2(0)
            for j in range(NI + 2):
                if j + 1 < NI:
                    scores2(j + 1)
                c = chunk_at(j)
                if c is not None:
                    chunk(c)
                hd = av_at(j)
                if hd is not None:
                    pe.wait_ge(sel_done, N_SEL)
                    pe.wait_ge(off_copied, len(CHUNKS) - N_SEL)
                    if hd >= 2:
                        pe.wait_ge(av_copied, hd - 1)
                    for t in range(QT):
                        for k in range(t + 1):
                            if k == t:
                                w = hs[:, hd, t * P:(t + 1) * P]
                            elif (k, t) in OFF_AT:
                                w = off[:, hd, OFF_AT[k, t]:OFF_AT[k, t] + P]
                            ins = pe.matmul(ps[CHUNK_BANK[hd % 2]][:, t * P:(t + 1) * P], iN[:, k, hd * P:(hd + 1) * P],
                                            w, start=k == 0, stop=k == t)
                    ins.then_inc(av_done, 1)
                n = gh_at(j)
                if n is not None:
                    tile(S_GH + n, h_hi, h_lo)
                if 1 <= j <= NI:
                    m = j - 1
                    nk = 1 if ITEMS[m][2] == 0 else 2
                    pe.wait_ge(p2_ready, m + 1)
                    if m:
                        pe.wait_ge(t2_copied, m)
                    for kt in range(nk):
                        ins = pe.transpose(ps[6][:, kt * P:(kt + 1) * P], sc2[:, m % 2, kt * P:(kt + 1) * P], ident[:, :])
                    ins.then_inc(t2_done, 1)
                if j >= 2:
                    m = j - 2
                    i, g, t = ITEMS[m]
                    nk = 1 if t == 0 else 2
                    pe.wait_ge(t2_copied, m + 1)
                    if m and m % (2 * QT) == 0:
                        pe.wait_ge(o2_copied, m // (2 * QT))
                    for n in range(nk):
                        ins = pe.matmul(ps[2][g * DH:(g + 1) * DH, t * P:(t + 1) * P],
                                        v2N[:, t + 1 - nk + n, g * DH:(g + 1) * DH], pT2[:, m % 2, n * P:(n + 1) * P],
                                        start=n == 0, stop=n == nk - 1)
                    ins.then_inc(pv2_done, 1)
                hd = av_at(j - 2)
                if hd is not None:
                    pe.wait_ge(r_sq, hd + 1)
                    if hd:
                        pe.wait_ge(r_var, hd)
                    pe.matmul(ps[R_BANK][:, :], ones[:, :], sq[:, hd % 2, :], start=True, stop=True).then_inc(r_sum, 1)
            pe.wait_ge(av_copied, HG)
            for i in range(PAIRS):
                pe.wait_ge(n2_sq, i + 1)
                pe.matmul(ps[7][:, :], ones[:, :], (hn, sq)[i // 2][:, i % 2, :], start=i == 0, stop=i == PAIRS - 1).then_inc(n2_sum, 1)
            keep_warm(4, 24)
            mixed_parts = lambda k: pe.wait_ge(n2_lo, k + 1) if k < PAIRS else pe.wait_ge(r_lo[k // 2 % 2], k % 2 + 1)
            for s in range(S_OUT2, S_UP2):
                tile(s, h_hi, h_lo, ready=mixed_parts if s == S_OUT2 else None)
                if s > S_OUT2:
                    norm_sum(4, s - S_OUT2 - 1)
            norm_sum(4, KD - 1)
            keep_warm(4, 22)
            ffn_pe(S_UP2, 4)
            down(S_DOWN2, 1)
            pe.wait_ge(squares_added, KD - 1)
            for t in range(QT):
                ins = pe.matmul(ps[7][:, t:t + 1], hn[:, 0, t * P:(t + 1) * P], ones[:, 0:1], start=True, stop=True)
            ins.then_inc(y_sum, 1)
            turn_output(1, range(4, KD), range(QT - 1))
            pe.wait_ge(y_root, 1)
            turn_output(1, range(4, KD), range(QT - 1, QT))


INPUTS = ["x", "norm1_g", "w_in", "cmp_pe_k", "cmp_pe_v", "cmp_k_w1", "cmp_k_w2", "cmp_v_w1", "cmp_v_w2",
          "w_attn_br", "conv_dw_w", "conv_dw_b", "conv_ln_g", "conv_ln_b", "w_conv_br", "w_out", "norm2_g",
          "ffn_w_up", "ffn_dw_w", "ffn_dw_b", "ffn_w_down", "final_g", "c_2", "ada_w_2", "ada_b_2",
          "mix_norm_g_2", "w_in_2", "b_in_2", "attn_sinks_2", "attn_out_g_2", "hgrn_lb_logits_2",
          "hgrn_out_g_2", "w_out_2", "ffn_norm_g_2", "w_up_2", "conv_w_2", "conv_b_2", "w_down_2",
          "final_norm_g_2"]


def kernel(**inputs):
    import concourse.bacc as bacc
    from concourse.bass_utils import run_bass_kernel_spmd as run

    nc = bacc.Bacc("TRN2", target_bir_lowering=False, num_devices=1)
    arrays, aps = {}, {}
    for name in INPUTS:
        arrays[f"in_{name}"] = np.ascontiguousarray(inputs[name])
        aps[name] = nc.dram_tensor(f"in_{name}", arrays[f"in_{name}"].shape, F32, kind="ExternalInput").ap()
    out = nc.dram_tensor("out", (1, T, D), F32, kind="ExternalOutput").ap()
    build(nc, aps, out)
    return run(nc, [arrays], core_ids=[0]).results[0]["out"]
```
